# Optimizing a Trainium2 kernel written in Bass

```python
import math
import jax, jax.numpy as jnp
from jax import lax
import numpy as np

D_MODEL = 1024
BATCH = 1
SEQ = 128
DEPTH = 2
DEC_BATCH = 1
DEC_SEQ = 1024
PAST_LEN = 128

GRID_W = 64
HEAD_DIM = 64
N_EVEN = (DEPTH + 1) // 2
N_ODD = DEPTH // 2
Q_BLOCK = 128
A_HEADS = D_MODEL // 128
A_KV_HEADS = A_HEADS // 4
A_WINDOW = 128
A_BLOCK = 128
ROPE_BASE = 10000.0
HY_CH = D_MODEL // 2
HY_ORDER = 2
HY_SHORT = 3
HY_EMB = 33
HY_FILT_W = 64
HY_FAST_DECAY = 0.3
HY_SLOW_DECAY = 1.5
HY_DECAY_TARGET = 1e-2
HY_SHIFT = 0.05
C_HEADS = D_MODEL // 128
C_SHORT = 3
C_CHUNK = 64
D_HEADS = D_MODEL // 128
NA_KH_MAX = 8
NA_KW = 16
N_EXPERTS = 16
EC_CAPACITY = 2
MOE_D_FF = D_MODEL
EPS = 1e-6
NEG_INF = -1e30

A_Q_W = A_HEADS * HEAD_DIM
A_KV_W = A_KV_HEADS * HEAD_DIM
EVEN_IN = A_Q_W + 2 * A_KV_W + 3 * HY_CH
EVEN_MIX = A_Q_W + HY_CH
C_W = C_HEADS * HEAD_DIM
D_W = D_HEADS * HEAD_DIM
ODD_IN = 4 * C_W + 4 * C_HEADS + 3 * D_W
ODD_MIX = C_W + D_W

kernel_name = 'hybrid_diffusion_trunk_step'

def rms_norm(x, g):
    xf = x.astype(jnp.float32)
    y = xf * lax.rsqrt(jnp.mean(xf * xf, axis=-1, keepdims=True) + EPS)
    return (y * g.astype(jnp.float32)).astype(x.dtype)

def ada_params(cond, w, b):
    m = jax.nn.silu(cond) @ w + b
    return jnp.split(m[:, None, :], 6, axis=-1)

def modulate(x, g, shift, scale):
    return rms_norm(x, g) * (1 + scale) + shift

def axial_rope(T):
    t = jnp.arange(T)
    n_freq = HEAD_DIM // 4
    inv = ROPE_BASE ** (-jnp.arange(n_freq, dtype=jnp.float32) / n_freq)
    ang = jnp.concatenate([(t // GRID_W).astype(jnp.float32)[:, None] * inv,
                           (t % GRID_W).astype(jnp.float32)[:, None] * inv], axis=-1)
    return jnp.cos(ang)[:, None, :], jnp.sin(ang)[:, None, :]

def apply_rope(x, cos, sin):
    xf = x.astype(jnp.float32)
    x1, x2 = jnp.split(xf, 2, axis=-1)
    return jnp.concatenate([x1 * cos - x2 * sin, x2 * cos + x1 * sin], axis=-1).astype(x.dtype)

def softmax_parts(parts, sink=None):
    sizes = [p.shape[-1] for p in parts]
    cols = list(parts)
    if sink is not None:
        cols.append(jnp.broadcast_to(sink, parts[0].shape[:-1] + (1,)))
    p = jax.nn.softmax(jnp.concatenate(cols, axis=-1), axis=-1)
    pieces = jnp.split(p, np.cumsum(sizes).tolist(), axis=-1)
    return pieces[:len(sizes)]

def context_attention(q, k, v, sink):
    B, S, HQ, hd = q.shape
    HK = k.shape[2]
    G = HQ // HK
    nb = S // Q_BLOCK
    scale = hd ** -0.5
    sink_b = None if sink is None else sink.astype(jnp.float32).reshape(1, HK, G, 1, 1)
    qb = q.reshape(B, nb, Q_BLOCK, HK, G, hd).swapaxes(0, 1)

    def one(qi):
        s = jnp.einsum('bqkgd,bskd->bkgqs', qi, k, preferred_element_type=jnp.float32) * scale
        (p,) = softmax_parts([s], sink_b)
        return jnp.einsum('bkgqs,bskd->bqkgd', p.astype(v.dtype), v)

    o = lax.map(one, qb)
    return o.swapaxes(0, 1).reshape(B, S, HQ, hd)

def window_attention(q, k, v, ck, cv, sink):
    B, T, HQ, hd = q.shape
    HK = k.shape[2]
    G = HQ // HK
    nb = T // A_BLOCK
    scale = hd ** -0.5
    qb = q.reshape(B, nb, A_BLOCK, HK, G, hd).swapaxes(0, 1)

    def band(x):
        xp = jnp.pad(x, ((0, 0), (A_BLOCK, A_BLOCK), (0, 0), (0, 0))).reshape(B, nb + 2, A_BLOCK, HK, hd)
        return jnp.concatenate([xp[:, :-2], xp[:, 1:-1], xp[:, 2:]], axis=2).swapaxes(0, 1)

    kb, vb = band(k), band(v)
    qpos = jnp.arange(nb)[:, None, None] * A_BLOCK + jnp.arange(A_BLOCK)[None, :, None]
    kpos = jnp.arange(nb)[:, None, None] * A_BLOCK - A_BLOCK + jnp.arange(3 * A_BLOCK)[None, None, :]
    mask = (jnp.abs(kpos - qpos) <= A_WINDOW) & (kpos >= 0) & (kpos < T)
    sink_b = sink.astype(jnp.float32).reshape(1, HK, G, 1, 1)

    def one(xs):
        qi, ki, vi, mi = xs
        s_loc = jnp.einsum('bqkgd,bskd->bkgqs', qi, ki, preferred_element_type=jnp.float32) * scale
        s_loc = jnp.where(mi[None, None, None], s_loc, NEG_INF)
        s_ctx = jnp.einsum('bqkgd,bpkd->bkgqp', qi, ck, preferred_element_type=jnp.float32) * scale
        p_loc, p_ctx = softmax_parts([s_loc, s_ctx], sink_b)
        return (jnp.einsum('bkgqs,bskd->bqkgd', p_loc.astype(vi.dtype), vi)
                + jnp.einsum('bkgqp,bpkd->bqkgd', p_ctx.astype(cv.dtype), cv))

    o = lax.map(one, (qb, kb, vb, mask))
    return o.swapaxes(0, 1).reshape(B, T, HQ, hd)

def short_conv(x, w):
    K = w.shape[0]
    L = x.shape[1]
    pad = K // 2
    xp = jnp.pad(x, ((0, 0), (pad, pad), (0, 0)))
    return sum(xp[:, i:i + L] * w[i] for i in range(K))

def hyena_filter_bank(L, w1, b1, w2, b2, w3, freq):
    f32 = jnp.float32
    t = jnp.linspace(0.0, 1.0, L, dtype=f32)[:, None]
    bands = (HY_EMB - 1) // 2
    omega = 2.0 * math.pi * jnp.arange(L, dtype=f32)[:, None] / L
    fb = jnp.linspace(1e-4, bands - 1, bands, dtype=f32)[None, :]
    feats = jnp.concatenate([t, jnp.cos(fb * omega), -jnp.sin(fb * omega)], axis=-1)
    fr = freq.astype(f32)
    h = jnp.sin(fr * (feats @ w1.astype(f32) + b1.astype(f32)))
    h = jnp.sin(fr * (h @ w2.astype(f32) + b2.astype(f32)))
    h = (h @ w3.astype(f32)).reshape(L, 2, HY_ORDER, HY_CH)
    max_decay = math.log(HY_DECAY_TARGET) / HY_FAST_DECAY
    min_decay = math.log(HY_DECAY_TARGET) / HY_SLOW_DECAY
    deltas = jnp.abs(jnp.linspace(min_decay, max_decay, HY_CH, dtype=f32))
    h = h * (jnp.exp(-t * deltas) + HY_SHIFT)[:, None, None, :]
    taps = jnp.concatenate([h[:, 0], jnp.zeros((1, HY_ORDER, HY_CH), f32), h[:0:-1, 1]], axis=0)
    taps = taps / jnp.sum(jnp.abs(taps), axis=0, keepdims=True)
    return jnp.fft.rfft(taps, axis=0)

def hyena_mixer(z, conv_w, conv_b, w1, b1, w2, b2, w3, freq, skip):
    L = z.shape[1]
    zf = (short_conv(z, conv_w) + conv_b).astype(jnp.float32)
    v, x1, x2 = jnp.split(zf, 3, axis=-1)
    filt = hyena_filter_bank(L, w1, b1, w2, b2, w3, freq)
    skip = skip.astype(jnp.float32)

    def long_conv(u, o):
        y = jnp.fft.irfft(jnp.fft.rfft(u, n=2 * L, axis=1) * filt[None, :, o], n=2 * L, axis=1)[:, :L]
        return y + u * skip[o]

    y = x1 * long_conv(v, 0)
    y = x2 * long_conv(y, 1)
    return y.astype(z.dtype)

def l2norm(x):
    xf = x.astype(jnp.float32)
    return xf * lax.rsqrt(jnp.sum(xf * xf, axis=-1, keepdims=True) + EPS)

def chunk_gated_delta(q, k, v, g, beta, s0):
    B, L, H, dk = q.shape
    dv = v.shape[-1]
    n = L // C_CHUNK

    def chunks(x):
        x = x.reshape((B, n, C_CHUNK, H) + x.shape[3:])
        return jnp.moveaxis(jnp.moveaxis(x, 1, 0), 3, 2)

    qc, kc, vc, bc = chunks(q), chunks(k), chunks(v), chunks(beta)
    gc = jnp.cumsum(chunks(g), axis=-1)
    tri = jnp.tril(jnp.ones((C_CHUNK, C_CHUNK), bool))
    strict = jnp.tril(jnp.ones((C_CHUNK, C_CHUNK), bool), k=-1)
    gamma = jnp.exp(jnp.where(tri, gc[..., :, None] - gc[..., None, :], NEG_INF))
    kb = kc * bc[..., None]
    a_mat = jnp.where(strict, jnp.einsum('nbhid,nbhjd->nbhij', kb, kc) * gamma, 0.0) + jnp.eye(C_CHUNK, dtype=jnp.float32)
    rhs = jnp.concatenate([vc * bc[..., None], kb * jnp.exp(gc)[..., None]], axis=-1)
    sol = lax.linalg.triangular_solve(a_mat, rhs, left_side=True, lower=True)
    u, w = sol[..., :dv], sol[..., dv:]
    attn = jnp.where(tri, jnp.einsum('nbhid,nbhjd->nbhij', qc, kc) * gamma, 0.0)
    g_last = gc[..., -1]
    q_dec = qc * jnp.exp(gc)[..., None]
    k_dec = kc * jnp.exp(g_last[..., None] - gc)[..., None]

    def step(S, xs):
        u_i, w_i, a_i, qd, kd, gl = xs
        v_new = u_i - jnp.einsum('bhck,bhkv->bhcv', w_i, S)
        o = jnp.einsum('bhck,bhkv->bhcv', qd, S) + jnp.einsum('bhij,bhjv->bhiv', a_i, v_new)
        S = S * jnp.exp(gl)[..., None, None] + jnp.einsum('bhck,bhcv->bhkv', kd, v_new)
        return S, o

    S, o = lax.scan(step, s0.astype(jnp.float32), (u, w, attn, q_dec, k_dec, g_last))
    o = jnp.moveaxis(jnp.moveaxis(o, 2, 3), 0, 1).reshape(B, L, H, dv)
    return o, S

def deltanet_mixer(zq, zk, zv, zg, za, zb, conv_w, a_log, dt_bias, norm_w, s0):
    B, L, _ = zq.shape
    qkv = jax.nn.silu(short_conv(jnp.concatenate([zq, zk, zv], axis=-1), conv_w))
    q, k, v = [t.reshape(B, L, C_HEADS, HEAD_DIM) for t in jnp.split(qkv, 3, axis=-1)]
    q = l2norm(q) * (HEAD_DIM ** -0.5)
    k = l2norm(k)
    v = v.astype(jnp.float32)
    beta = jax.nn.sigmoid(zb.astype(jnp.float32))
    g = -jnp.exp(a_log.astype(jnp.float32)) * jax.nn.softplus(za.astype(jnp.float32) + dt_bias.astype(jnp.float32))
    o_f, s_f = chunk_gated_delta(q, k, v, g[:, :, 0], beta[:, :, 0], s0[:, 0])
    o_b, s_b = chunk_gated_delta(q[:, ::-1], k[:, ::-1], v[:, ::-1], g[:, ::-1, 1], beta[:, ::-1, 1], s0[:, 1])
    o = o_f + o_b[:, ::-1]
    gate = jax.nn.silu(zg.reshape(B, L, C_HEADS, HEAD_DIM).astype(jnp.float32))
    o = rms_norm(o, norm_w) * gate
    return o.reshape(B, L, C_W).astype(zq.dtype), jnp.stack([s_f, s_b], axis=1)

def neighbourhood_attention(q, k, v, ck, cv, rpb):
    B, T, H, hd = q.shape
    rows = T // GRID_W
    kh = min(NA_KH_MAX, rows)
    scale = hd ** -0.5
    r = jnp.arange(rows)
    rs = jnp.clip(r - kh // 2, 0, rows - kh)
    key_rows = rs[:, None] + jnp.arange(kh)[None, :]
    idx = (key_rows[:, :, None] * GRID_W + jnp.arange(GRID_W)).reshape(rows, kh * GRID_W)
    col = jnp.arange(GRID_W)
    cs = jnp.clip(col - NA_KW // 2, 0, GRID_W - NA_KW)
    kcol = jnp.tile(col, kh)
    col_ok = (kcol[None, :] >= cs[:, None]) & (kcol[None, :] < cs[:, None] + NA_KW)
    roff = jnp.repeat(key_rows - r[:, None], GRID_W, axis=1) + NA_KH_MAX - 1
    coff = jnp.clip(kcol[None, :] - col[:, None] + NA_KW - 1, 0, 2 * NA_KW - 2)
    qr = q.reshape(B, rows, GRID_W, H, hd).swapaxes(0, 1)
    rpb_f = rpb.astype(jnp.float32)

    def one(xs):
        qi, ii, ro = xs
        ki = k[:, ii]
        vi = v[:, ii]
        bias = rpb_f[:, ro[None, :], coff]
        s_loc = jnp.einsum('bqhd,bkhd->bhqk', qi, ki, preferred_element_type=jnp.float32) * scale + bias[None]
        s_loc = jnp.where(col_ok[None, None], s_loc, NEG_INF)
        s_ctx = jnp.einsum('bqhd,bphd->bhqp', qi, ck, preferred_element_type=jnp.float32) * scale
        p_loc, p_ctx = softmax_parts([s_loc, s_ctx])
        return (jnp.einsum('bhqk,bkhd->bqhd', p_loc.astype(vi.dtype), vi)
                + jnp.einsum('bhqp,bphd->bqhd', p_ctx.astype(cv.dtype), cv))

    o = lax.map(one, (qr, idx, roff))
    return o.swapaxes(0, 1).reshape(B, T, H, hd)

def expert_choice_ffn(h, w_router, w_gate, w_up, w_down):
    B, T, D = h.shape
    cap = EC_CAPACITY * T // N_EXPERTS
    aff = jax.nn.softmax(jnp.einsum('btd,de->bte', h, w_router, preferred_element_type=jnp.float32), axis=-1)
    gate, idx = lax.top_k(aff.swapaxes(1, 2), cap)
    xg = jax.vmap(lambda hb, ib: hb[ib])(h, idx)
    a = jnp.einsum('becd,edf->becf', xg, w_gate)
    u = jnp.einsum('becd,edf->becf', xg, w_up)
    y = jnp.einsum('becf,efd->becd', jax.nn.silu(a) * u, w_down) * gate[..., None].astype(h.dtype)
    return jax.vmap(lambda yb, ib: jnp.zeros((T, D), yb.dtype).at[ib.reshape(-1)].add(yb.reshape(-1, D)))(y, idx)

def split_even(z):
    B, L = z.shape[:2]
    q = z[..., :A_Q_W].reshape(B, L, A_HEADS, HEAD_DIM)
    k = z[..., A_Q_W:A_Q_W + A_KV_W].reshape(B, L, A_KV_HEADS, HEAD_DIM)
    v = z[..., A_Q_W + A_KV_W:A_Q_W + 2 * A_KV_W].reshape(B, L, A_KV_HEADS, HEAD_DIM)
    return q, k, v, z[..., A_Q_W + 2 * A_KV_W:]

def split_odd(z):
    B, L = z.shape[:2]
    zq, zk, zv, zg = [z[..., i * C_W:(i + 1) * C_W] for i in range(4)]
    off = 4 * C_W
    za = z[..., off:off + 2 * C_HEADS].reshape(B, L, 2, C_HEADS)
    zb = z[..., off + 2 * C_HEADS:off + 4 * C_HEADS].reshape(B, L, 2, C_HEADS)
    off = off + 4 * C_HEADS
    nq, nk, nv = [z[..., off + i * D_W:off + (i + 1) * D_W].reshape(B, L, D_HEADS, HEAD_DIM) for i in range(3)]
    return zq, zk, zv, zg, za, zb, nq, nk, nv

def setup_inputs(seed: int = 0) -> dict:
    key = jax.random.key(seed)
    ks = iter(jax.random.split(key, 48))
    f32 = jnp.float32

    def nrm(shape, s):
        return jax.random.normal(next(ks), shape, f32) * s

    def gain(shape):
        return 1.0 + nrm(shape, 0.02)

    dt = jnp.exp(jax.random.uniform(next(ks), (N_ODD, 2, C_HEADS), f32, math.log(1e-3), math.log(1e-1)))
    a_log = jnp.log(jax.random.uniform(next(ks), (N_ODD, 2, C_HEADS), f32, 1.0, 16.0))
    return {
        'x_prompt': nrm((BATCH, SEQ, D_MODEL), 1.0),
        'x_sample': nrm((DEC_BATCH, DEC_SEQ, D_MODEL), 1.0),
        'cache_attn_k': nrm((DEC_BATCH, N_EVEN, PAST_LEN, A_KV_HEADS, HEAD_DIM), 1.0),
        'cache_attn_v': nrm((DEC_BATCH, N_EVEN, PAST_LEN, A_KV_HEADS, HEAD_DIM), 1.0),
        'state_delta': nrm((DEC_BATCH, N_ODD, 2, C_HEADS, HEAD_DIM, HEAD_DIM), 0.1),
        'cache_na_k': nrm((DEC_BATCH, N_ODD, PAST_LEN, D_HEADS, HEAD_DIM), 1.0),
        'cache_na_v': nrm((DEC_BATCH, N_ODD, PAST_LEN, D_HEADS, HEAD_DIM), 1.0),
        'c': nrm((DEC_BATCH, D_MODEL), 1.0),
        'c_ctx': nrm((D_MODEL,), 1.0),
        'w_ada': nrm((DEPTH, D_MODEL, 6 * D_MODEL), 0.5 * D_MODEL ** -0.5),
        'b_ada': nrm((DEPTH, 6 * D_MODEL), 0.02),
        'norm_mix': gain((DEPTH, D_MODEL)),
        'norm_ffn': gain((DEPTH, D_MODEL)),
        'norm_final': gain((D_MODEL,)),
        'even_w_in': nrm((N_EVEN, D_MODEL, EVEN_IN), D_MODEL ** -0.5),
        'even_w_out': nrm((N_EVEN, EVEN_MIX, D_MODEL), EVEN_MIX ** -0.5),
        'attn_sink': nrm((N_EVEN, A_HEADS), 0.5),
        'hy_conv_w': nrm((N_EVEN, HY_SHORT, 3 * HY_CH), HY_SHORT ** -0.5),
        'hy_conv_b': nrm((N_EVEN, 3 * HY_CH), 0.02),
        'hy_w1': nrm((N_EVEN, HY_EMB, HY_FILT_W), HY_EMB ** -0.5),
        'hy_b1': nrm((N_EVEN, HY_FILT_W), 0.02),
        'hy_w2': nrm((N_EVEN, HY_FILT_W, HY_FILT_W), HY_FILT_W ** -0.5),
        'hy_b2': nrm((N_EVEN, HY_FILT_W), 0.02),
        'hy_w3': nrm((N_EVEN, HY_FILT_W, 2 * HY_ORDER * HY_CH), HY_FILT_W ** -0.5),
        'hy_freq': gain((N_EVEN, HY_FILT_W)),
        'hy_skip': nrm((N_EVEN, HY_ORDER, HY_CH), 0.5),
        'odd_w_in': nrm((N_ODD, D_MODEL, ODD_IN), D_MODEL ** -0.5),
        'odd_w_out': nrm((N_ODD, ODD_MIX, D_MODEL), ODD_MIX ** -0.5),
        'gdn_conv_w': nrm((N_ODD, C_SHORT, 3 * C_W), C_SHORT ** -0.5),
        'gdn_a_log': a_log,
        'gdn_dt_bias': dt + jnp.log(-jnp.expm1(-dt)),
        'gdn_norm': gain((N_ODD, HEAD_DIM)),
        'na_rpb': nrm((N_ODD, D_HEADS, 2 * NA_KH_MAX - 1, 2 * NA_KW - 1), 0.1),
        'moe_router': nrm((DEPTH, D_MODEL, N_EXPERTS), D_MODEL ** -0.5),
        'moe_w_gate': nrm((DEPTH, N_EXPERTS, D_MODEL, MOE_D_FF), D_MODEL ** -0.5),
        'moe_w_up': nrm((DEPTH, N_EXPERTS, D_MODEL, MOE_D_FF), D_MODEL ** -0.5),
        'moe_w_down': nrm((DEPTH, N_EXPERTS, MOE_D_FF, D_MODEL), MOE_D_FF ** -0.5),
    }

def reference(x_prompt, x_sample, cache_attn_k, cache_attn_v, state_delta, cache_na_k, cache_na_v,
              c, c_ctx, w_ada, b_ada, norm_mix, norm_ffn, norm_final,
              even_w_in, even_w_out, attn_sink, hy_conv_w, hy_conv_b, hy_w1, hy_b1, hy_w2, hy_b2,
              hy_w3, hy_freq, hy_skip, odd_w_in, odd_w_out, gdn_conv_w, gdn_a_log, gdn_dt_bias,
              gdn_norm, na_rpb, moe_router, moe_w_gate, moe_w_up, moe_w_down):
    xp, xs = x_prompt, x_sample
    bp = xp.shape[0]
    cos, sin = axial_rope(xs.shape[1])
    new_ak, new_av, new_st, new_nk, new_nv = [], [], [], [], []
    for l in range(DEPTH):
        j = l // 2
        mp = ada_params(c_ctx[None, :], w_ada[l], b_ada[l])
        ms = ada_params(c, w_ada[l], b_ada[l])
        hp = modulate(xp, norm_mix[l], mp[0], mp[1])
        hs = modulate(xs, norm_mix[l], ms[0], ms[1])
        if l % 2 == 0:
            hy = (hy_conv_w[j], hy_conv_b[j], hy_w1[j], hy_b1[j], hy_w2[j], hy_b2[j], hy_w3[j], hy_freq[j], hy_skip[j])
            q, k, v, zh = split_even(hp @ even_w_in[j])
            oa = context_attention(q, k, v, attn_sink[j])
            mix_p = jnp.concatenate([oa.reshape(oa.shape[:2] + (A_Q_W,)), hyena_mixer(zh, *hy)], axis=-1) @ even_w_out[j]
            new_ak.append(k)
            new_av.append(v)
            q, k, v, zh = split_even(hs @ even_w_in[j])
            q, k = apply_rope(q, cos, sin), apply_rope(k, cos, sin)
            oa = window_attention(q, k, v, cache_attn_k[:, j], cache_attn_v[:, j], attn_sink[j])
            mix_s = jnp.concatenate([oa.reshape(oa.shape[:2] + (A_Q_W,)), hyena_mixer(zh, *hy)], axis=-1) @ even_w_out[j]
        else:
            gdn = (gdn_conv_w[j], gdn_a_log[j], gdn_dt_bias[j], gdn_norm[j])
            zq, zk, zv, zg, za, zb, nq, nk, nv = split_odd(hp @ odd_w_in[j])
            s0 = jnp.zeros((bp, 2, C_HEADS, HEAD_DIM, HEAD_DIM), jnp.float32)
            oc, st = deltanet_mixer(zq, zk, zv, zg, za, zb, *gdn, s0)
            od = context_attention(nq, nk, nv, None)
            mix_p = jnp.concatenate([oc, od.reshape(od.shape[:2] + (D_W,))], axis=-1) @ odd_w_out[j]
            new_st.append(st)
            new_nk.append(nk)
            new_nv.append(nv)
            zq, zk, zv, zg, za, zb, nq, nk, nv = split_odd(hs @ odd_w_in[j])
            oc, _ = deltanet_mixer(zq, zk, zv, zg, za, zb, *gdn, state_delta[:, j])
            od = neighbourhood_attention(nq, nk, nv, cache_na_k[:, j], cache_na_v[:, j], na_rpb[j])
            mix_s = jnp.concatenate([oc, od.reshape(od.shape[:2] + (D_W,))], axis=-1) @ odd_w_out[j]
        xp = xp + mp[2] * mix_p
        xs = xs + ms[2] * mix_s
        moe = (moe_router[l], moe_w_gate[l], moe_w_up[l], moe_w_down[l])
        xp = xp + mp[5] * expert_choice_ffn(modulate(xp, norm_ffn[l], mp[3], mp[4]), *moe)
        xs = xs + ms[5] * expert_choice_ffn(modulate(xs, norm_ffn[l], ms[3], ms[4]), *moe)
    y_prompt = rms_norm(xp, norm_final)
    y_sample = rms_norm(xs, norm_final)
    return (y_prompt, y_sample, jnp.stack(new_ak, axis=1), jnp.stack(new_av, axis=1), jnp.stack(new_st, axis=1), jnp.stack(new_nk, axis=1), jnp.stack(new_nv, axis=1))


_drawn_inputs = setup_inputs


def setup_inputs(seed=0):
    import zlib

    import numpy as np

    out = dict(_drawn_inputs(seed))
    spreads = {}
    factors = {'cache_attn_k': 4.951,
     'cache_attn_v': 4.401,
     'state_delta': 6.694,
     'cache_na_k': 4.186,
     'cache_na_v': 9.403,
     'norm_ffn': 5.167,
     'norm_final': 22.637,
     'attn_sink': 8.0,
     'hy_conv_b': 8.0,
     'hy_b1': 8.0,
     'hy_b2': 8.0,
     'hy_freq': 8.0,
     'gdn_norm': 50.523,
     'na_rpb': 64.0}
    for name, (base, spread) in spreads.items():
        noise = np.random.default_rng([zlib.crc32(name.encode()), seed]).standard_normal(out[name].shape)
        drawn = base * np.exp(spread * noise) if base else spread * noise
        out[name] = __import__('jax').numpy.asarray(drawn.astype(out[name].dtype))
    for name, factor in factors.items():
        out[name] = (out[name] * factor).astype(out[name].dtype)
    return out
```

```python
import math
from contextlib import ExitStack

import numpy as np
import concourse.bass as bass
from concourse import mybir

F32 = mybir.dt.float32
U32 = mybir.dt.uint32
ALU = mybir.AluOpType
ACT = mybir.ActivationFunctionType
AX = mybir.AxisListType

P = 128
D = 1024
KD = D // P
TS = 1024
TP = 128
T = TS + TP
NT = T // P
NTS = TS // P
HD = 64
BANK = 512
EPS = 1e-6
NEG = -1e30
GRID_W = 64
MIX = 512
CONV = 3 * MIX
CC = CONV // P
ZW = T + 3
EVEN_TM = 768
ODD_TM = 2080
E = 16
CAP_S = 2 * TS // E
CAP_P = 2 * TP // E
SLOTS = CAP_S + CAP_P


class Link:

    def __init__(self, eng, sem, base=0):
        self.eng, self.sem, self.base, self.n = eng, sem, base, 0

    def __call__(self, ins):
        ins.then_inc(self.sem, 1)
        self.n += 1
        self.eng.wait_ge(self.sem, self.base + self.n)


class Stage:

    def __init__(self, nc, name):
        self.nc, self.name, self.ctx, self.sems, self.blk = nc, name, ExitStack(), [], None

    def __enter__(self):
        self.ctx.__enter__()
        return self

    def __exit__(self, *a):
        if self.blk is not None:
            self.blk.__exit__(*a)
            nums = sorted(q.num for q in self.sems)
            while nums:
                n = 1
                while n < len(nums) and nums[n] == nums[0] + n:
                    n += 1
                self.nc.gpsimd.sem_clear(range(nums[0], nums[0] + n))
                nums = nums[n:]
            self.nc.all_engine_barrier()
        return self.ctx.__exit__(*a)

    def sb(self, name, shape, dt=F32):
        return self.ctx.enter_context(self.nc.sbuf_tensor(f"{self.name}_{name}", shape, dt))

    def ps(self, name, shape, dt=F32):
        return self.ctx.enter_context(self.nc.psum_tensor(f"{self.name}_{name}", shape, dt))

    def sem(self, name):
        self.sems.append(self.ctx.enter_context(self.nc.semaphore(f"{self.name}_{name}")))
        return self.sems[-1]

    def pool_dma_sem(self, name):
        return self.nc.alloc_semaphore(f"{self.name}_{name}")

    def block(self):
        self.blk = self.nc.Block()
        return self.blk.__enter__()


def token_groups():
    return [(0, BANK, 0), (BANK, BANK, 0), (TS, TP, 1)]



def all_rows(ap, rows=P):
    return bass.AP(ap.tensor, ap.offset, [[0, rows]] + list(ap.ap))


def modulation(nc, io, keep):
    PAN = 6 * D // BANK
    RING = 4
    TURNS = PAN // RING
    with Stage(nc, "ada") as s:
        cond = s.sb("cond", [P, 2, KD])
        sil = s.sb("silu", [P, KD, 2])
        bias = s.sb("bias", [2, 2, 6 * D])
        rows = s.sb("rows", [2, 2, 6 * D])
        ring = [s.sb(f"w{i}", [P, KD, BANK]) for i in range(RING)]
        flat = s.sb("flat", [96, 2, P])
        gains = s.sb("gains", [4 * KD, P])
        gain_cols = s.sb("gain_cols", [P, 4 * KD])
        ps = [s.ps(f"p{i}", [2, BANK]) for i in range(RING)]
        pt = [s.ps(f"pt{i}", [P, BANK]) for i in range(3)]
        w_in = [s.sem(f"w_in{i}") for i in range(RING)]
        small_in, ident_in, silu_done = s.sem("small_in"), s.sem("ident_in"), s.sem("silu_done")
        row_done, rows_out, flat_in = s.sem("row_done"), s.sem("rows_out"), s.sem("flat_in")
        mm_done, turned, gain_done = s.sem("mm_done"), s.sem("turned"), s.sem("gain_done")
        blk = s.block()

        @blk.sync
        def _(sp):
            for l in range(2):
                w = io["w_ada"][l].rearrange("(k p) n -> p k n", p=P)
                with sp.Fori(0, TURNS) as i:
                    for r in range(RING):
                        sp.wait_ge(mm_done, i * RING + (l * PAN + r + 1))
                        sp.dma_start(ring[r][:], w[:, :, bass.ds(i * (RING * BANK) + r * BANK, BANK)]).then_inc(w_in[r], 16)

        @blk.scalar
        def _(act):
            act.dma_start(cond[:, 0, :], io["c"][0].rearrange("(k p) -> p k", p=P), allow_slow_non_contiguous=True).then_inc(small_in, 16)
            act.dma_start(cond[:, 1, :], io["c_ctx"].rearrange("(k p) -> p k", p=P), allow_slow_non_contiguous=True).then_inc(small_in, 16)
            for l in range(2):
                act.dma_start(bias[0:1, l, :], io["b_ada"][l:l + 1, :]).then_inc(small_in, 16)
                act.dma_start(bias[1:2, l, :], io["b_ada"][l:l + 1, :]).then_inc(small_in, 16)
            for n, g in enumerate(("norm_mix", "norm_ffn")):
                for l in range(2):
                    act.dma_start(gains[(2 * l + n) * KD:(2 * l + n + 1) * KD, :],
                                  io[g][l].rearrange("(k p) -> k p", p=P)).then_inc(small_in, 16)
            act.dma_start(keep.ident[:], io["ident"]).then_inc(ident_in, 16)
            act.wait_ge(small_in, 16 * 10)
            nc.scalar.activation(sil[:].rearrange("p k c -> p c k"), cond[:], ACT.Silu).then_inc(silu_done, 1)
            act.wait_ge(row_done, RING + 2 * PAN)
            for l in range(2):
                act.dma_start(io["mrow"][l], rows[:, l, :]).then_inc(rows_out, 16)
            act.wait_ge(rows_out, 32)
            for l in range(2):
                act.dma_start(flat[:, l, :], io["mrow"][l].rearrange("c (j p) -> (c j) p", p=P)).then_inc(flat_in, 16)

        @blk.tensor
        def _(pe):
            pe.sem_inc(row_done, RING)
            pe.sem_inc(mm_done, RING)
            pe.wait_ge(silu_done, 1)
            with pe.Fori(0, 2 * TURNS) as i:
                for r in range(RING):
                    pe.wait_ge(w_in[r], i * 16 + 16)
                    pe.wait_ge(row_done, i * RING + (r + 1))
                    for k in range(KD):
                        mm = nc.tensor.matmul(ps[r][:], sil[:, k, :], ring[r][:, k, :], start=k == 0, stop=k == KD - 1)
                    mm.then_inc(mm_done, 1)
            pe.wait_ge(ident_in, 16)
            nc.tensor.transpose(pt[2][:, 0:32], gains[:], keep.ident[0:32, 0:32]).then_inc(turned, 1)
            pe.wait_ge(flat_in, 32)
            for l in range(2):
                nc.tensor.transpose(pt[l][:, 0:96], flat[:, l, :], keep.ident[0:96, 0:96]).then_inc(turned, 1)

        @blk.vector
        def _(dve):
            dve.wait_ge(small_in, 16 * 10)
            for l in range(2):
                with dve.Fori(0, TURNS) as i:
                    for r in range(RING):
                        dve.wait_ge(mm_done, i * RING + (RING + l * PAN + r + 1))
                        at = bass.ds(i * (RING * BANK) + r * BANK, BANK)
                        nc.vector.tensor_tensor(rows[:, l, at], ps[r][:], bias[:, l, at], ALU.add).then_inc(row_done, 1)
            dve.wait_ge(turned, 1)
            nc.vector.tensor_copy(gain_cols[:], pt[2][:, 0:32]).then_inc(gain_done, 1)
            dve.wait_ge(gain_done, 1)
            for l in range(2):
                dve.wait_ge(turned, 2 + l)
                for n in range(2):
                    for c in range(2):
                        at = c * 48 + 24 * n
                        nc.vector.scalar_tensor_tensor(keep.coef[:, l, n, c, 0, :], pt[l][:, at + 8:at + 16], 1.0,
                                                       gain_cols[:, (2 * l + n) * KD:(2 * l + n + 1) * KD], ALU.add, ALU.mult)
                        nc.vector.tensor_copy(keep.coef[:, l, n, c, 1, :], pt[l][:, at:at + 8])


class Norm:

    def __init__(self, s, nc, keep, l, n, x, hT, make_hT=True):
        self.nc, self.keep, self.l, self.n, self.x, self.hT = nc, keep, l, n, x, hT
        self.sq = s.sb("sq", [P, D])
        self.ss = s.sb("ss", [P, NT])
        self.rstd = s.sb("rstd", [P, NT])
        self.eps = s.sb("eps", [P, 1])
        self.banks = [s.ps(f"turn{i}", [P, BANK]) for i in range(2)]
        self.ready = s.sem("x_ready")
        self.eps_set = s.sem("eps_set")
        self.squared = s.sem("squared")
        self.rooted = s.sem("rooted")
        self.scaled = s.sem("xn_done")
        self.rec = s.sem("rstd_done")
        self.turned = s.sem("turned")
        self.taken = s.sem("hT_done")

    def scalar(self, act, wait_x):
        nc = self.nc
        for t in range(NT):
            wait_x(act, t)
            if t:
                act.wait_ge(self.squared, t)
            nc.scalar.activation(self.sq[:], self.x[:, t, :], ACT.Square, accum_out=self.ss[:, t:t + 1]).then_inc(self.squared, 1)
        act.wait_ge(self.squared, NT)
        act.wait_ge(self.eps_set, 1)
        nc.scalar.activation(self.rstd[:], self.ss[:], ACT.Sqrt, bias=self.eps[:], scale=1.0 / D).then_inc(self.rooted, 1)

    def vector_scale(self, dve):
        nc = self.nc
        nc.vector.memset(self.eps[:], EPS).then_inc(self.eps_set, 1)
        dve.wait_ge(self.rooted, 1)
        nc.vector.reciprocal(self.rstd[:], self.rstd[:]).then_inc(self.rec, 1)
        dve.wait_ge(self.rec, 1)
        for t in range(NT):
            nc.vector.tensor_scalar(self.x[:, t, :], self.x[:, t, :], self.rstd[:, t:t + 1], None, ALU.mult).then_inc(self.scaled, 1)

    def tensor(self, pe):
        nc, n = self.nc, 0
        for at, width, _ in token_groups():
            for k in range(KD):
                pe.wait_ge(self.scaled, (at + width) // P)
                if n >= 2:
                    pe.wait_ge(self.taken, n - 1)
                for j in range(width // P):
                    mm = nc.tensor.transpose(self.banks[n % 2][:, j * P:(j + 1) * P],
                                             self.x[:, at // P + j, k * P:(k + 1) * P], self.keep.ident[:])
                mm.then_inc(self.turned, 1)
                n += 1

    def vector_turn(self, dve):
        nc, n = self.nc, 0
        for at, width, c in token_groups():
            for k in range(KD):
                dve.wait_ge(self.turned, n + 1)
                co = self.keep.coef[:, self.l, self.n, c]
                nc.vector.tensor_scalar(self.hT[:, k, at:at + width], self.banks[n % 2][:, 0:width],
                                        co[:, 0, k:k + 1], co[:, 1, k:k + 1], ALU.mult, ALU.add).then_inc(self.taken, 1)
                n += 1
    TURNS = 3 * KD


def load_x(sp, io, x, sems, source):
    for t in range(NT):
        src = source["x"][t * P:(t + 1) * P, :] if "x" in source else (
            source["xs"][t * P:(t + 1) * P, :] if t < NTS else source["xp"])
        sp.dma_start(x[:, t, :], src).then_inc(sems[t], 16)


def project(nc, io, keep, l):
    even = l == 0
    conv_at = EVEN_TM if even else 0
    tm_cols = [(0, 512), (512, 256)] if even else [(1536, 512), (2048, 32), (2080, 512), (2592, 512), (3104, 512)]
    w = io["even_w_in" if even else "odd_w_in"][0].rearrange("(k p) n -> p k n", p=P)
    cw, cb = (io["hy_conv_w"], io["hy_conv_b"]) if even else (io["gdn_conv_w"], None)
    panels = [(conv_at + j * BANK, BANK) for j in range(3)] + tm_cols
    NCONV = 3 * CC
    with Stage(nc, f"proj{l}") as s:
        x = s.sb("x", [P, NT, D])
        hT = s.sb("hT", [P, KD, T])
        ring = [s.sb(f"w{i}", [P, KD, BANK]) for i in range(2)]
        z = [s.sb(f"z{i}", [P, ZW]) for i in range(2)]
        zf = [s.sb(f"zf{i}", [P, ZW]) for i in range(2)]
        out = [s.sb(f"tm{i}", [P, BANK]) for i in range(4)]
        convw = s.sb("convw", [P, 4, CC])
        norm = Norm(s, nc, keep, l, 0, x, hT)
        banks = [s.ps(f"mm{i}", [P, BANK]) for i in range(6)]
        x_in = [s.sem(f"x_in{t}") for t in range(NT)]
        w_in = [s.sem(f"w_in{i}") for i in range(2)]
        conv_in, pads = s.pool_dma_sem("conv_in"), s.sem("pads")
        mm_done, z_done, tm_done = s.sem("mm_done"), s.sem("z_done"), s.sem("tm_done")
        chain, zf_done = s.sem("conv_step"), s.sem("zf_done")
        zf_out = [s.pool_dma_sem(f"zf_out{i}") for i in range(2)]
        tm_out = [s.sem(f"tm_out{i}") for i in range(4)]
        blk = s.block()

        @blk.sync
        def _(sp):
            load_x(sp, io, x, x_in, io["x_of"][l])

            def tiles_out(p):
                col = sum(c[1] for c in tm_cols[:p])
                for t in range(NT):
                    n = p * NT + t
                    sp.wait_ge(tm_done, n + 1)
                    sp.dma_start(io["tm"][l][t * P:(t + 1) * P, col:col + tm_cols[p][1]],
                                 out[n % 4][:, 0:tm_cols[p][1]]).then_inc(tm_out[n % 4], 16)

            for n, (at, width) in enumerate(panels):
                if n >= 5:
                    tiles_out(n - 5)
                if n >= 2:
                    before = min(n - 1, 3) * 12 + max(n - 1 - 3, 0) * NT
                    sp.wait_ge(mm_done, before)
                sp.dma_start(ring[n % 2][:, :, 0:width], w[:, :, at:at + width]).then_inc(w_in[n % 2], 16)
            for p in range(len(panels) - 5, len(tm_cols)):
                tiles_out(p)
            for i in range(4):
                sp.wait_ge(tm_out[i], 16 * len(range(i, len(tm_cols) * NT, 4)))

        @blk.gpsimd
        def _(pool):
            for i in range(3):
                pool.dma_start(convw[:, i, :], cw[0, i].rearrange("(c p) -> p c", p=P), allow_slow_non_contiguous=True).then_inc(conv_in, 16)
            if cb is not None:
                pool.dma_start(convw[:, 3, :], cb[0].rearrange("(c p) -> p c", p=P), allow_slow_non_contiguous=True).then_inc(conv_in, 16)
            for c in range(CC):
                pool.wait_ge(zf_done, c + 1)
                rows = io["conv"][l][c * P:(c + 1) * P, :]
                pool.dma_start(rows[:, 0:TS], zf[c % 2][:, 1:1 + TS]).then_inc(zf_out[c % 2], 16)
                pool.dma_start(rows[:, TS:T], zf[c % 2][:, 2 + TS:2 + T]).then_inc(zf_out[c % 2], 16)
            for i in range(2):
                pool.wait_ge(zf_out[i], 32 * CC // 2)

        @blk.tensor
        def _(pe):
            norm.tensor(pe)
            pe.wait_ge(norm.taken, norm.TURNS)
            n = 0
            for p in range(3):
                pe.wait_ge(w_in[p % 2], 16 * (p // 2 + 1))
                for j in range(4):
                    for at, width, _ in token_groups():
                        if n >= 6:
                            pe.wait_ge(z_done, n - 5)
                        for k in range(KD):
                            mm = nc.tensor.matmul(banks[n % 6][:, 0:width], ring[p % 2][:, k, j * P:(j + 1) * P],
                                                  hT[:, k, at:at + width], start=k == 0, stop=k == KD - 1)
                        mm.then_inc(mm_done, 1)
                        n += 1
            for p, (_, width) in enumerate(tm_cols, 3):
                pe.wait_ge(w_in[p % 2], 16 * (p // 2 + 1))
                for t in range(NT):
                    pe.wait_ge(z_done, min(n - 5, NCONV))
                    if n - 5 > NCONV:
                        pe.wait_ge(tm_done, n - 5 - NCONV)
                    for k in range(KD):
                        mm = nc.tensor.matmul(banks[n % 6][:, 0:width], hT[:, k, t * P:(t + 1) * P],
                                              ring[p % 2][:, k, 0:width], start=k == 0, stop=k == KD - 1)
                    mm.then_inc(mm_done, 1)
                    n += 1

        @blk.scalar
        def _(act):
            norm.scalar(act, lambda eng, t: eng.wait_ge(x_in[t], 16))
            act.wait_ge(pads, 2)
            n = 0
            for c in range(CC):
                if c >= 2:
                    act.wait_ge(zf_done, c - 1)
                for at, width, cond in token_groups():
                    act.wait_ge(mm_done, n + 1)
                    nc.scalar.activation(z[c % 2][:, at + 1 + cond:at + 1 + cond + width], banks[n % 6][:, 0:width],
                                         ACT.Copy).then_inc(z_done, 1)
                    n += 1
            for i in range(len(tm_cols) * NT):
                act.wait_ge(mm_done, n + 1)
                if i >= 4:
                    act.wait_ge(tm_out[i % 4], 16 * (i // 4))
                width = tm_cols[i // NT][1]
                nc.scalar.activation(out[i % 4][:, 0:width], banks[n % 6][:, 0:width], ACT.Copy).then_inc(tm_done, 1)
                n += 1

        @blk.vector
        def _(dve):
            norm.vector_scale(dve)
            for i in range(2):
                nc.vector.memset(z[i][:], 0.0).then_inc(pads, 1)
            norm.vector_turn(dve)
            link = Link(dve, chain)
            dve.wait_ge(conv_in, 16 * (3 if cb is None else 4))
            if cb is None:
                link(nc.vector.memset(convw[:, 3, :], 0.0))
            for c in range(CC):
                dve.wait_ge(z_done, 3 * (c + 1))
                if c >= 2:
                    dve.wait_ge(zf_out[c % 2], 32 * (c // 2))
                zi, zo, n = z[c % 2], zf[c % 2], ZW - 2
                link(nc.vector.tensor_scalar(zo[:, 1:1 + n], zi[:, 1:1 + n], convw[:, 1, c:c + 1], convw[:, 3, c:c + 1], ALU.mult, ALU.add))
                link(nc.vector.scalar_tensor_tensor(zo[:, 1:1 + n], zi[:, 0:n], convw[:, 0, c:c + 1], zo[:, 1:1 + n], ALU.mult, ALU.add))
                nc.vector.scalar_tensor_tensor(zo[:, 1:1 + n], zi[:, 2:2 + n], convw[:, 2, c:c + 1], zo[:, 1:1 + n],
                                               ALU.mult, ALU.add).then_inc(zf_done, 1)


class AttnPlan:

    def __init__(self, l):
        self.l = l
        self.even = l == 0
        self.nkc = 1 if self.even else 4
        self.W = 512 if self.even else 768
        self.groups = []
        for t in range(NTS):
            if self.even:
                keys = [k for k in (t - 1, t, t + 1) if 0 <= k < NTS]
            else:
                lo = [0, 0, 0, 1, 2, 3, 4, 4][t]
                hi = [4, 4, 5, 6, 7, 8, 8, 8][t]
                keys = list(range(lo, hi))
            self.groups.append((t, keys, True))
        self.groups.append((NTS, [NTS], False))
        self.units = [(g, h) for g in range(len(self.groups)) for h in range(8)]

    def chunk_half(self, h):
        return (h % 4, h // 4) if self.even else (h // 2, h % 2)

    def kv_chunk(self, h):
        return 0 if self.even else h // 2

    def columns(self, g):
        t, keys, cached = self.groups[g]
        return P * (len(keys) + cached)


def attention(nc, io, keep, l):
    plan = AttnPlan(l)
    even, W, nkc = plan.even, plan.W, plan.nkc
    tmw = EVEN_TM if even else 3 * MIX
    tm_at = 0 if even else MIX + 32
    k_at, v_at = (512, 640) if even else (512, 1024)
    kw = nkc * P
    units, groups = plan.units, plan.groups
    with Stage(nc, f"attn{l}") as s:
        tok = s.sb("tok", [P, NT, tmw])
        QT = s.sb("QT", [P, 4, T])
        KT = s.sb("KT", [P, nkc, T])
        CKT = s.sb("CKT", [P, nkc, P])
        ck = s.sb("ck", [P, kw])
        cv = s.sb("cv", [P, kw])
        SB = 8 if even else 2
        sc_sb = s.sb("sc_sb", [P, SB, W + 1])
        if even:
            band = s.sb("band", [P, 512 + 384])
        else:
            bias = s.sb("bias", [P, 8, 14, GRID_W])
            bias_mid = s.sb("bias_mid", [P, 8, 10, GRID_W])
            zeros = s.sb("zeros", [P, P])
        sink = s.sb("sink", [P, 8])
        attention_setup(nc, io, keep, plan, locals())
        attention_units(nc, io, keep, plan, locals())


def attention_setup(nc, io, keep, plan, m):
    l, even, nkc, W = plan.l, plan.even, plan.nkc, plan.W
    tok, QT, KT, CKT, ck, cv, sink, sc_sb = (m[x] for x in ("tok", "QT", "KT", "CKT", "ck", "cv", "sink", "sc_sb"))
    tm_at, tmw, k_at, v_at, kw = (m[x] for x in ("tm_at", "tmw", "k_at", "v_at", "kw"))
    tm = io["tm"][l]
    cache = ("cache_attn_k", "cache_attn_v") if even else ("cache_na_k", "cache_na_v")
    outk, outv = ("new_attn_k", "new_attn_v") if even else ("new_na_k", "new_na_v")
    with Stage(nc, f"attnset{l}") as s:
        tok_in = [s.sem(f"tok_in{t}") for t in range(NT)]
        ck_in, cv_in, kv_out, mask_in = s.sem("ck_in"), s.sem("cv_in"), s.sem("kv_out"), s.pool_dma_sem("mask_in")
        roped, chain, turned, q_taken, k_taken = (s.sem(n) for n in ("roped", "rope_step", "turned", "q_taken", "k_taken"))
        pq = [s.ps(f"pq{i}", [P, BANK]) for i in range(2)]
        pk = [s.ps(f"pk{i}", [P, BANK]) for i in range(2)]
        if even:
            trig_in = s.sem("trig_in")
            trig = s.sb("trig", [P, 2, NTS, 32])
            c1 = s.sb("c1", [P, 10, 2, 32])
            s1 = s.sb("s1", [P, 10, 2, 32])
        else:
            pad = s.sb("pad", [120, P])
            colm = s.sb("colm", [P, GRID_W])
            pad_zero, bias_done = s.sem("pad_zero"), s.sem("bias_done")
            rpb_in, pad_out, bias_in = (s.pool_dma_sem(n) for n in ("rpb_in", "pad_out", "bias_in"))
        blk = s.block()

        @blk.sync
        def _(sp):
            for t in range(NT):
                sp.dma_start(tok[:, t, :], tm[t * P:(t + 1) * P, tm_at:tm_at + tmw]).then_inc(tok_in[t], 16)
            sp.dma_start(ck[:], io[cache[0]][0, 0].rearrange("t h d -> t (h d)")).then_inc(ck_in, 16)
            sp.dma_start(cv[:], io[cache[1]][0, 0].rearrange("t h d -> t (h d)")).then_inc(cv_in, 16)
            rows = tm[TS:T, :]
            sp.dma_start(io[outk][0, 0].rearrange("t h d -> t (h d)"), rows[:, tm_at + k_at:tm_at + k_at + kw]).then_inc(kv_out, 16)
            sp.dma_start(io[outv][0, 0].rearrange("t h d -> t (h d)"), rows[:, tm_at + v_at:tm_at + v_at + kw]).then_inc(kv_out, 16)
            sp.wait_ge(kv_out, 32)
            sp.wait_ge(cv_in, 16)

        @blk.tensor
        def _(pe):
            for n in range(NT + 1):
                cached = n == NT
                if cached:
                    pe.wait_ge(ck_in, 16)
                else:
                    pe.wait_ge(tok_in[n], 16)
                if even and n < NT:
                    pe.wait_ge(roped, n + 1)
                if n >= 2:
                    pe.wait_ge(q_taken, n - 1)
                    pe.wait_ge(k_taken, n - 1)
                if not cached:
                    for j in range(4):
                        nc.tensor.transpose(pq[n % 2][:, j * P:(j + 1) * P], tok[:, n, j * P:(j + 1) * P], keep.ident[:])
                for j in range(nkc):
                    src = ck[:, j * P:(j + 1) * P] if cached else tok[:, n, k_at + j * P:k_at + (j + 1) * P]
                    mm = nc.tensor.transpose(pk[n % 2][:, j * P:(j + 1) * P], src, keep.ident[:])
                mm.then_inc(turned, 1)

        @blk.scalar
        def _(act):
            if even:
                act.dma_start(trig[:, 0], io["cos"]).then_inc(trig_in, 16)
                act.dma_start(trig[:, 1], io["sin"]).then_inc(trig_in, 16)
            for n in range(NT):
                act.wait_ge(turned, n + 1)
                nc.scalar.activation(QT[:, :, n * P:(n + 1) * P], pq[n % 2][:].rearrange("p (j t) -> p j t", j=4),
                                     ACT.Copy, scale=HD ** -0.5).then_inc(q_taken, 1)

        @blk.gpsimd
        def _(pool):
            if even:
                pool.dma_start(m["band"][:], io["band"]).then_inc(mask_in, 16)
                pool.dma_start(sink[:], all_rows(io["attn_sink"][0])).then_inc(mask_in, 16)
                pool.wait_ge(mask_in, 32)
                nc.gpsimd.tensor_copy(sc_sb[:, :, W:W + 1], sink[:].rearrange("p (h o) -> p h o", o=1))
            else:
                bias, mid = m["bias"], m["bias_mid"]
                nc.gpsimd.memset(m["zeros"][:], 0.0)
                nc.gpsimd.memset(pad[:], 0.0).then_inc(pad_zero, 1)
                pool.wait_ge(pad_zero, 1)
                pool.dma_start(pad[:, 48:79], io["na_rpb"][0].rearrange("h r c -> (h r) c")).then_inc(rpb_in, 16)
                pool.dma_start(colm[:], io["colmask"]).then_inc(mask_in, 16)
                pool.wait_ge(rpb_in, 16)
                pool.dma_start(io["rpbpad"], pad[:].unsqueeze(1).broadcast_to([120, GRID_W, P])).then_inc(pad_out, 16)
                pool.wait_ge(pad_out, 16)
                for half in range(2):
                    flat = io["rpbpad"]
                    for h in range(8):
                        src = bass.AP(flat.tensor, flat.offset + (h * 15 + 1 - half) * GRID_W * P + 63,
                                      [[P - 1, 64], [GRID_W * P, 14], [1, GRID_W]])
                        pool.dma_start(bias[half * 64:half * 64 + 64, h], src).then_inc(bias_in, 16)
                pool.wait_ge(bias_in, 256)
                pool.wait_ge(mask_in, 16)
                flatb = bias[:].rearrange("p h r c -> p (h r) c")
                nc.gpsimd.tensor_tensor(flatb, flatb, colm[:].rearrange("p (o c) -> p o c", o=1).broadcast_to([P, 112, GRID_W]), ALU.add).then_inc(bias_done, 1)
                pool.wait_ge(bias_done, 1)
                nc.gpsimd.tensor_copy(mid[:], bias[:, :, 2:12, :]).then_inc(bias_done, 1)
                pool.wait_ge(bias_done, 2)
                nc.gpsimd.memset(mid[0:64, :, 8:10, :], NEG)
                nc.gpsimd.memset(mid[64:128, :, 0:1, :], NEG)
                nc.gpsimd.memset(mid[64:128, :, 9:10, :], NEG)

        def take_keys(dve, n):
            dve.wait_ge(turned, n + 1)
            dst = CKT[:] if n == NT else KT[:, :, n * P:(n + 1) * P]
            nc.vector.tensor_copy(dst, pk[n % 2][:, 0:kw].rearrange("p (j t) -> p j t", j=nkc)).then_inc(k_taken, 1)

        @blk.vector
        def _(dve):
            if even:
                dve.wait_ge(trig_in, 32)
            for n in range(NT):
                if even:
                    dve.wait_ge(tok_in[n], 16)
                    x = tok[:, n, 0:640].rearrange("p (h a d) -> p h a d", a=2, d=32)
                    q_out = tok[:, n, 0:512].rearrange("p (j s a d) -> p s j a d", s=2, a=2, d=32)
                    if n < NTS:
                        cos, sin = (trig[:, i, n:n + 1, :].unsqueeze(1).broadcast_to([P, 10, 2, 32]) for i in range(2))
                        nc.vector.tensor_tensor(c1[:], x, cos, ALU.mult).then_inc(chain, 1)
                        nc.vector.tensor_tensor(s1[:], x, sin, ALU.mult).then_inc(chain, 1)
                        dve.wait_ge(chain, 2 * n + 2)
                        for a, op in ((0, ALU.subtract), (1, ALU.add)):
                            nc.vector.tensor_tensor(x[:, 8:10, a, :], c1[:, 8:10, a, :], s1[:, 8:10, 1 - a, :], op)
                            ins = nc.vector.tensor_tensor(q_out[:, :, :, a, :], c1[:, 0:8, a, :].rearrange("p (s j) d -> p s j d", s=2),
                                                          s1[:, 0:8, 1 - a, :].rearrange("p (s j) d -> p s j d", s=2), op)
                    else:
                        nc.vector.tensor_copy(c1[:], x).then_inc(chain, 1)
                        dve.wait_ge(chain, 2 * n + 1)
                        for a in range(2):
                            ins = nc.vector.tensor_copy(q_out[:, :, :, a, :], c1[:, 0:8, a, :].rearrange("p (s j) d -> p s j d", s=2))
                    ins.then_inc(roped, 1)
                    dve.wait_ge(roped, n + 1)
                if n >= 1:
                    take_keys(dve, n - 1)
            take_keys(dve, NT - 1)
            take_keys(dve, NT)


def attention_units(nc, io, keep, plan, m):
    l, even, W, units, groups = plan.l, plan.even, plan.W, plan.units, plan.groups
    tok, QT, KT, CKT, cv, sink, sc_sb, SB, v_at = (m[x] for x in ("tok", "QT", "KT", "CKT", "cv", "sink", "sc_sb", "SB", "v_at"))
    NU, NG, WB = len(units), len(groups), -(-W // BANK) * BANK
    RT = 2 if even else 1
    row0 = 0 if even else MIX
    with Stage(nc, f"attnrun{l}") as s:
        mx1 = s.sb("mx1", [P, 4])
        mx = s.sb("mx", [P, 4])
        neg = s.sb("neg", [P, 4])
        prob = s.sb("prob", [P, 2, W + 1])
        rs = s.sb("rs", [P, 2, 8])
        rinv = s.sb("rinv", [P, 2, 8])
        pT = s.sb("pT", [P, 2, W])
        o_sb = s.sb("o_sb", [P, 2, 8, HD])
        oT = s.sb("oT", [P, 2, 4, P])
        psc = [s.ps(f"sc{i}", [P, WB]) for i in range(2)]
        pt = [s.ps(f"pt{i}", [P, WB]) for i in range(RT)]
        po = s.ps("po", [P, 8, P])
        sc_done, red_part, red_done, neg_done, exp_done = (s.sem(n) for n in ("sc_done", "red_part", "red_done", "neg_done", "exp_done"))
        p_turned, pT_done, pv_done, rinv_done, o_done, o_turned, oT_done = (
            s.sem(n) for n in ("p_turned", "pT_done", "pv_done", "rinv_done", "o_done", "o_turned", "oT_done"))
        out = [s.sem(f"oT_out{i}") for i in range(2)]
        blk = s.block()

        turns = []
        for u in range(NU):
            turns.append(("p", u))
            if u % 8 == 1 and u >= 8:
                turns.append(("o", u // 8 - 1))
        turns.append(("o", NG - 1))

        def slot_free(eng, what):
            n = turns.index(what)
            if n >= RT:
                kind, i = turns[n - RT]
                eng.wait_ge(pT_done if kind == "p" else oT_done, i + 1)
            return pt[n % RT]

        def slot(what):
            return pt[turns.index(what) % RT]

        def scores(pe, u):
            g, h = units[u]
            t, keys, cached = groups[g]
            j, half = plan.chunk_half(h)
            rows = slice(64 * half, 64 * half + 64)
            if u >= 2:
                pe.wait_ge(red_done, u - 1)
            q = QT[rows, j, t * P:(t + 1) * P]
            tiles = [KT[rows, plan.kv_chunk(h), k * P:(k + 1) * P] for k in keys]
            if cached:
                tiles = [CKT[rows, plan.kv_chunk(h), :]] + tiles if even else tiles + [CKT[rows, plan.kv_chunk(h), :]]
            at = W - P * len(tiles)
            for i, k in enumerate(tiles):
                mm = nc.tensor.matmul(psc[u % 2][:, at + i * P:at + (i + 1) * P], q, k, start=True, stop=True)
            mm.then_inc(sc_done, 1)

        def turn_probs(pe, u):
            n = plan.columns(units[u][0]) // P
            dst = slot_free(pe, ("p", u))
            pe.wait_ge(exp_done, u + 1)
            for i in range(n):
                mm = nc.tensor.transpose(dst[:, i * P:(i + 1) * P], prob[:, u % 2, W - (n - i) * P:W - (n - i - 1) * P], keep.ident[:])
            mm.then_inc(p_turned, 1)

        def values(pe, u):
            g, h = units[u]
            t, keys, cached = groups[g]
            at = P * plan.kv_chunk(h)
            tiles = [tok[:, k, v_at + at:v_at + at + P] for k in keys]
            if cached:
                tiles = [cv[:, at:at + P]] + tiles if even else tiles + [cv[:, at:at + P]]
            if h == 0 and g >= 1:
                pe.wait_ge(o_done, g)
            pe.wait_ge(pT_done, u + 1)
            for i, v in enumerate(tiles):
                mm = nc.tensor.matmul(po[:, h, :], pT[:, u % 2, i * P:(i + 1) * P], v, start=i == 0, stop=i == len(tiles) - 1)
            mm.then_inc(pv_done, 1)

        def turn_outputs(pe, g):
            dst = slot_free(pe, ("o", g))
            pe.wait_ge(o_done, g + 1)
            for j in range(4):
                mm = nc.tensor.transpose(dst[:, j * P:(j + 1) * P], o_sb[:, g % 2, 2 * j:2 * j + 2, :], keep.ident[:])
            mm.then_inc(o_turned, 1)

        @blk.tensor
        def _(pe):
            scores(pe, 0)
            scores(pe, 1)
            for u in range(NU):
                turn_probs(pe, u)
                if u + 2 < NU:
                    scores(pe, u + 2)
                if u >= 1:
                    values(pe, u - 1)
                if u % 8 == 1 and u >= 8:
                    turn_outputs(pe, u // 8 - 1)
            values(pe, NU - 1)
            turn_outputs(pe, NG - 1)

        @blk.vector
        def _(dve):
            parts = 0

            def take_probs(u):
                n = plan.columns(units[u][0])
                if u >= 2:
                    dve.wait_ge(pv_done, u - 1)
                dve.wait_ge(p_turned, u + 1)
                nc.vector.tensor_copy(pT[:, u % 2, 0:n], slot(("p", u))[:, 0:n]).then_inc(pT_done, 1)

            def take_outputs(g):
                dve.wait_ge(exp_done, 8 * (g + 1))
                nc.vector.reciprocal(rinv[:, g % 2, :], rs[:, g % 2, :]).then_inc(rinv_done, 1)
                dve.wait_ge(rinv_done, g + 1)
                dve.wait_ge(pv_done, 8 * (g + 1))
                if g >= 2:
                    dve.wait_ge(o_turned, g - 1)
                for half in range(2):
                    if even:
                        src, r, dst = po[:, 4 * half:4 * half + 4, 64 * half:64 * half + 64], rinv[:, g % 2, 4 * half:4 * half + 4], o_sb[:, g % 2, 4 * half:4 * half + 4, :]
                    else:
                        src, r, dst = po[:, half:8:2, 64 * half:64 * half + 64], rinv[:, g % 2, half:8:2], o_sb[:, g % 2, half:8:2, :]
                    ins = nc.vector.tensor_tensor(dst, src, r.unsqueeze(2).broadcast_to([P, 4, HD]), ALU.mult)
                ins.then_inc(o_done, 1)

            for u in range(NU + 2):
                if u < NU:
                    g, h = units[u]
                    t, keys, cached = groups[g]
                    n = plan.columns(g)
                    at = W - n
                    dve.wait_ge(sc_done, u + 1)
                    if u >= SB:
                        dve.wait_ge(exp_done, u - SB + 1)
                    if u >= 4:
                        dve.wait_ge(exp_done, u - 3)
                    red = mx[:, u % 4:u % 4 + 1]
                    if even:
                        band = m["band"]
                        mask = band[:, 512:896] if g == 0 else band[:, 0:n]
                        nc.vector.tensor_tensor_reduce(out=sc_sb[:, u % SB, at:W], in0=psc[u % 2][:, at:W], in1=mask, scale=1.0,
                                                       scalar=sink[:, h:h + 1], op0=ALU.add, op1=ALU.max, accum_out=red).then_inc(red_done, 1)
                    elif not cached:
                        nc.vector.tensor_tensor_reduce(out=sc_sb[:, u % SB, at:W], in0=psc[u % 2][:, at:W], in1=m["zeros"][:, 0:n], scale=1.0,
                                                       scalar=-3e38, op0=ALU.add, op1=ALU.max, accum_out=red).then_inc(red_done, 1)
                    else:
                        r0 = 2 * t
                        first = 2 * keys[0] - r0
                        nrow = 2 * len(keys)
                        src = m["bias_mid"][:, h, :, :] if nrow == 10 else m["bias"][:, h, first + 6:first + 6 + nrow, :]
                        nc.vector.tensor_tensor_reduce(out=sc_sb[:, u % SB, W - P:W], in0=psc[u % 2][:, W - P:W], in1=m["zeros"][:], scale=1.0,
                                                       scalar=-3e38, op0=ALU.add, op1=ALU.max, accum_out=mx1[:, u % 4:u % 4 + 1]).then_inc(red_part, 1)
                        parts += 1
                        dve.wait_ge(red_part, parts)
                        nc.vector.tensor_tensor_reduce(out=sc_sb[:, u % SB, at:W - P], in0=psc[u % 2][:, at:W - P], in1=src.rearrange("p r c -> p (r c)"), scale=1.0,
                                                       scalar=mx1[:, u % 4:u % 4 + 1], op0=ALU.add, op1=ALU.max, accum_out=red).then_inc(red_done, 1)
                    dve.wait_ge(red_done, u + 1)
                    nc.vector.tensor_scalar(neg[:, u % 4:u % 4 + 1], red, -1.0, None, ALU.mult).then_inc(neg_done, 1)
                if 1 <= u <= NU:
                    take_probs(u - 1)
                if u >= 9 and (u - 9) % 8 == 0:
                    take_outputs((u - 9) // 8)

        @blk.scalar
        def _(act):
            def take_turned(g):
                if g >= 2:
                    act.wait_ge(out[g % 2], 16 * (g // 2))
                act.wait_ge(o_turned, g + 1)
                nc.scalar.activation(oT[:, g % 2], slot(("o", g))[:, 0:BANK].rearrange("p (j t) -> p j t", j=4), ACT.Copy).then_inc(oT_done, 1)

            for u in range(NU):
                g, h = units[u]
                at = W - plan.columns(g)
                act.wait_ge(neg_done, u + 1)
                if u >= 2:
                    act.wait_ge(p_turned, u - 1)
                if h == 0 and g >= 2:
                    act.wait_ge(rinv_done, g - 1)
                end = W + 1 if even else W
                nc.scalar.activation(prob[:, u % 2, at:end], sc_sb[:, u % SB, at:end], ACT.Exp, bias=neg[:, u % 4:u % 4 + 1],
                                     accum_out=rs[:, g % 2, h:h + 1]).then_inc(exp_done, 1)
                if u % 8 == 3 and u >= 8:
                    take_turned(u // 8 - 1)
            take_turned(NG - 1)

        @blk.sync
        def _(sp):
            for g, (t, _, _) in enumerate(groups):
                sp.wait_ge(oT_done, g + 1)
                sp.dma_start(io["mixT"][l][row0:row0 + MIX, t * P:(t + 1) * P].rearrange("(j p) t -> p j t", p=P), oT[:, g % 2]).then_inc(out[g % 2], 16)
            for i in range(2):
                sp.wait_ge(out[i], 16 * len(range(i, NG, 2)))



SIN_TURN = 2.0 * math.pi
TURN_HI = 6.28125
TURN_LO = SIN_TURN - TURN_HI
ROUND = 1.5 * 2.0 ** 23
PI_DOWN = 3.1415925


def hyena_filters(nc, io, keep):
    FW = 64
    with Stage(nc, "filt") as s:
        feats = s.sb("feats", [33, T])
        w1 = s.sb("w1", [33, FW])
        w2 = s.sb("w2", [FW, FW])
        w3 = s.sb("w3", [FW, 4 * MIX])
        cols = s.sb("cols", [FW, 3])
        fb = s.sb("fb", [FW, 2])
        arg = s.sb("arg", [FW, T])
        turns = s.sb("turns", [FW, T])
        hid = [s.sb(f"hid{i}", [FW, T]) for i in range(2)]
        win = s.sb("win", [P, NT, MIX])
        win_b = s.sb("win_b", [P, 2, MIX])
        A = s.sb("A", [P, 2, MIX])
        B = s.sb("B", [P, 2, MIX])
        absA = s.sb("absA", [P, 2, MIX])
        absB = s.sb("absB", [P, 2, MIX])
        taps = s.sb("taps", [P, NT, 2, 2 * MIX])
        ones = s.sb("ones", [P, P])
        inv = s.sb("inv", [P, 2 * MIX])
        cf = s.sb("cf", [P, 2, NTS, 512])
        cfp = s.sb("cfp", [P, 2, P])
        first = s.sb("first", [P, 2, MIX])
        res = s.sb("res", [P, 2, 2, MIX])
        bk = [s.ps(f"b{i}", [P, BANK]) for i in range(2)]
        hp = s.ps("hp", [P, 4, MIX])
        sp_ = s.ps("sum", [P, 2, MIX])
        small_in, w3_in, win_in, cf_in = s.sem("small_in"), s.sem("w3_in"), s.sem("win_in"), s.sem("cf_in")
        hid_mm, arg_done, red, sin_done = s.sem("hid_mm"), s.sem("arg_done"), s.sem("reduced"), s.sem("sin_done")
        chain, h_done, ab_done, abs_done, abs_sum, taps_done, sum_done = (
            s.sem(n) for n in ("chain", "h_done", "ab_done", "abs_done", "abs_sum", "taps_done", "sum_done"))
        inv_done, inv_turned, inv_taken = s.sem("inv_done"), s.sem("inv_turned"), s.sem("inv_taken")
        dft_done, first_done, res_done, ones_set = s.sem("dft_done"), s.sem("first_done"), s.sem("res_done"), s.sem("ones_set")
        res_out = [s.sem(f"res_out{i}") for i in range(2)]
        blk = s.block()
        spans = [(0, 512), (512, 512), (1024, 128)]
        jobs = [(q, o, cs) for q in range(4) for o in range(2) for cs in range(2)] + [(8, o, cs) for o in range(2) for cs in range(2)]

        @blk.sync
        def _(sp):
            sp.dma_start(feats[:], io["feats"]).then_inc(small_in, 16)
            sp.dma_start(w1[:], io["hy_w1"][0]).then_inc(small_in, 16)
            sp.dma_start(w2[:], io["hy_w2"][0]).then_inc(small_in, 16)
            for i, n in enumerate(("hy_b1", "hy_b2", "hy_freq")):
                sp.dma_start(cols[:, i:i + 1], io[n][0].rearrange("(p o) -> p o", o=1), allow_slow_non_contiguous=True).then_inc(small_in, 16)
            sp.dma_start(w3[:], io["hy_w3"][0]).then_inc(w3_in, 16)
            sp.dma_start(win[:], io["win"].rearrange("(t p) c -> p t c", p=P)).then_inc(win_in, 16)
            sp.dma_start(win_b[:], io["win_b"].rearrange("t p c -> p t c")).then_inc(win_in, 16)
            for i in range(2):
                sp.dma_start(cf[:, i], io["filt_dft"][i].rearrange("(t p) f -> p t f", p=P)).then_inc(cf_in, 16)
                sp.dma_start(cfp[:, i], io["filt_dft_p"][i]).then_inc(cf_in, 16)
            for n, (q, o, cs) in enumerate(jobs):
                sp.wait_ge(res_done, n + 1)
                sp.dma_start(io["spec"][q, :, o, cs, :], res[:, n % 2, 0, :]).then_inc(res_out[n % 2], 16)
                if q < 8:
                    sp.dma_start(io["spec"][4 + q, :, o, cs, :], res[:, n % 2, 1, :]).then_inc(res_out[n % 2], 16)
            for i in range(2):
                sp.wait_ge(res_out[i], 16 * sum(1 if q == 8 else 2 for q, _, _ in jobs[i::2]))

        def sums(pe, t):
            if t == NTS:
                pe.wait_ge(inv_done, 1)
            pe.wait_ge(abs_sum, t + 1)
            for o in range(2):
                mm = nc.tensor.matmul(sp_[:, o, :], ones[:], absA[:, o, :], start=t in (0, NTS), stop=t >= NTS - 1)
            mm.then_inc(sum_done, 1)

        @blk.tensor
        def _(pe):
            pe.wait_ge(small_in, 96)
            for layer in range(2):
                if layer:
                    pe.wait_ge(sin_done, 1)
                for i, (at, w) in enumerate(spans):
                    dst = (bk + [hp[:, 0, :]])[i]
                    lhs, rhs = (w1[:], feats[:, at:at + w]) if layer == 0 else (w2[:], hid[0][:, at:at + w])
                    mm = nc.tensor.matmul(dst[0:FW, 0:w], lhs, rhs, start=True, stop=True)
                mm.then_inc(hid_mm, 1)
            pe.wait_ge(sin_done, 2)
            pe.wait_ge(w3_in, 16)
            pe.wait_ge(ones_set, 1)
            for t in range(NT):
                if t:
                    pe.wait_ge(ab_done, t)
                for j in range(4):
                    mm = nc.tensor.matmul(hp[:, j, :], hid[1][:, t * P:(t + 1) * P], w3[:, j * MIX:(j + 1) * MIX], start=True, stop=True)
                mm.then_inc(h_done, 1)
                if t >= 1:
                    sums(pe, t - 1)
            sums(pe, NT - 1)
            for l in range(2):
                pe.wait_ge(inv_done, l + 1)
                for j in range(8):
                    mm = nc.tensor.transpose(hp[:, j // 4, (j % 4) * P:(j % 4 + 1) * P], inv[:, j * P:(j + 1) * P], keep.ident[:])
                mm.then_inc(inv_turned, 1)
            pe.wait_ge(taps_done, NT)
            pe.wait_ge(inv_taken, 2)
            pe.wait_ge(cf_in, 64)
            for n, (q, o, cs) in enumerate(jobs):
                if n >= 2:
                    pe.wait_ge(res_done, n - 1)
                pair = [hp[:, 2 * (n % 2), :], hp[:, 2 * (n % 2) + 1, :]]
                if q == 8:
                    mm = nc.tensor.matmul(pair[0], cfp[:, cs, :], taps[:, 8, cs, o * MIX:(o + 1) * MIX], start=True, stop=True)
                else:
                    for par in range(2):
                        for k in range(4):
                            mm = nc.tensor.matmul(pair[par], cf[:, cs, 4 * par + k, q * P:(q + 1) * P],
                                                  taps[:, 4 * par + k, cs, o * MIX:(o + 1) * MIX], start=k == 0, stop=k == 3)
                mm.then_inc(dft_done, 1)

        @blk.scalar
        def _(act):
            act.wait_ge(small_in, 96)
            for layer in range(2):
                nc.scalar.activation(fb[:, layer:layer + 1], cols[:, layer:layer + 1], ACT.Identity, scale=cols[:, 2:3]).then_inc(arg_done, 1)
                act.wait_ge(arg_done, 4 * layer + 1)
                act.wait_ge(hid_mm, layer + 1)
                for i, (at, w) in enumerate(spans):
                    src = (bk + [hp[:, 0, :]])[i]
                    nc.scalar.activation(arg[:, at:at + w], src[0:FW, 0:w], ACT.Identity, bias=fb[:, layer:layer + 1], scale=cols[:, 2:3]).then_inc(arg_done, 1)
                act.wait_ge(red, layer + 1)
                nc.scalar.activation(hid[layer][:], arg[:], ACT.Sin).then_inc(sin_done, 1)
            for t in range(NT):
                act.wait_ge(ab_done, t + 1)
                if t:
                    act.wait_ge(sum_done, t)
                nc.scalar.activation(absA[:], A[:], ACT.Abs)
                nc.scalar.activation(absB[:], B[:], ACT.Abs).then_inc(abs_done, 1)
            for n, (q, o, cs) in enumerate(jobs):
                act.wait_ge(dft_done, n + 1)
                if n >= 2:
                    act.wait_ge(res_done, n - 1)
                nc.scalar.activation(first[:, n % 2, :], hp[:, 2 * (n % 2), :], ACT.Copy).then_inc(first_done, 1)

        @blk.gpsimd
        def _(pool):
            nc.gpsimd.memset(ones[:], 1.0).then_inc(ones_set, 1)
            for t in range(NT):
                pool.wait_ge(abs_done, t + 1)
                nc.gpsimd.tensor_tensor(absA[:], absA[:], absB[:], ALU.add).then_inc(abs_sum, 1)

        def take_sums(dve, l):
            dve.wait_ge(sum_done, NTS + l)
            if l:
                dve.wait_ge(inv_turned, 1)
            nc.vector.reciprocal(inv[:], sp_[:].rearrange("p o c -> p (o c)")).then_inc(inv_done, 1)
            dve.wait_ge(inv_turned, l + 1)
            nc.vector.tensor_copy(keep.tap_scale[:, l, :], hp[:, 0:2, :].rearrange("p a (b c) -> p (a b) c", c=P)[:, :, 0]).then_inc(inv_taken, 1)

        @blk.vector
        def _(dve):
            link = Link(dve, chain)
            for layer in range(2):
                dve.wait_ge(arg_done, 4 * layer + 4)
                link(nc.vector.tensor_scalar(turns[:], arg[:], 1.0 / SIN_TURN, ROUND, ALU.mult, ALU.add))
                link(nc.vector.tensor_scalar(turns[:], turns[:], ROUND, None, ALU.subtract))
                link(nc.vector.scalar_tensor_tensor(arg[:], turns[:], -TURN_HI, arg[:], ALU.mult, ALU.add))
                link(nc.vector.scalar_tensor_tensor(arg[:], turns[:], -TURN_LO, arg[:], ALU.mult, ALU.add))
                nc.vector.tensor_scalar(arg[:], arg[:], PI_DOWN, -PI_DOWN, ALU.min, ALU.max).then_inc(red, 1)
            dve.wait_ge(win_in, 32)
            for t in range(NT):
                dve.wait_ge(h_done, t + 1)
                if t:
                    dve.wait_ge(abs_done, t)
                wa = win[:, t:t + 1, :].broadcast_to([P, 2, MIX])
                wb = win_b[:, t // NTS:t // NTS + 1, :].broadcast_to([P, 2, MIX]) if t in (0, NTS) else wa
                nc.vector.tensor_tensor(A[:], hp[:, 0:2, :], wa, ALU.mult)
                nc.vector.tensor_tensor(B[:], hp[:, 2:4, :], wb, ALU.mult).then_inc(ab_done, 1)
                dve.wait_ge(ab_done, t + 1)
                a, b = A[:].rearrange("p o c -> p (o c)"), B[:].rearrange("p o c -> p (o c)")
                nc.vector.tensor_tensor(taps[:, t, 0, :], a, b, ALU.add)
                nc.vector.tensor_tensor(taps[:, t, 1, :], a, b, ALU.subtract).then_inc(taps_done, 1)
                dve.wait_ge(taps_done, t + 1)
                if t == NT - 1:
                    take_sums(dve, 0)
            take_sums(dve, 1)
            for n, (q, o, cs) in enumerate(jobs):
                if n >= 2:
                    dve.wait_ge(res_out[n % 2], 16 * sum(1 if j[0] == 8 else 2 for j in jobs[n % 2:n:2]))
                dve.wait_ge(first_done, n + 1)
                f, second = first[:, n % 2, :], hp[:, 2 * (n % 2) + 1, :]
                if q == 8:
                    nc.vector.tensor_copy(res[:, n % 2, 0, :], f).then_inc(res_done, 1)
                    continue
                nc.vector.tensor_tensor(res[:, n % 2, 0, :], second, f, ALU.add)
                if cs == 0:
                    nc.vector.tensor_tensor(res[:, n % 2, 1, :], f, second, ALU.subtract).then_inc(res_done, 1)
                else:
                    nc.vector.tensor_tensor(res[:, n % 2, 1, :], second, f, ALU.subtract).then_inc(res_done, 1)



class Signal:

    def __init__(self, i):
        self.i = i
        self.L = (TS, TP)[i]
        self.at = (0, TS)[i]
        self.half = self.L // 2
        self.rows = min(self.half, P)
        self.nt = self.half // self.rows
        self.ft = self.L // P
        self.spec0 = (0, NTS)[i]


def hyena_signals(nc, io, keep):
    NCH = MIX // P
    sigs = [Signal(0), Signal(1)]
    runs = [(g, o) for g in sigs for o in range(2)]
    with Stage(nc, "hyena") as s:
        u = s.sb("u", [P, NCH, TS])
        gate = s.sb("gate", [P, 2, TS])
        eo = s.sb("eo", [P, NCH, 2, TS // 2])
        eoT = s.sb("eoT", [P, 4, 2, MIX])
        fwd = s.sb("fwd", [P, 2, 4, TS])
        bwd = s.sb("bwd", [P, 2, 8, TS // 2])
        fwd_p = s.sb("fwd_p", [64, 2, P])
        bwd_p = s.sb("bwd_p", [P, 2, 64])
        spec = [s.sb(f"spec{i}", [P, 2, MIX]) for i in range(2)]
        prod = s.sb("prod", [P, 2, 2, MIX])
        Y = s.sb("Y", [P, 8, 2, MIX])
        odd = s.sb("odd", [P, 2, TS // 2])
        conv = s.sb("conv", [P, TS])
        skip = s.sb("skip", [P, 2, NCH])
        bk = [s.ps(f"b{i}", [P, BANK]) for i in range(8)]
        u_in = [s.sem(f"u_in{i}") for i in range(2)]
        mat_in = s.sem("mat_in")
        spec_in = [s.sem(f"spec_in{i}") for i in range(2)]
        gate_in = [s.sem(f"gate_in{i}") for i in range(2)]
        folded, turned, turn_taken, dft_done, prod_done, y_done, inv_done, odd_done, conv_done, u_done = (
            s.sem(n) for n in ("folded", "turned", "turn_taken", "dft_done", "prod_done", "y_done", "inv_done", "odd_done", "conv_step", "u_done"))
        u_out = s.sem("u_out")
        blk = s.block()
        FT = [g.ft for g, _ in runs]
        NTN = [g.nt for g, _ in runs]
        ft0 = [sum(FT[:r]) for r in range(5)]
        nt0 = [2 * sum(NTN[:r]) for r in range(5)]

        @blk.sync
        def _(sp):
            for c in range(NCH):
                sp.dma_start(u[:, c, :], io["conv"][0][c * P:(c + 1) * P, 0:TS]).then_inc(u_in[0], 16)
            for i in range(2):
                sp.dma_start(fwd[:, i], io["sig_dft"][i].rearrange("(t p) f -> p t f", p=P)).then_inc(mat_in, 16)
                sp.dma_start(fwd_p[:, i], io["sig_dft_p"][i]).then_inc(mat_in, 16)
                sp.dma_start(bwd_p[:, i], io["sig_idft_p"][i]).then_inc(mat_in, 16)
                sp.dma_start(bwd[:, i], io["sig_idft"][i].rearrange("(t p) n -> p t n", p=P)).then_inc(mat_in, 16)
                sp.dma_start(skip[:, i], io["hy_skip"][0, i].rearrange("(c p) -> p c", p=P), allow_slow_non_contiguous=True).then_inc(mat_in, 16)
            for r, (g, o) in enumerate(runs):
                for f in range(g.ft):
                    n = ft0[r] + f
                    if n >= 2:
                        sp.wait_ge(prod_done, 2 * (n - 1))
                    sp.dma_start(spec[n % 2][:], io["spec"][g.spec0 + f, :, o]).then_inc(spec_in[n % 2], 16)
                for c in range(NCH):
                    n = r * NCH + c
                    if n >= 2:
                        sp.wait_ge(u_done, n - 1)
                    row = MIX * (1 + o) + c * P
                    sp.dma_start(gate[:, n % 2, 0:g.L], io["conv"][0][row:row + P, g.at:g.at + g.L]).then_inc(gate_in[n % 2], 16)
                    if o == 1:
                        sp.wait_ge(u_done, n + 1)
                        sp.dma_start(io["mixT"][0][MIX + c * P:MIX + (c + 1) * P, g.at:g.at + g.L], u[:, c, 0:g.L]).then_inc(u_out, 16)
                if r == 1:
                    sp.wait_ge(u_out, 16 * NCH)
                    for c in range(NCH):
                        sp.dma_start(u[:, c, 0:TP], io["conv"][0][c * P:(c + 1) * P, TS:T]).then_inc(u_in[1], 16)
            sp.wait_ge(u_out, 32 * NCH)

        def ready(dve, r):
            if r % 2 == 0:
                dve.wait_ge(u_in[r // 2], 16 * NCH)
            else:
                dve.wait_ge(u_done, NCH * r)

        @blk.tensor
        def _(pe):
            pe.wait_ge(mat_in, 160)
            for r, (g, o) in enumerate(runs):
                fm, bm = (fwd, bwd) if g.i == 0 else (fwd_p, bwd_p)
                pe.wait_ge(folded, NCH * (r + 1))
                if r:
                    pe.wait_ge(odd_done, NCH * r)
                    pe.wait_ge(u_done, NCH * r)
                for t in range(g.nt):
                    for part in range(2):
                        n = nt0[r] + 2 * t + part
                        if n >= 2:
                            pe.wait_ge(turn_taken, n - 1)
                        for c in range(NCH):
                            mm = nc.tensor.transpose(bk[n % 2][0:g.rows, c * P:(c + 1) * P], eo[:, c, part, t * g.rows:(t + 1) * g.rows], keep.ident[:])
                        mm.then_inc(turned, 1)
                pe.wait_ge(turn_taken, nt0[r + 1])
                for f in range(g.ft):
                    n = ft0[r] + f
                    if n >= 2:
                        pe.wait_ge(prod_done, 2 * (n - 1))
                    for cs in range(2):
                        for t in range(g.nt):
                            lhs = fm[:, cs, t, f * P:(f + 1) * P] if g.i == 0 else fm[:, cs, :]
                            mm = nc.tensor.matmul(bk[2 + 2 * (n % 2) + cs][:], lhs, eoT[0:g.rows, t, cs, :], start=t == 0, stop=t == g.nt - 1)
                    mm.then_inc(dft_done, 1)
                pe.wait_ge(y_done, 2 * ft0[r + 1])
                for c in range(NCH):
                    n = r * NCH + c
                    if n >= 1:
                        pe.wait_ge(conv_done, 3 * n - 1)
                    for cs in range(2):
                        for f in range(g.ft):
                            rhs = bm[:, cs, f, :] if g.i == 0 else bm[:, cs, :]
                            mm = nc.tensor.matmul(bk[6 + cs][:, 0:g.half], Y[:, f, cs, c * P:(c + 1) * P], rhs, start=f == 0, stop=f == g.ft - 1)
                    mm.then_inc(inv_done, 1)

        @blk.scalar
        def _(act):
            for r, (g, o) in enumerate(runs):
                for n in range(nt0[r], nt0[r + 1]):
                    t, part = divmod(n - nt0[r], 2)
                    act.wait_ge(turned, n + 1)
                    if r:
                        act.wait_ge(dft_done, ft0[r])
                    nc.scalar.activation(eoT[0:g.rows, t, part, :], bk[n % 2][0:g.rows, :], ACT.Copy).then_inc(turn_taken, 1)
                for c in range(NCH):
                    n = r * NCH + c
                    act.wait_ge(inv_done, n + 1)
                    if n >= 2:
                        act.wait_ge(conv_done, 3 * (n - 1) - 1)
                    at = 4 * o + c
                    nc.scalar.activation(odd[:, n % 2, 0:g.half], bk[7][:, 0:g.half], ACT.Copy, scale=keep.tap_scale[:, g.i, at:at + 1]).then_inc(odd_done, 1)

        @blk.vector
        def _(dve):
            for r, (g, o) in enumerate(runs):
                h = g.half
                ready(dve, r)
                if r:
                    dve.wait_ge(turned, nt0[r])
                for c in range(NCH):
                    later, earlier = u[:, c, h:2 * h], u[:, c, h - 1::-1]
                    nc.vector.tensor_tensor(eo[:, c, 0, 0:h], later, earlier, ALU.add)
                    nc.vector.tensor_tensor(eo[:, c, 1, 0:h], later, earlier, ALU.subtract).then_inc(folded, 1)
                for f in range(g.ft):
                    n = ft0[r] + f
                    dve.wait_ge(dft_done, n + 1)
                    dve.wait_ge(spec_in[n % 2], 16 * (n // 2 + 1))
                    if n >= 1:
                        dve.wait_ge(y_done, 2 * n)
                    uc, us = bk[2 + 2 * (n % 2)], bk[3 + 2 * (n % 2)]
                    hc, hs = spec[n % 2][:, 0, :], spec[n % 2][:, 1, :]
                    nc.vector.tensor_tensor(prod[:, 0, 0, :], uc[:], hc, ALU.mult)
                    nc.vector.tensor_tensor(prod[:, 0, 1, :], us[:], hs, ALU.mult).then_inc(prod_done, 1)
                    nc.vector.tensor_tensor(prod[:, 1, 0, :], uc[:], hs, ALU.mult)
                    nc.vector.tensor_tensor(prod[:, 1, 1, :], us[:], hc, ALU.mult).then_inc(prod_done, 1)
                for c in range(NCH):
                    n = r * NCH + c
                    at = 4 * o + c
                    scale = keep.tap_scale[:, g.i, at:at + 1]
                    dve.wait_ge(odd_done, n + 1)
                    nc.vector.scalar_tensor_tensor(conv[:, h:2 * h], bk[6][:, 0:h], scale, odd[:, n % 2, 0:h], ALU.mult, ALU.add).then_inc(conv_done, 1)
                    nc.vector.scalar_tensor_tensor(conv[:, h - 1::-1], bk[6][:, 0:h], scale, odd[:, n % 2, 0:h], ALU.mult, ALU.subtract).then_inc(conv_done, 1)
                    dve.wait_ge(conv_done, 3 * n + 2)
                    nc.vector.scalar_tensor_tensor(conv[:, 0:g.L], u[:, c, 0:g.L], skip[:, o, c:c + 1], conv[:, 0:g.L], ALU.mult, ALU.add).then_inc(conv_done, 1)
                    dve.wait_ge(conv_done, 3 * n + 3)
                    dve.wait_ge(gate_in[n % 2], 16 * (n // 2 + 1))
                    nc.vector.tensor_tensor(u[:, c, 0:g.L], conv[:, 0:g.L], gate[:, n % 2, 0:g.L], ALU.mult).then_inc(u_done, 1)
                    dve.wait_ge(u_done, n + 1)

        @blk.gpsimd
        def _(pool):
            for r, (g, o) in enumerate(runs):
                if r:
                    pool.wait_ge(inv_done, NCH * r)
                for f in range(g.ft):
                    n = ft0[r] + f
                    pool.wait_ge(prod_done, 2 * n + 1)
                    nc.gpsimd.tensor_tensor(Y[:, f, 0, :], prod[:, 0, 0, :], prod[:, 0, 1, :], ALU.subtract).then_inc(y_done, 1)
                    pool.wait_ge(prod_done, 2 * n + 2)
                    nc.gpsimd.tensor_tensor(Y[:, f, 1, :], prod[:, 1, 0, :], prod[:, 1, 1, :], ALU.add).then_inc(y_done, 1)



def mix_out(nc, io, keep, l):
    w = io["even_w_out" if l == 0 else "odd_w_out"][0].rearrange("(k p) n -> p k n", p=P)
    with Stage(nc, f"out{l}") as s:
        x = s.sb("x", [P, NT, D])
        hT = s.sb("hT", [P, KD, T])
        mixT = s.sb("mixT", [P, KD, T])
        wo = s.sb("wo", [P, KD, D])
        gate = s.sb("gate", [P, 2, D])
        tmp = s.sb("tmp", [P, D])
        wr = s.sb("wr", [P, KD, E])
        logT = s.sb("logT", [E, T])
        lg = s.sb("lg", [P, NT, E])
        red = s.sb("red", [P, 2, NT])
        aff = s.sb("aff", [E, T])
        top = s.sb("top", [E, SLOTS])
        idx = s.sb("idx", [E, SLOTS], U32)
        idxf = s.sb("idxf", [E, SLOTS])
        norm = Norm(s, nc, keep, l, 1, x, hT)
        acc = [s.ps(f"acc{i}", [P, 2, BANK]) for i in range(2)]
        rt = [s.ps(f"rt{i}", [P, BANK]) for i in range(2)]
        x_in = [s.sem(f"x_in{t}") for t in range(NT)]
        mix_in, w_in, gate_in, wr_in = s.sem("mix_in"), s.sem("w_in"), s.sem("gate_in"), s.sem("wr_in")
        acc_done, gated, x_done, xn_out = s.sem("acc_done"), s.sem("gated"), s.sem("x_done"), s.sem("xn_out")
        x_out = s.sem("x_out")
        log_done, log_taken, log_turned, soft, prob_done, aff_turned, aff_done, top_step, top_done, slots_turned = (
            s.sem(n) for n in ("log_done", "log_taken", "log_turned", "soft_step", "prob_done", "aff_turned", "aff_done", "top_step", "top_done", "slots_turned"))
        shifted, exp_done = s.sem("shifted"), s.sem("exp_done")
        blk = s.block()

        @blk.sync
        def _(sp):
            sp.dma_start(mixT[:], io["mixT"][l].rearrange("(k p) t -> p k t", p=P)).then_inc(mix_in, 16)
            sp.dma_start(wo[:], w).then_inc(w_in, 16)
            for c in range(2):
                sp.dma_start(gate[:, c, :], all_rows(io["mrow"][l, c, 2 * D:3 * D])).then_inc(gate_in, 16)
            load_x(sp, io, x, x_in, io["x_of"][l])
            sp.dma_start(wr[:], io["moe_router"][l].rearrange("(k p) e -> p k e", p=P)).then_inc(wr_in, 16)
            for t in range(NT):
                sp.wait_ge(x_done, t + 1)
                sp.dma_start(io["x"][l][t * P:(t + 1) * P, :], x[:, t, :]).then_inc(x_out, 16)
            for t in range(NT):
                sp.wait_ge(norm.scaled, t + 1)
                sp.dma_start(io["xn"][t * P:(t + 1) * P, :], x[:, t, :]).then_inc(xn_out, 16)
            sp.wait_ge(xn_out, 16 * NT)

        @blk.tensor
        def _(pe):
            pe.wait_ge(mix_in, 16)
            pe.wait_ge(w_in, 16)
            for t in range(NT):
                if t >= 2:
                    pe.wait_ge(gated, t - 1)
                for h in range(2):
                    for k in range(KD):
                        mm = nc.tensor.matmul(acc[t % 2][:, h, :], mixT[:, k, t * P:(t + 1) * P], wo[:, k, h * BANK:(h + 1) * BANK],
                                              start=k == 0, stop=k == KD - 1)
                mm.then_inc(acc_done, 1)
            norm.tensor(pe)
            pe.wait_ge(wr_in, 16)
            pe.wait_ge(norm.taken, norm.TURNS)
            for n, (at, width, _) in enumerate(token_groups()):
                if n == 2:
                    pe.wait_ge(log_taken, 1)
                for k in range(KD):
                    mm = nc.tensor.matmul(rt[n % 2][0:E, 0:width], wr[:, k, :], hT[:, k, at:at + width], start=k == 0, stop=k == KD - 1)
                mm.then_inc(log_done, 1)
            pe.wait_ge(log_taken, 3)
            for t in range(NT):
                mm = nc.tensor.transpose(rt[1][:, t * E:(t + 1) * E], logT[:, t * P:(t + 1) * P], keep.ident[0:E, 0:E])
            mm.then_inc(log_turned, 1)
            pe.wait_ge(prob_done, 1)
            for t in range(NT):
                dst = acc[0][0:E, t // 4, (t % 4) * P:(t % 4 + 1) * P] if t < 8 else acc[1][0:E, 0, 0:P]
                mm = nc.tensor.transpose(dst, lg[:, t, :], keep.ident[:])
            mm.then_inc(aff_turned, 1)
            pe.wait_ge(top_done, 1)
            for n, src in enumerate((idxf, top)):
                nc.tensor.transpose(rt[0][:, n * E:(n + 1) * E], src[:, 0:CAP_S], keep.ident[0:E, 0:E])
                mm = nc.tensor.transpose(rt[1][0:CAP_P, n * E:(n + 1) * E], src[:, CAP_S:SLOTS], keep.ident[0:E, 0:E])
            mm.then_inc(slots_turned, 1)

        @blk.scalar
        def _(act):
            norm.scalar(act, lambda eng, t: eng.wait_ge(x_done, t + 1))
            for n, (at, width, _) in enumerate(token_groups()):
                act.wait_ge(log_done, n + 1)
                nc.scalar.activation(logT[:, at:at + width], rt[n % 2][0:E, 0:width], ACT.Copy).then_inc(log_taken, 1)
            act.wait_ge(shifted, 1)
            nc.scalar.activation(lg[:], lg[:], ACT.Exp).then_inc(exp_done, 1)

        @blk.vector
        def _(dve):
            dve.wait_ge(gate_in, 32)
            for t in range(NT):
                dve.wait_ge(acc_done, t + 1)
                nc.vector.tensor_tensor(tmp[:], acc[t % 2][:].rearrange("p h n -> p (h n)"), gate[:, t // NTS, :], ALU.mult).then_inc(gated, 1)
                dve.wait_ge(gated, t + 1)
                dve.wait_ge(x_in[t], 16)
                nc.vector.tensor_tensor(x[:, t, :], x[:, t, :], tmp[:], ALU.add).then_inc(x_done, 1)
                dve.wait_ge(x_done, t + 1)
            dve.wait_ge(x_out, 16 * NT)
            norm.vector_scale(dve)
            norm.vector_turn(dve)
            link = Link(dve, soft)
            dve.wait_ge(log_turned, 1)
            logits = rt[1][:, 0:NT * E].rearrange("p (t e) -> p t e", e=E)
            link(nc.vector.tensor_reduce(red[:, 0, :], logits, axis=AX.X, op=ALU.max))
            nc.vector.tensor_tensor(lg[:], logits, red[:, 0, :].unsqueeze(2).broadcast_to([P, NT, E]), ALU.subtract).then_inc(shifted, 1)
            dve.wait_ge(shifted, 1)
            dve.wait_ge(exp_done, 1)
            link(nc.vector.tensor_reduce(red[:, 0, :], lg[:], axis=AX.X, op=ALU.add))
            link(nc.vector.reciprocal(red[:, 1, :], red[:, 0, :]))
            nc.vector.tensor_tensor(lg[:], lg[:], red[:, 1, :].unsqueeze(2).broadcast_to([P, NT, E]), ALU.mult).then_inc(prob_done, 1)
            dve.wait_ge(aff_turned, 1)
            nc.vector.tensor_copy(aff[:, 0:TS], acc[0][0:E, :, :].rearrange("p h n -> p (h n)"))
            nc.vector.tensor_copy(aff[:, TS:T], acc[1][0:E, 0, 0:P]).then_inc(aff_done, 1)
            dve.wait_ge(aff_done, 1)
            best = Link(dve, top_step)
            for n in range(SLOTS // 8):
                row = aff[:, 0:TS] if n < CAP_S // 8 else aff[:, TS:T]
                eight = slice(8 * n, 8 * n + 8)
                best(nc.vector.max(top[:, eight], row))
                nc.vector.max_index(idx[:, eight], top[:, eight], row)
                best(nc.vector.match_replace(row, top[:, eight], row, -1.0))
            best(nc.vector.tensor_copy(idxf[:], idx[:]))
            nc.vector.tensor_scalar(idxf[:, CAP_S:SLOTS], idxf[:, CAP_S:SLOTS], float(TS), None, ALU.add).then_inc(top_done, 1)
            dve.wait_ge(slots_turned, 1)
            for dst, src, rows in ((keep.slot_s, rt[0], CAP_S), (keep.slot_p, rt[1], CAP_P)):
                nc.vector.tensor_copy(dst[0:rows, 0:E], src[0:rows, 0:E])
                nc.vector.tensor_copy(dst[0:rows, E:E + 1], src[0:rows, 0:1])
            nc.vector.tensor_copy(keep.gate_s[:], rt[0][:, E:2 * E])
            nc.vector.tensor_copy(keep.gate_p[0:CAP_P, :], rt[1][0:CAP_P, E:2 * E])


def experts(nc, io, keep, l):
    FC = D // P
    weights = [io[n][l] for n in ("moe_w_gate", "moe_w_up", "moe_w_down")]
    with Stage(nc, f"moe{l}") as s:
        w = [s.sb(f"w{i}", [P, KD, D]) for i in range(3)]
        xg = [s.sb(f"xg{i}", [P, D]) for i in range(2)]
        xgp = [s.sb(f"xgp{i}", [CAP_P, D]) for i in range(2)]
        slot = [s.sb(f"slot{i}", [P, 1], U32) for i in range(2)]
        slotp = [s.sb(f"slotp{i}", [CAP_P, 1], U32) for i in range(2)]
        xT = s.sb("xT", [P, KD, SLOTS])
        sg = s.sb("sg", [P, FC, SLOTS])
        gu = s.sb("gu", [P, FC, SLOTS])
        yT = s.sb("yT", [P, KD, SLOTS])
        ys = [s.sb(f"ys{i}", [P, D]) for i in range(2)]
        yp = [s.sb(f"yp{i}", [CAP_P, D]) for i in range(2)]
        rowg = s.sb("rowg", [P, 2, D])
        bk = [s.ps(f"b{i}", [P, BANK]) for i in range(3)]
        bx = [s.ps(f"x{i}", [P, BANK]) for i in range(2)]
        by = [s.ps(f"y{i}", [P, BANK]) for i in range(2)]
        byp = s.ps("yp", [P, BANK])
        w_in = [s.sem(f"w_in{i}") for i in range(3)]
        g_mm, u_mm, d_mm = s.sem("g_mm"), s.sem("u_mm"), s.sem("d_mm")
        mm_sems = (g_mm, u_mm, d_mm)
        sg_done, gu_done, yT_done = s.sem("sg_done"), s.sem("gu_done"), s.sem("yT_done")
        slot_set = s.sem("slot_set")
        xg_in = [s.pool_dma_sem(f"xg_in{i}") for i in range(2)]
        x_turned, xT_done = s.sem("x_turned"), s.sem("xT_done")
        y_turned, yp_turned, ys_done, yp_done = s.sem("y_turned"), s.sem("yp_turned"), s.sem("ys_done"), s.sem("yp_done")
        row_in, fetching, results_free = s.sem("row_in"), s.sem("fetching"), s.sem("results_free")
        added = [s.pool_dma_sem(f"added{i}") for i in range(2)]
        blk = s.block()

        @blk.sync
        def _(sp):
            for c in range(2):
                sp.dma_start(rowg[:, c, :], all_rows(io["mrow"][l, c, 5 * D:6 * D])).then_inc(row_in, 16)
            with sp.Fori(0, E) as e:
                for i in range(3):
                    sp.wait_ge(mm_sems[i], e * FC + FC)
                    sp.dma_start(w[i][:], weights[i][bass.ds(e, 1)].rearrange("o (k p) n -> p (o k) n", p=P)).then_inc(w_in[i], 16)

        def set_slots(pool, e, par):
            nc.gpsimd.tensor_copy(slot[par][:], keep.slot_s[:, bass.ds(e, 1)])
            nc.gpsimd.tensor_copy(slotp[par][:], keep.slot_p[0:CAP_P, bass.ds(e, 1)]).then_inc(slot_set, 1)

        def fetch(pool, par):
            for dst, sl in ((xg, slot), (xgp, slotp)):
                nc.gpsimd.indirect_dma_start(out=dst[par][:], out_offset=None, in_=io["xn"],
                                             in_offset=bass.IndirectOffsetOnAxis(ap=sl[par][:, 0:1], axis=0)).then_inc(xg_in[par], 16)

        def add_back(pool, par):
            for src, sl in ((ys, slot), (yp, slotp)):
                nc.gpsimd.indirect_dma_start(out=io["x"][l], out_offset=bass.IndirectOffsetOnAxis(ap=sl[par][:, 0:1], axis=0),
                                             in_=src[par][:], in_offset=None, compute_op=ALU.add).then_inc(added[par], 16)

        @blk.gpsimd
        def _(pool):
            pool.sem_inc(results_free, 2)
            set_slots(pool, 0, 0)
            pool.wait_ge(slot_set, 1)
            fetch(pool, 0)
            with pool.Fori(0, E // 2) as i:
                for j in range(2):
                    set_slots(pool, i * 2 + (j + 1), 1 - j)
                    pool.wait_ge(slot_set, i * 2 + (j + 2))
                    pool.wait_ge(x_turned, i * (2 * KD) + (j + 1) * KD)
                    pool.sem_inc(fetching, 1)
                    fetch(pool, 1 - j)
                    pool.wait_ge(ys_done, i * 4 + (2 * j + 4))
                    pool.wait_ge(yp_done, i * 4 + (2 * j + 3))
                    pool.sem_inc(fetching, 1)
                    add_back(pool, j)
                    pool.wait_ge(added[j], i * 32 + 32)
                    pool.sem_inc(results_free, 1)
            pool.wait_ge(xg_in[0], 32 * (E // 2 + 1))

        def turn_tokens(pe, par, base):
            for k in range(KD):
                pe.wait_ge(xT_done, base + (k + 1))
                nc.tensor.transpose(bx[k % 2][:, 0:CAP_S], xg[par][:, k * P:(k + 1) * P], keep.ident[:])
                nc.tensor.transpose(bx[k % 2][:, CAP_S:SLOTS], xgp[par][:, k * P:(k + 1) * P],
                                    keep.ident[0:CAP_P, 0:CAP_P]).then_inc(x_turned, 1)

        def turn_results(pe, i, j, f, e8):
            h, q = divmod(f, 4)
            if q == 0:
                pe.wait_ge(ys_done, i * 4 + (2 * j + h + 1))
                pe.wait_ge(yp_done, i * 4 + (2 * j + h + 1))
            pe.wait_ge(yT_done, e8(FC + f + 1))
            ms = nc.tensor.transpose(by[h][:, q * P:(q + 1) * P], yT[:, f, 0:CAP_S], keep.ident[:])
            if q == 3:
                ms.then_inc(y_turned, 1)
            mp = nc.tensor.transpose(byp[0:CAP_P, q * P:(q + 1) * P], yT[:, f, CAP_S:SLOTS], keep.ident[:])
            if q == 3:
                mp.then_inc(yp_turned, 1)

        @blk.tensor
        def _(pe):
            for q, n in ((g_mm, FC), (u_mm, FC), (d_mm, FC), (yT_done, FC), (xT_done, 2), (ys_done, 2), (yp_done, 1)):
                pe.sem_inc(q, n)
            pe.wait_ge(xg_in[0], 32)
            turn_tokens(pe, 0, 0)
            with pe.Fori(0, E // 2) as i:
                for j in range(2):
                    e8 = lambda n: i * (2 * FC) + (j * FC + n)

                    def bank_free(c):
                        b = c - 3
                        if b < 0:
                            pe.wait_ge(yT_done, e8(FC + 1 + b))
                        elif b < FC:
                            pe.wait_ge(sg_done, e8(b + 1))
                        elif b < 2 * FC:
                            pe.wait_ge(gu_done, e8(b - FC + 1))
                        else:
                            pe.wait_ge(yT_done, e8(FC + b - 2 * FC + 1))

                    pe.wait_ge(xT_done, e8(FC + 2))
                    for m in range(3):
                        pe.wait_ge(w_in[m], i * 32 + 16 * (j + 1))
                        if m == 2:
                            pe.wait_ge(xg_in[1 - j], i * 32 + 32 * (j + 1))
                            turn_tokens(pe, 1 - j, e8(FC))
                            pe.wait_ge(gu_done, e8(FC))
                        for f in range(FC):
                            c = m * FC + f
                            bank_free(c)
                            src = gu if m == 2 else xT
                            for k in range(KD):
                                mm = nc.tensor.matmul(bk[c % 3][:, 0:SLOTS], w[m][:, k, f * P:(f + 1) * P], src[:, k, :],
                                                      start=k == 0, stop=k == KD - 1)
                            mm.then_inc(mm_sems[m], 1)
                            if m == 2 and f >= 2:
                                turn_results(pe, i, j, f - 2, e8)
                    for f in (FC - 2, FC - 1):
                        turn_results(pe, i, j, f, e8)

        @blk.scalar
        def _(act):
            with act.Fori(0, E // 2) as i:
                for j in range(2):
                    for f in range(FC):
                        act.wait_ge(g_mm, i * (2 * FC) + ((j + 1) * FC + f + 1))
                        nc.scalar.activation(sg[:, f, :], bk[f % 3][:, 0:SLOTS], ACT.Silu).then_inc(sg_done, 1)
                    for f in range(FC):
                        act.wait_ge(d_mm, i * (2 * FC) + ((j + 1) * FC + f + 1))
                        nc.scalar.activation(yT[:, f, :], bk[(2 * FC + f) % 3][:, 0:SLOTS], ACT.Copy).then_inc(yT_done, 1)

        def take_tokens(dve, base):
            for k in range(KD):
                dve.wait_ge(x_turned, base + (k + 1))
                for c, cols in ((0, slice(0, CAP_S)), (1, slice(CAP_S, SLOTS))):
                    co = keep.coef[:, l, 1, c]
                    ins = nc.vector.tensor_scalar(xT[:, k, cols], bx[k % 2][:, cols], co[:, 0, k:k + 1], co[:, 1, k:k + 1], ALU.mult, ALU.add)
                ins.then_inc(xT_done, 1)

        @blk.vector
        def _(dve):
            dve.wait_ge(row_in, 32)
            take_tokens(dve, 0)
            with dve.Fori(0, E // 2) as i:
                for j in range(2):
                    for f in range(FC):
                        dve.wait_ge(u_mm, i * (2 * FC) + ((j + 1) * FC + f + 1))
                        dve.wait_ge(sg_done, i * (2 * FC) + (j * FC + f + 1))
                        nc.vector.tensor_tensor(gu[:, f, :], sg[:, f, :], bk[(FC + f) % 3][:, 0:SLOTS], ALU.mult).then_inc(gu_done, 1)
                    take_tokens(dve, i * (2 * KD) + (j + 1) * KD)
                    dve.wait_ge(results_free, i * 2 + (j + 1))
                    for h in range(2):
                        half = slice(h * BANK, (h + 1) * BANK)
                        dve.wait_ge(y_turned, i * 4 + (2 * j + h + 1))
                        nc.vector.scalar_tensor_tensor(ys[j][:, half], by[h][:], keep.gate_s[:, bass.ds(i * 2 + j, 1)], rowg[:, 0, half],
                                                       ALU.mult, ALU.mult).then_inc(ys_done, 1)
                        dve.wait_ge(yp_turned, i * 4 + (2 * j + h + 1))
                        nc.vector.scalar_tensor_tensor(yp[j][:, half], byp[0:CAP_P, :], keep.gate_p[0:CAP_P, bass.ds(i * 2 + j, 1)],
                                                       rowg[0:CAP_P, 1, half], ALU.mult, ALU.mult).then_inc(yp_done, 1)


def final_norm(nc, io, keep):
    with Stage(nc, "final") as s:
        x = s.sb("x", [P, NT, D])
        gain = s.sb("gain", [P, D])
        norm = Norm(s, nc, keep, 0, 0, x, None)
        x_in = [s.sem(f"x_in{t}") for t in range(NT)]
        gain_in, y_done, y_out = s.sem("gain_in"), s.sem("y_done"), s.sem("y_out")
        blk = s.block()

        @blk.sync
        def _(sp):
            load_x(sp, io, x, x_in, {"x": io["x"][1]})
            sp.dma_start(gain[:], all_rows(io["norm_final"])).then_inc(gain_in, 16)
            for t in range(NT):
                sp.wait_ge(y_done, t + 1)
                dst = io["y_sample"][0, t * P:(t + 1) * P, :] if t < NTS else io["y_prompt"][0]
                sp.dma_start(dst, x[:, t, :]).then_inc(y_out, 16)
            sp.wait_ge(y_out, 16 * NT)

        @blk.scalar
        def _(act):
            norm.scalar(act, lambda eng, t: eng.wait_ge(x_in[t], 16))

        @blk.vector
        def _(dve):
            norm.vector_scale(dve)
            dve.wait_ge(gain_in, 16)
            for t in range(NT):
                dve.wait_ge(norm.scaled, t + 1)
                nc.vector.tensor_tensor(x[:, t, :], x[:, t, :], gain[:], ALU.mult).then_inc(y_done, 1)



HEADS = 8
LEVELS = 7


def delta_net(nc, io, keep):
    with Stage(nc, "gdn") as s:
        m = {}
        m["kv"] = s.sb("kv", [P, NT, 2, MIX])
        m["QT"] = s.sb("QT", [P, 4, T])
        m["KT"] = s.sb("KT", [P, 4, T])
        for n in ("beta", "g", "gc", "egc", "begc"):
            m[n] = s.sb(n, [P, NT, 2, HEADS])
        m["incl"] = s.sb("incl", [P, 2, P])
        m["joins"] = s.sb("joins", [P, LEVELS, 2, P])
        m["S"] = s.sb("S", [P, 4, 4, P])
        delta_prepare(nc, io, keep, m)
        m["o"] = s.sb("o", [P, NT, MIX])
        delta_chunks(nc, io, keep, m)
        delta_outputs(nc, io, keep, m)


def delta_prepare(nc, io, keep, m):
    kv, QT, KT, beta, g, gc, egc, begc, incl, S = (m[x] for x in ("kv", "QT", "KT", "beta", "g", "gc", "egc", "begc", "incl", "S"))
    with Stage(nc, "gdnp") as s:
        zc = s.sb("zc", [P, CC, T])
        q = s.sb("q", [P, NT, MIX])
        sq = s.sb("sq", [P, 2, MIX])
        ss = s.sb("ss", [P, NT, 2, HEADS])
        ab = s.sb("ab", [P, NT, 4, HEADS])
        a_log = s.sb("a_log", [P, 2, HEADS])
        dt_bias = s.sb("dt_bias", [P, 2, HEADS])
        x = s.sb("x", [P, NT, 2, HEADS])
        soft = s.sb("soft", [P, NT, 2, HEADS])
        eps = s.sb("eps", [P, 1])
        bq, bkk, bv = ([s.ps(f"{n}{i}", [P, BANK]) for i in range(2)] for n in ("bq", "bk", "bv"))
        bg = s.ps("bg", [P, 2, NT * HEADS])
        z_in, ab_in, small_in, s_in, s_zero = s.sem("z_in"), s.sem("ab_in"), s.sem("small_in"), s.sem("s_in"), s.sem("s_zero")
        silu_done, turned, q_taken, v_taken, squared, summed = (s.sem(n) for n in ("silu_done", "turned", "q_taken", "v_taken", "squared", "summed"))
        rooted, recip, scaled, back, back_taken = (s.sem(n) for n in ("rooted", "recip", "scaled", "back", "back_taken"))
        gate_act, gate_dve, g_mm, eps_set = s.sem("gate_act"), s.sem("gate_dve"), s.sem("g_mm"), s.sem("eps_set")
        blk = s.block()

        @blk.sync
        def _(sp):
            for c in range(CC):
                sp.dma_start(zc[:, c, :], io["conv"][1][c * P:(c + 1) * P, :]).then_inc(z_in, 16)
            sp.dma_start(ab[:].rearrange("p t a h -> p t (a h)"), io["tm"][1][:, MIX:MIX + 32].rearrange("(t p) a -> p t a", p=P)).then_inc(ab_in, 16)
            sp.dma_start(incl[:], io["incl"].rearrange("d p i -> p d i")).then_inc(small_in, 16)
            sp.dma_start(m["joins"][:], io["joins"].rearrange("s d p i -> p s d i")).then_inc(small_in, 16)
            sp.dma_start(a_log[:].rearrange("p d h -> p (d h)"), all_rows(io["gdn_a_log"][0].rearrange("d h -> (d h)"))).then_inc(small_in, 16)
            sp.dma_start(dt_bias[:].rearrange("p d h -> p (d h)"), all_rows(io["gdn_dt_bias"][0].rearrange("d h -> (d h)"))).then_inc(small_in, 16)
            sp.wait_ge(s_zero, 1)
            for d in range(2):
                for r in range(2):
                    sp.dma_start(S[64 * r:64 * r + 64, d, :, 64 * r:64 * r + 64],
                                 io["state_delta"][0, 0, d, r:8:2].rearrange("h k v -> k h v")).then_inc(s_in, 16)
            sp.wait_ge(s_in, 64)

        @blk.gpsimd
        def _(pool):
            nc.gpsimd.memset(S[:], 0.0).then_inc(s_zero, 1)
            nc.gpsimd.memset(eps[:], EPS).then_inc(eps_set, 1)

        @blk.tensor
        def _(pe):
            pe.wait_ge(silu_done, CC)
            for t in range(NT):
                if t >= 2:
                    pe.wait_ge(q_taken, 2 * (t - 1))
                    pe.wait_ge(v_taken, t - 1)
                for n, bank in enumerate((bq, bkk, bv)):
                    for j in range(4):
                        mm = nc.tensor.transpose(bank[t % 2][:, j * P:(j + 1) * P], zc[:, 4 * n + j, t * P:(t + 1) * P], keep.ident[:])
                mm.then_inc(turned, 1)
            pe.wait_ge(gate_dve, 4)
            for d in range(2):
                mm = nc.tensor.matmul(bg[:, d, :], incl[:, d, :], g[:, :, d, :], start=True, stop=True)
            mm.then_inc(g_mm, 1)
            for t in range(NT):
                if t >= 2:
                    pe.wait_ge(back_taken, 2 * (t - 1))
                elif t == 0:
                    pe.wait_ge(q_taken, 2 * NT)
                pe.wait_ge(scaled, 2 * (t + 1))
                for n, (bank, src) in enumerate(((bq, q[:, t, :]), (bkk, kv[:, t, 0, :]))):
                    for j in range(4):
                        mm = nc.tensor.transpose(bank[t % 2][:, j * P:(j + 1) * P], src[:, j * P:(j + 1) * P], keep.ident[:])
                mm.then_inc(back, 1)

        @blk.scalar
        def _(act):
            act.wait_ge(z_in, 16 * CC)
            for c in range(CC):
                nc.scalar.activation(zc[:, c, :], zc[:, c, :], ACT.Silu).then_inc(silu_done, 1)
            act.wait_ge(ab_in, 16)
            act.wait_ge(small_in, 64)
            nc.scalar.activation(beta[:], ab[:, :, 2:4, :], ACT.Sigmoid).then_inc(gate_act, 1)
            for t in range(NT):
                act.wait_ge(turned, t + 1)
                nc.scalar.activation(kv[:, t, 1, :], bv[t % 2][:], ACT.Copy).then_inc(v_taken, 1)
                act.wait_ge(q_taken, 2 * (t + 1))
                if t:
                    act.wait_ge(summed, t)
                nc.scalar.activation(sq[:, 0, :], q[:, t, :], ACT.Square)
                nc.scalar.activation(sq[:, 1, :], kv[:, t, 0, :], ACT.Square).then_inc(squared, 1)
            act.wait_ge(gate_dve, 1)
            nc.scalar.activation(soft[:], x[:], ACT.Abs).then_inc(gate_act, 1)
            act.wait_ge(gate_act, 2)
            nc.scalar.activation(soft[:], soft[:], ACT.Exp, scale=-1.0).then_inc(gate_act, 1)
            nc.scalar.activation(a_log[:], a_log[:], ACT.Exp).then_inc(gate_act, 1)
            act.wait_ge(gate_act, 4)
            act.wait_ge(gate_dve, 2)
            nc.scalar.activation(soft[:], soft[:], ACT.Ln).then_inc(gate_act, 1)
            act.wait_ge(gate_dve, 5)
            nc.scalar.activation(egc[:], gc[:], ACT.Exp).then_inc(gate_act, 1)
            act.wait_ge(summed, NT)
            act.wait_ge(eps_set, 1)
            nc.scalar.activation(ss[:], ss[:], ACT.Sqrt, bias=eps[:]).then_inc(rooted, 1)
            for t in range(NT):
                act.wait_ge(back, t + 1)
                at = slice(t * P, (t + 1) * P)
                nc.scalar.activation(QT[:, :, at], bq[t % 2][:].rearrange("p (j t) -> p j t", j=4), ACT.Copy).then_inc(back_taken, 1)
                nc.scalar.activation(KT[:, :, at], bkk[t % 2][:].rearrange("p (j t) -> p j t", j=4), ACT.Copy).then_inc(back_taken, 1)

        @blk.vector
        def _(dve):
            dve.wait_ge(ab_in, 16)
            dve.wait_ge(small_in, 64)
            rows = lambda a: a[:].unsqueeze(1).broadcast_to([P, NT, 2, HEADS])
            nc.vector.tensor_tensor(x[:], ab[:, :, 0:2, :], rows(dt_bias), ALU.add).then_inc(gate_dve, 1)
            for t in range(NT):
                dve.wait_ge(turned, t + 1)
                nc.vector.tensor_copy(q[:, t, :], bq[t % 2][:]).then_inc(q_taken, 1)
                nc.vector.tensor_copy(kv[:, t, 0, :], bkk[t % 2][:]).then_inc(q_taken, 1)
                dve.wait_ge(squared, t + 1)
                nc.vector.tensor_reduce(ss[:, t].rearrange("p a h -> p (a h)"), sq[:].rearrange("p a (h d) -> p (a h) d", d=HD), axis=AX.X, op=ALU.add).then_inc(summed, 1)
            dve.wait_ge(gate_act, 3)
            nc.vector.tensor_scalar(soft[:], soft[:], 1.0, None, ALU.add).then_inc(gate_dve, 1)
            dve.wait_ge(gate_act, 5)
            nc.vector.scalar_tensor_tensor(x[:].rearrange("p t d h -> p (t d h)"), x[:].rearrange("p t d h -> p (t d h)"), 0.0,
                                           soft[:].rearrange("p t d h -> p (t d h)"), ALU.max, ALU.add).then_inc(gate_dve, 1)
            dve.wait_ge(gate_dve, 3)
            nc.vector.scalar_tensor_tensor(g[:].rearrange("p t d h -> p t (d h)"), x[:].rearrange("p t d h -> p t (d h)"), -1.0,
                                           a_log[:].rearrange("p d h -> p (d h)").unsqueeze(1).broadcast_to([P, NT, 16]), ALU.mult, ALU.mult).then_inc(gate_dve, 1)
            dve.wait_ge(g_mm, 1)
            nc.vector.tensor_copy(gc[:].rearrange("p t d h -> p d t h"), bg[:].rearrange("p d (t h) -> p d t h", h=HEADS)).then_inc(gate_dve, 1)
            dve.wait_ge(gate_act, 6)
            nc.vector.tensor_tensor(begc[:], egc[:], beta[:], ALU.mult)
            dve.wait_ge(rooted, 1)
            nc.vector.reciprocal(ss[:], ss[:]).then_inc(recip, 1)
            dve.wait_ge(recip, 1)
            nc.vector.tensor_scalar(ss[:, :, 0, :], ss[:, :, 0, :], HD ** -0.5, None, ALU.mult).then_inc(recip, 1)
            dve.wait_ge(recip, 2)
            for t in range(NT):
                for a, y in ((0, q[:, t, :]), (1, kv[:, t, 0, :])):
                    y = y.rearrange("p (h d) -> p h d", d=HD)
                    nc.vector.tensor_tensor(y, y, ss[:, t, a, :].unsqueeze(2).broadcast_to([P, HEADS, HD]), ALU.mult).then_inc(scaled, 1)


def delta_chunks(nc, io, keep, m):
    kv, QT, KT, beta, g, gc, egc, begc, incl, joins, S, o = (
        m[x] for x in ("kv", "QT", "KT", "beta", "g", "gc", "egc", "begc", "incl", "joins", "S", "o"))
    items = [(NTS, 0, 2), (NTS, 1, 3)]
    for t in range(NTS):
        items += [(t, 0, 0), (NTS - 1 - t, 1, 1)]
    N_IT = len(items)
    NL = LEVELS - 1
    with Stage(nc, "gdnc") as s:
        HW = [P, HEADS, P]
        E_ = s.sb("E", HW)
        gam = s.sb("gam", HW)
        kg = s.sb("kg", HW)
        qg = s.sb("qg", HW)
        N = s.sb("N", HW)
        NTr = [s.sb(f"NT{i}", HW) for i in range(2)]
        AT = [s.sb(f"AT{i}", HW) for i in range(2)]
        part = [s.sb(f"part{i}", HW) for i in range(2)]
        Tm = [s.sb(f"T{i}", HW) for i in range(2)]
        TT = [s.sb(f"TT{i}", HW) for i in range(2)]
        W = s.sb("W", HW)
        gl = s.sb("gl", [P, 3, HEADS])
        dl = s.sb("dl", [P, 3, HEADS])
        egl = s.sb("egl", [P, 3, HEADS])
        egk = s.sb("egk", [P, 3, HEADS])
        vb = s.sb("vb", [P, MIX])
        kd = s.sb("kd", [P, MIX])
        r = s.sb("r", [P, MIX])
        vn = s.sb("vn", [P, MIX])
        mq = s.sb("mq", [P, MIX])
        ba = [s.ps(f"a{i}", [P, 4, P]) for i in range(2)]
        bb = [s.ps(f"b{i}", [P, 4, P]) for i in range(2)]
        bz = s.ps("z", HW)
        bx = s.ps("x", HW)
        z_mm, gbc_taken, gam_step, kk_taken, kq_taken, nt_taken = (s.sem(n) for n in ("z_mm", "gbc_taken", "gam_step", "kk_taken", "kq_taken", "nt_taken"))
        N_done, AT_done, T_set, T_step, TT_set, TT_step, part_done = (s.sem(n) for n in ("N_done", "AT_done", "T_set", "T_step", "TT_set", "TT_step", "part_done"))
        W_mm, W_taken, TU_mm, TU_done = s.sem("W_mm"), s.sem("W_taken"), s.sem("TU_mm"), s.sem("TU_done")
        x_mm, r_step, r_done, vn_done, o_step, o_done, S_step, S_done = (s.sem(n) for n in ("x_mm", "r_step", "r_done", "vn_done", "o_step", "o_done", "S_step", "S_done"))
        vb_done, kd_done, last_done, small_done = s.sem("vb_done"), s.sem("kd_done"), s.sem("last_done"), s.sem("small_done")
        st_out = s.sem("st_out")
        blk = s.block()

        def lvl(n, li, hg):
            return (n * NL + li) * 2 + hg + 1

        def z_decay(pe, n):
            t, d, _ = items[n]
            if n:
                pe.wait_ge(nt_taken, n)
            for h in range(HEADS):
                mm = nc.tensor.matmul(bz[:, h, :], g[:, t, d, h:h + 1].broadcast_to([P, P]), incl[:, d, :], start=True, stop=True)
            mm.then_inc(z_mm, 1)

        def z_keys(pe, n, src, taken):
            t = items[n][0]
            pe.wait_ge(taken, n + 1)
            at = slice(t * P, (t + 1) * P)
            for h in range(HEADS):
                rows = slice(64 * (h % 2), 64 * (h % 2) + 64)
                mm = nc.tensor.matmul(bz[:, 4 * (h % 2) + h // 2, :], KT[rows, h // 2, at], src[rows, h // 2, at], start=True, stop=True)
            mm.then_inc(z_mm, 1)

        def z_turn(pe, n):
            pe.wait_ge(kq_taken, n + 1)
            pe.wait_ge(N_done, n + 1)
            for h in range(HEADS):
                mm = nc.tensor.transpose(bz[:, h, :], N[:, h, :], keep.ident[:])
            mm.then_inc(z_mm, 1)

        def prep(pe, n, li):
            if n < N_IT:
                if li == 0:
                    z_decay(pe, n)
                elif li == 1:
                    z_keys(pe, n, KT, gbc_taken)
                elif li == 2:
                    z_keys(pe, n, QT, kk_taken)
                elif li == 4:
                    z_turn(pe, n)

        def scan(pe, n, li):
            if n < 0 or li > 3:
                return
            t, d, st = items[n]
            at = slice(t * P, (t + 1) * P)
            xf = bx[:].rearrange("p h i -> p (h i)")
            if li == 0:
                if n:
                    pe.wait_ge(S_done, n)
                for a, src in enumerate((KT, QT)):
                    for j in range(4):
                        mm = nc.tensor.matmul(xf[:, a * MIX + j * P:a * MIX + (j + 1) * P], src[:, j, at], S[:, st, j, :], start=True, stop=True)
            elif li == 1:
                pe.wait_ge(r_done, n + 1)
                pe.wait_ge(TU_done, lvl(n, NL - 1, 1))
                for h in range(HEADS):
                    mm = nc.tensor.matmul(bx[:, h, :], TT[n % 2][:, h, :], r[:, (h // 2) * P:(h // 2 + 1) * P], start=True, stop=True)
            elif li == 2:
                pe.wait_ge(vn_done, n + 1)
                pe.wait_ge(AT_done, n + 1)
                for h in range(HEADS):
                    mm = nc.tensor.matmul(bx[:, h, :], AT[n % 2][:, h, :], vn[:, (h // 2) * P:(h // 2 + 1) * P], start=True, stop=True)
            else:
                pe.wait_ge(o_done, n + 1)
                pe.wait_ge(kd_done, n + 1)
                for j in range(4):
                    mm = nc.tensor.matmul(xf[:, j * P:(j + 1) * P], kd[:, j * P:(j + 1) * P], vn[:, j * P:(j + 1) * P], start=True, stop=True)
            mm.then_inc(x_mm, 1)

        @blk.tensor
        def _(pe):
            for n in range(-1, N_IT + 1):
                live = 0 <= n < N_IT
                b = n % 2
                for li in range(NL):
                    if live:
                        pe.wait_ge(part_done, n * NL + li + 1)
                        if li == 0:
                            pe.wait_ge(T_set, n + 1)
                        for hg in range(2):
                            if n or li:
                                pe.wait_ge(TU_done, lvl(n, li - 1, hg))
                            for h in range(4):
                                mm = nc.tensor.matmul(ba[hg][:, h, :], part[li % 2][:, 4 * hg + h, :], Tm[b][:, 4 * hg + h, :], start=True, stop=True)
                            mm.then_inc(W_mm, 1)
                    prep(pe, n + 1, li)
                    if live:
                        if li == 0:
                            pe.wait_ge(TT_set, n + 1)
                        for hg in range(2):
                            pe.wait_ge(W_taken, lvl(n, li, hg))
                            if li < NL - 1:
                                for h in range(4):
                                    nc.tensor.matmul(bb[hg][:, h, :], TT[b][:, 4 * hg + h, :], W[:, 4 * hg + h, :], start=True, stop=True)
                            for h in range(4):
                                mm = nc.tensor.matmul(ba[hg][:, h, :], W[:, 4 * hg + h, :], TT[b][:, 4 * hg + h, :], start=True, stop=True)
                            mm.then_inc(TU_mm, 1)
                    scan(pe, n - 1, li)

        @blk.scalar
        def _(act):
            for n in range(-1, N_IT + 1):
                live = 0 <= n < N_IT
                p = n + 1
                for li in range(NL):
                    if live:
                        for hg in range(2):
                            act.wait_ge(W_mm, lvl(n, li, hg))
                            if n or li:
                                act.wait_ge(TU_mm, lvl(n, li - 1, hg))
                            nc.scalar.activation(W[:, 4 * hg:4 * hg + 4, :], ba[hg][:], ACT.Copy).then_inc(W_taken, 1)
                    if p < N_IT and li == 0:
                        act.wait_ge(gbc_taken, p + 1)
                        nc.scalar.activation(E_[:], E_[:], ACT.Abs).then_inc(gam_step, 1)
                        act.wait_ge(gam_step, 2 * p + 1)
                        if p:
                            act.wait_ge(kq_taken, p)
                        nc.scalar.activation(gam[:], E_[:], ACT.Exp, scale=-1.0).then_inc(gam_step, 1)
                        act.wait_ge(last_done, p + 1)
                        nc.scalar.activation(egl[:, p % 3, :], gl[:, p % 3, :], ACT.Exp)
                        nc.scalar.activation(egk[:, p % 3, :], dl[:, p % 3, :], ACT.Exp).then_inc(small_done, 1)
                    if p < N_IT and li == 4:
                        act.wait_ge(z_mm, 4 * p + 4)
                        if p >= 2:
                            act.wait_ge(part_done, (p - 1) * NL)
                            act.wait_ge(TT_set, p - 1)
                        nc.scalar.activation(NTr[p % 2][:], bz[:], ACT.Copy).then_inc(nt_taken, 1)

        def by_half(a):
            return a[:].rearrange("p (j r) i -> p r j i", r=2)

        def prep_dve(dve, p, li):
            t, d, _ = items[p]
            halves = bz[:].rearrange("p (r j) i -> p r j i", r=2)
            if li == 0:
                dve.wait_ge(z_mm, 4 * p + 1)
                if p:
                    dve.wait_ge(gam_step, 2 * p)
                nc.vector.tensor_tensor(E_[:], bz[:], gc[:, t, d, :].unsqueeze(2).broadcast_to(HW), ALU.subtract)
                last = P - 1 if d == 0 else 0
                nc.vector.tensor_copy(gl[:, p % 3, :], bz[:, :, last]).then_inc(gbc_taken, 1)
                dve.wait_ge(gbc_taken, p + 1)
                nc.vector.tensor_tensor(dl[:, p % 3, :], gl[:, p % 3, :], gc[:, t, d, :], ALU.subtract).then_inc(last_done, 1)
            elif li == 1:
                dve.wait_ge(z_mm, 4 * p + 2)
                dve.wait_ge(gam_step, 2 * p + 2)
                if p:
                    dve.wait_ge(N_done, p)
                nc.vector.tensor_tensor(by_half(kg), halves, by_half(gam), ALU.mult).then_inc(kk_taken, 1)
            elif li == 2:
                dve.wait_ge(z_mm, 4 * p + 3)
                if p:
                    dve.wait_ge(AT_done, p)
                nc.vector.tensor_tensor(by_half(qg), halves, by_half(gam), ALU.mult).then_inc(kq_taken, 1)
            elif li == 4:
                dve.wait_ge(N_done, p + 1)
                nc.vector.tensor_tensor(Tm[p % 2][:], N[:], joins[:, 0, 1 - d, :].unsqueeze(1).broadcast_to(HW), ALU.mult).then_inc(T_step, 1)
                dve.wait_ge(T_step, p + 1)
                nc.vector.tensor_tensor(Tm[p % 2][:], keep.ident[:].unsqueeze(1).broadcast_to(HW), Tm[p % 2][:], ALU.subtract).then_inc(T_set, 1)

        def scan_dve(dve, q, li):
            t, d, st = items[q]
            heads = lambda a: a.rearrange("p (h e) -> p h e", e=HD)
            spread = lambda a: a.unsqueeze(2).broadcast_to([P, HEADS, HD])
            xf = bx[:].rearrange("p h i -> p (h i)")
            if li == 0:
                dve.wait_ge(x_mm, 4 * q + 1)
                nc.vector.tensor_tensor(heads(r[:]), heads(xf[:, 0:MIX]), spread(begc[:, t, d, :]), ALU.mult).then_inc(r_step, 1)
                nc.vector.tensor_tensor(heads(mq[:]), heads(xf[:, MIX:2 * MIX]), spread(egc[:, t, d, :]), ALU.mult)
                dve.wait_ge(r_step, q + 1)
                dve.wait_ge(vb_done, q + 1)
                nc.vector.tensor_tensor(r[:], vb[:], r[:], ALU.subtract).then_inc(r_done, 1)
            elif li == 1:
                dve.wait_ge(x_mm, 4 * q + 2)
                for half in range(2):
                    cols = slice(64 * half, 64 * half + 64)
                    ins = nc.vector.tensor_copy(heads(vn[:])[:, half:8:2, :], bx[:, half:8:2, cols])
                ins.then_inc(vn_done, 1)
            elif li == 2:
                dve.wait_ge(x_mm, 4 * q + 3)
                for half in range(2):
                    cols = slice(64 * half, 64 * half + 64)
                    dst = heads(mq[:])[:, half:8:2, :]
                    ins = nc.vector.tensor_tensor(dst, dst, bx[:, half:8:2, cols], ALU.add)
                ins.then_inc(o_step, 1)
                dve.wait_ge(o_step, q + 1)
                first = t not in [x[0] for x in items[:q]]
                if first:
                    nc.vector.tensor_copy(o[:, t, :], mq[:]).then_inc(o_done, 1)
                else:
                    nc.vector.tensor_tensor(o[:, t, :], o[:, t, :], mq[:], ALU.add).then_inc(o_done, 1)
            elif li == 3:
                for half in range(2):
                    rows = slice(64 * half, 64 * half + 64)
                    ins = nc.vector.tensor_tensor(S[rows, st, :, rows], S[rows, st, :, rows],
                                                  egl[rows, q % 3, half:8:2].unsqueeze(2).broadcast_to([64, 4, HD]), ALU.mult)
                ins.then_inc(S_step, 1)
                dve.wait_ge(S_step, q + 1)
                dve.wait_ge(x_mm, 4 * q + 4)
                for half in range(2):
                    rows = slice(64 * half, 64 * half + 64)
                    ins = nc.vector.tensor_tensor(S[rows, st, :, rows], S[rows, st, :, rows],
                                                  bx[:].rearrange("p h i -> p (h i)")[rows, 0:MIX].rearrange("p (j c) -> p j c", c=P)[:, :, rows], ALU.add)
                ins.then_inc(S_done, 1)

        @blk.vector
        def _(dve):
            for n in range(-1, N_IT + 1):
                live = 0 <= n < N_IT
                p, q = n + 1, n - 1
                for li in range(NL):
                    if p < N_IT:
                        prep_dve(dve, p, li)
                    if live:
                        b = n % 2
                        for hg in range(2):
                            dve.wait_ge(TU_mm, lvl(n, li, hg))
                            hs = slice(4 * hg, 4 * hg + 4)
                            if li < NL - 1:
                                nc.vector.tensor_tensor(Tm[b][:, hs, :], Tm[b][:, hs, :], bb[hg][:], ALU.subtract)
                            nc.vector.tensor_tensor(TT[b][:, hs, :], TT[b][:, hs, :], ba[hg][:], ALU.subtract).then_inc(TU_done, 1)
                    if q >= 0:
                        scan_dve(dve, q, li)

        @blk.gpsimd
        def _(pool):
            for n in range(-1, N_IT + 1):
                live = 0 <= n < N_IT
                p = n + 1

                def join(li):
                    if not live:
                        return
                    k = n * NL + li
                    if li == 0:
                        pool.wait_ge(nt_taken, n + 1)
                    if k >= 2:
                        pool.wait_ge(W_mm, 2 * (k - 1))
                    mask = joins[:, li + 1, items[n][1], :].unsqueeze(1).broadcast_to(HW)
                    nc.gpsimd.tensor_tensor(part[li % 2][:], NTr[n % 2][:], mask, ALU.mult).then_inc(part_done, 1)

                join(0)
                join(1)
                if p < N_IT:
                    t, d, _ = items[p]
                    pool.wait_ge(kk_taken, p + 1)
                    if p:
                        pool.wait_ge(T_set, p)
                        pool.wait_ge(z_mm, 4 * p)
                    nc.gpsimd.tensor_tensor(N[:], kg[:], beta[:, t, d, :].unsqueeze(2).broadcast_to(HW), ALU.mult).then_inc(N_done, 1)
                join(2)
                join(3)
                if p < N_IT:
                    pool.wait_ge(kq_taken, p + 1)
                    if p >= 2:
                        pool.wait_ge(x_mm, 4 * (p - 2) + 3)
                    nc.gpsimd.tensor_tensor(AT[p % 2][:], qg[:], incl[:, d, :].unsqueeze(1).broadcast_to(HW), ALU.mult).then_inc(AT_done, 1)
                if live:
                    t, d, _ = items[n]
                    if n:
                        pool.wait_ge(r_done, n)
                    heads = lambda a: a.rearrange("p (h e) -> p h e", e=HD)
                    spread = lambda a: a.unsqueeze(2).broadcast_to([P, HEADS, HD])
                    nc.gpsimd.tensor_tensor(heads(vb[:]), heads(kv[:, t, 1, :]), spread(beta[:, t, d, :]), ALU.mult).then_inc(vb_done, 1)
                join(4)
                if live:
                    if n:
                        pool.wait_ge(x_mm, 4 * n)
                    pool.wait_ge(small_done, n + 1)
                    nc.gpsimd.tensor_tensor(heads(kd[:]), heads(kv[:, t, 0, :]), spread(egk[:, n % 3, :]), ALU.mult).then_inc(kd_done, 1)
                join(5)
                if p < N_IT:
                    d = items[p][1]
                    pool.wait_ge(nt_taken, p + 1)
                    if p >= 2:
                        pool.wait_ge(x_mm, 4 * (p - 2) + 2)
                    nc.gpsimd.tensor_tensor(TT[p % 2][:], NTr[p % 2][:], joins[:, 0, d, :].unsqueeze(1).broadcast_to(HW), ALU.mult).then_inc(TT_step, 1)
                    pool.wait_ge(TT_step, p + 1)
                    nc.gpsimd.tensor_tensor(TT[p % 2][:], keep.ident[:].unsqueeze(1).broadcast_to(HW), TT[p % 2][:], ALU.subtract).then_inc(TT_set, 1)

        @blk.sync
        def _(sp):
            sp.wait_ge(S_done, 2)
            for d in range(2):
                for h in range(2):
                    sp.dma_start(io["new_state"][0, 0, d, h:8:2].rearrange("h k v -> k h v"),
                                 S[64 * h:64 * h + 64, 2 + d, :, 64 * h:64 * h + 64]).then_inc(st_out, 16)
            sp.wait_ge(st_out, 64)


def delta_outputs(nc, io, keep, m):
    o = m["o"]
    with Stage(nc, "gdno") as s:
        zg = s.sb("zg", [P, NT, MIX])
        sq = s.sb("sq", [P, 2, MIX])
        ss = s.sb("ss", [P, NT, HEADS])
        w = s.sb("w", [P, HD])
        eps = s.sb("eps", [P, 1])
        oT = s.sb("oT", [P, 2, 4, P])
        bt = [s.ps(f"t{i}", [P, BANK]) for i in range(2)]
        zg_in, w_in, silu_done, squared, summed, eps_set, rooted, recip, step, o_done, turned, taken = (
            s.sem(n) for n in ("zg_in", "w_in", "silu_done", "squared", "summed", "eps_set", "rooted", "recip", "step", "o_done", "turned", "taken"))
        out = [s.sem(f"out{i}") for i in range(2)]
        blk = s.block()

        @blk.sync
        def _(sp):
            sp.dma_start(zg[:], io["tm"][1][:, 0:MIX].rearrange("(t p) c -> p t c", p=P)).then_inc(zg_in, 16)
            sp.dma_start(w[:], all_rows(io["gdn_norm"][0])).then_inc(w_in, 16)
            for t in range(NT):
                sp.wait_ge(taken, t + 1)
                sp.dma_start(io["mixT"][1][0:MIX, t * P:(t + 1) * P].rearrange("(j p) t -> p j t", p=P), oT[:, t % 2]).then_inc(out[t % 2], 16)
            for i in range(2):
                sp.wait_ge(out[i], 16 * len(range(i, NT, 2)))

        @blk.scalar
        def _(act):
            for t in range(NT):
                if t >= 2:
                    act.wait_ge(summed, t - 1)
                nc.scalar.activation(sq[:, t % 2, :], o[:, t, :], ACT.Square).then_inc(squared, 1)
            act.wait_ge(summed, NT)
            act.wait_ge(eps_set, 1)
            nc.scalar.activation(ss[:], ss[:], ACT.Sqrt, bias=eps[:], scale=1.0 / HD).then_inc(rooted, 1)
            act.wait_ge(zg_in, 16)
            for t in range(NT):
                nc.scalar.activation(zg[:, t, :], zg[:, t, :], ACT.Silu).then_inc(silu_done, 1)
            for t in range(NT):
                act.wait_ge(turned, t + 1)
                if t >= 2:
                    act.wait_ge(out[t % 2], 16 * (t // 2))
                nc.scalar.activation(oT[:, t % 2], bt[t % 2][:].rearrange("p (j t) -> p j t", j=4), ACT.Copy).then_inc(taken, 1)

        @blk.vector
        def _(dve):
            nc.vector.memset(eps[:], EPS).then_inc(eps_set, 1)
            for t in range(NT):
                dve.wait_ge(squared, t + 1)
                nc.vector.tensor_reduce(ss[:, t, :], sq[:, t % 2, :].rearrange("p (h d) -> p h d", d=HD), axis=AX.X, op=ALU.add).then_inc(summed, 1)
            dve.wait_ge(rooted, 1)
            nc.vector.reciprocal(ss[:], ss[:]).then_inc(recip, 1)
            dve.wait_ge(recip, 1)
            dve.wait_ge(w_in, 16)
            link = Link(dve, step)
            for t in range(NT):
                y = o[:, t, :].rearrange("p (h d) -> p h d", d=HD)
                z = zg[:, t, :].rearrange("p (h d) -> p h d", d=HD)
                dve.wait_ge(silu_done, t + 1)
                nc.vector.tensor_tensor(z, z, w[:].unsqueeze(1).broadcast_to([P, HEADS, HD]), ALU.mult)
                link(nc.vector.tensor_tensor(y, y, ss[:, t, :].unsqueeze(2).broadcast_to([P, HEADS, HD]), ALU.mult))
                nc.vector.tensor_tensor(y, y, z, ALU.mult).then_inc(o_done, 1)

        @blk.tensor
        def _(pe):
            for t in range(NT):
                pe.wait_ge(o_done, t + 1)
                if t >= 2:
                    pe.wait_ge(taken, t - 1)
                for j in range(4):
                    mm = nc.tensor.transpose(bt[t % 2][:, j * P:(j + 1) * P], o[:, t, j * P:(j + 1) * P], keep.ident[:])
                mm.then_inc(turned, 1)



class Keep:

    def __init__(self, s):
        self.ident = s.sb("ident", [P, P])
        self.coef = s.sb("coef", [P, 2, 2, 2, 2, KD])
        self.tap_scale = s.sb("tap_scale", [P, 2, 2 * MIX // P])

        self.slot_s = s.sb("slot_s", [P, E + 1], U32)
        self.slot_p = s.sb("slot_p", [P, E + 1], U32)
        self.gate_s = s.sb("gate_s", [P, E])
        self.gate_p = s.sb("gate_p", [P, E])


SCRATCH = {
    "mrow": (2, 2, 6 * D),
    "tm0": (T, EVEN_TM), "tm1": (T, ODD_TM),
    "conv0": (CONV, T), "conv1": (CONV, T),
    "mixT0": (D, T), "mixT1": (D, T),
    "x0": (T, D), "x1": (T, D),
    "xn": (T, D), "rpbpad": (120, GRID_W, P), "spec": (NT, P, 2, 2, MIX),
}
INPUTS = ["x_prompt", "x_sample", "cache_attn_k", "cache_attn_v", "state_delta", "cache_na_k", "cache_na_v", "c", "c_ctx",
          "w_ada", "b_ada", "norm_mix", "norm_ffn", "norm_final", "even_w_in", "even_w_out", "attn_sink", "hy_conv_w",
          "hy_conv_b", "hy_w1", "hy_b1", "hy_w2", "hy_b2", "hy_w3", "hy_freq", "hy_skip", "odd_w_in", "odd_w_out",
          "gdn_conv_w", "gdn_a_log", "gdn_dt_bias", "gdn_norm", "na_rpb", "moe_router", "moe_w_gate", "moe_w_up",
          "moe_w_down", "ident", "band", "cos", "sin", "colmask", "feats", "win", "win_b", "filt_dft", "filt_dft_p",
          "sig_dft", "sig_dft_p", "sig_idft", "sig_idft_p", "incl", "joins"]
OUTPUTS = {
    "y_prompt": (1, TP, D), "y_sample": (1, TS, D), "new_attn_k": (1, 1, TP, 2, HD), "new_attn_v": (1, 1, TP, 2, HD),
    "new_state": (1, 1, 2, 8, HD, HD), "new_na_k": (1, 1, TP, 8, HD), "new_na_v": (1, 1, TP, 8, HD),
}


def constants():
    f = np.float32
    i, j = np.arange(P)[:, None], np.arange(P)[None, :]
    none, before, after = np.zeros((P, P), f), np.where(j >= i, f(0), f(NEG)), np.where(j <= i, f(0), f(NEG))
    band = np.concatenate([none, before, none, after, none, none, after], axis=1).astype(f)
    t = np.arange(TS)
    inv = (10000.0 ** (-np.arange(HD // 4, dtype=f) / (HD // 4))).astype(f)
    angle = np.concatenate([(t // GRID_W).astype(f)[:, None] * inv, (t % GRID_W).astype(f)[:, None] * inv], axis=-1)
    by_tile = lambda a: np.ascontiguousarray(a.reshape(NTS, P, 32).transpose(1, 0, 2)).astype(f)
    c = np.arange(P)[:, None] % GRID_W
    lo = np.clip(c - 8, 0, GRID_W - 16)
    kc = np.arange(GRID_W)[None, :]
    colmask = np.where((kc >= lo) & (kc < lo + 16), f(0), f(NEG)).astype(f)
    out = {}
    feats, wins, last = [], [], []
    for L in (TS, TP):
        n = np.arange(L)
        order = np.concatenate([n[0::2], n[1::2]]) if L == TS else n
        tt = np.linspace(0.0, 1.0, L, dtype=f)[:, None]
        bands = np.linspace(1e-4, 15, 16, dtype=f)[None, :]
        omega = (2.0 * math.pi * n.astype(f)[:, None] / L).astype(f)
        ph = (bands * omega).astype(f).astype(np.float64)
        feats.append(np.concatenate([tt, np.cos(ph), -np.sin(ph)], axis=1)[order].T)
        lo, hi = math.log(1e-2) / 1.5, math.log(1e-2) / 0.3
        deltas = np.abs(np.linspace(lo, hi, MIX, dtype=f))
        w = (np.exp((-tt * deltas).astype(np.float64)) + 0.05)[order]
        wins.append(w)
        head = w[0:P].copy()
        head[0] = 0.0
        last.append(head)
        freq = np.pi * (2 * np.arange(L) + 1) / (2 * L)
        if L == TS:
            a = np.outer(order, freq[0:L // 2])
            freq = np.concatenate([freq[0:L // 2], np.pi - freq[0:L // 2]])
            names = ("filt_dft", "sig_dft", "sig_idft")
        else:
            a = np.outer(order, freq)
            names = ("filt_dft_p", "sig_dft_p", "sig_idft_p")
        b = np.outer(np.arange(L // 2) + 0.5, freq)
        out[names[0]] = np.stack([np.cos(a), np.sin(a)]).astype(f)
        out[names[1]] = np.stack([np.cos(b), np.sin(b)]).astype(f)
        out[names[2]] = np.stack([np.cos(b).T / L, np.sin(b).T / L]).astype(f)
    out["feats"] = np.concatenate(feats, axis=1).astype(f)
    out["win"] = np.concatenate(wins).astype(f)
    out["win_b"] = np.stack(last).astype(f)
    out["incl"] = np.stack([j >= i, j <= i]).astype(f)
    joins = []
    for lv in range(LEVELS):
        b = 2 << lv
        later = (i // b == j // b) & (i % b < b // 2) & (j % b >= b // 2)
        joins.append(np.stack([later, later.T]))
    out["joins"] = np.stack(joins).astype(f)
    return out | {"ident": np.eye(P, dtype=f), "band": band, "cos": by_tile(np.cos(angle)), "sin": by_tile(np.sin(angle)),
            "colmask": colmask}


def wire(io, scratch, outs):
    io["mrow"] = scratch["mrow"]
    io["x_of"] = [{"xs": io["x_sample"][0], "xp": io["x_prompt"][0]}, {"x": scratch["x0"]}]
    for n in ("tm", "conv", "mixT", "x"):
        io[n] = [scratch[n + "0"], scratch[n + "1"]]
    io["rpbpad"], io["spec"] = scratch["rpbpad"], scratch["spec"]
    io["xn"] = scratch["xn"]
    io.update(outs)


def program(nc, io):
    with Stage(nc, "keep") as s:
        keep = Keep(s)
        modulation(nc, io, keep)
        project(nc, io, keep, 0)
        attention(nc, io, keep, 0)
        hyena_filters(nc, io, keep)
        hyena_signals(nc, io, keep)
        mix_out(nc, io, keep, 0)
        experts(nc, io, keep, 0)
        project(nc, io, keep, 1)
        attention(nc, io, keep, 1)
        delta_net(nc, io, keep)
        mix_out(nc, io, keep, 1)
        experts(nc, io, keep, 1)
        final_norm(nc, io, keep)


def kernel(**inputs):
    import concourse.bacc as bacc
    from concourse.bass_utils import run_bass_kernel_spmd

    nc = bacc.Bacc("TRN2", target_bir_lowering=False, num_devices=1)
    shapes = constants()
    arrays, io, scratch, outs = {}, {}, {}, {}
    for name in INPUTS:
        a = np.ascontiguousarray(shapes[name] if name in shapes else inputs[name])
        arrays[name] = a
        io[name] = nc.dram_tensor(name, a.shape, F32, kind="ExternalInput").ap()
    for name, shape in SCRATCH.items():
        scratch[name] = nc.dram_tensor("scratch_" + name, shape, F32, kind="Internal").ap()
    for name, shape in OUTPUTS.items():
        outs[name] = nc.dram_tensor(name, shape, F32, kind="ExternalOutput").ap()
    wire(io, scratch, outs)
    program(nc, io)
    r = run_bass_kernel_spmd(nc, [arrays], core_ids=[0])
    return tuple(r.results[0][name] for name in OUTPUTS)
```

```python
import math
from contextlib import ExitStack

import numpy as np
import concourse.bass as bass
from concourse import mybir

F32 = mybir.dt.float32
U32 = mybir.dt.uint32
F32R = mybir.dt.float32r
ALU = mybir.AluOpType
ACT = mybir.ActivationFunctionType
AX = mybir.AxisListType

P = 128
D = 1024
KD = D // P
TS = 1024
TP = 128
T = TS + TP
NT = T // P
NTS = TS // P
HD = 64
BANK = 512
EPS = 1e-6
NEG = -1e30
GRID_W = 64
MIX = 512
CONV = 3 * MIX
CC = CONV // P
ZW = T + 3
EVEN_TM = 768
ODD_TM = 2080
E = 16
CAP_S = 2 * TS // E
CAP_P = 2 * TP // E
SLOTS = CAP_S + CAP_P


class Link:

    def __init__(self, eng, sem, base=0):
        self.eng, self.sem, self.base, self.n = eng, sem, base, 0

    def __call__(self, ins):
        ins.then_inc(self.sem, 1)
        self.n += 1
        self.eng.wait_ge(self.sem, self.base + self.n)


class Stage:

    def __init__(self, nc, name):
        self.nc, self.name, self.ctx, self.sems, self.blk = nc, name, ExitStack(), [], None

    def __enter__(self):
        self.ctx.__enter__()
        return self

    def __exit__(self, *a):
        if self.blk is not None:
            self.blk.__exit__(*a)
            nums = sorted(q.num for q in self.sems)
            while nums:
                n = 1
                while n < len(nums) and nums[n] == nums[0] + n:
                    n += 1
                self.nc.gpsimd.sem_clear(range(nums[0], nums[0] + n))
                nums = nums[n:]
            self.nc.all_engine_barrier()
        return self.ctx.__exit__(*a)

    def sb(self, name, shape, dt=F32):
        return self.ctx.enter_context(self.nc.sbuf_tensor(f"{self.name}_{name}", shape, dt))

    def ps(self, name, shape, dt=F32):
        return self.ctx.enter_context(self.nc.psum_tensor(f"{self.name}_{name}", shape, dt))

    def sem(self, name):
        self.sems.append(self.ctx.enter_context(self.nc.semaphore(f"{self.name}_{name}")))
        return self.sems[-1]

    def pool_dma_sem(self, name):
        return self.nc.alloc_semaphore(f"{self.name}_{name}")

    def block(self):
        self.blk = self.nc.Block()
        return self.blk.__enter__()


def token_groups():
    return [(0, BANK, 0), (BANK, BANK, 0), (TS, TP, 1)]



def all_rows(ap, rows=P):
    return bass.AP(ap.tensor, ap.offset, [[0, rows]] + list(ap.ap))


def modulation(nc, io, keep):
    PAN = 6 * D // BANK
    TILES = 4
    RING = 2 * TILES
    with Stage(nc, "ada") as s:
        cond = s.sb("cond", [P, 2, KD])
        sil = keep.silu
        rows = s.sb("rows", [2, 6 * D])
        ring = [s.sb(f"w{i}", [P, KD, BANK]) for i in range(RING)]
        flat = s.sb("flat", [96, P])
        gains = s.sb("gains", [4 * KD, P])
        gain_cols = keep.gain_cols
        ps = [s.ps(f"p{i}", [P, BANK]) for i in range(TILES)]
        pt = [s.ps(f"pt{i}", [P, BANK]) for i in range(2)]
        w_in = [s.sem(f"w_in{i}") for i in range(RING)]
        cond_in = s.sem("cond_in")
        small_in, ident_in, silu_done = s.sem("small_in"), s.sem("ident_in"), s.sem("silu_done")
        row_done, rows_out, flat_in = s.sem("row_done"), s.sem("rows_out"), s.sem("flat_in")
        mm_done, turned, gain_done = s.sem("mm_done"), s.sem("turned"), s.sem("gain_done")
        blk = s.block()

        @blk.sync
        def _(sp):
            for n in range(PAN):
                if n >= RING and n % TILES == 0:
                    sp.wait_ge(mm_done, n - RING + TILES)
                sp.dma_start(ring[n % RING][:], io["w_ada"][0].rearrange("(k p) n -> p k n", p=P)[:, :, n * BANK:(n + 1) * BANK]).then_inc(w_in[n % RING], 16)

        @blk.scalar
        def _(act):
            act.dma_start(cond[:, 0, :], io["c"][0].rearrange("(k p) -> p k", p=P), allow_slow_non_contiguous=True).then_inc(cond_in, 16)
            act.dma_start(cond[:, 1, :], io["c_ctx"].rearrange("(k p) -> p k", p=P), allow_slow_non_contiguous=True).then_inc(cond_in, 16)
            act.wait_ge(cond_in, 32)
            nc.scalar.activation(sil[:].rearrange("p k c -> p c k"), cond[:], ACT.Silu).then_inc(silu_done, 1)
            for c in range(2):
                act.dma_start(rows[c:c + 1, :], io["b_ada"][0:1, :]).then_inc(small_in, 16)
            for n, g in enumerate(("norm_mix", "norm_ffn")):
                for l in range(2):
                    act.dma_start(gains[(2 * l + n) * KD:(2 * l + n + 1) * KD, :],
                                  io[g][l].rearrange("(k p) -> k p", p=P)).then_inc(small_in, 16)
            act.dma_start(keep.ident[:], io["ident"]).then_inc(ident_in, 16)
            act.wait_ge(row_done, TILES + PAN)
            act.dma_start(io["mrow"][0], rows[:]).then_inc(rows_out, 16)
            act.wait_ge(rows_out, 16)
            act.dma_start(flat[:], io["mrow"][0].rearrange("c (j p) -> (c j) p", p=P)).then_inc(flat_in, 16)

        @blk.tensor
        def _(pe):
            pe.sem_inc(row_done, TILES)
            pe.wait_ge(silu_done, 1)
            for g in range(PAN // TILES):
                slots = [(g * TILES + q) % RING for q in range(TILES)]
                for r in slots:
                    pe.wait_ge(w_in[r], 16 * (g * TILES // RING + 1))
                pe.wait_ge(row_done, (g + 1) * TILES)
                side_by_side(nc, keep.silu, [ring[r] for r in slots], [ps[q][32 * q:32 * q + 2, :] for q in range(TILES)], mm_done)
            pe.wait_ge(ident_in, 16)
            pe.wait_ge(small_in, 16 * 6)
            nc.tensor.transpose(pt[1][:, 0:32], gains[:], keep.ident[0:32, 0:32]).then_inc(turned, 1)
            pe.wait_ge(flat_in, 16)
            nc.tensor.transpose(pt[0][:, 0:96], flat[:], keep.ident[0:96, 0:96]).then_inc(turned, 1)

        @blk.vector
        def _(dve):
            dve.wait_ge(small_in, 16 * 6)
            for n in range(PAN):
                q = n % TILES
                if q == 0:
                    dve.wait_ge(mm_done, n + TILES)
                at = slice(n * BANK, (n + 1) * BANK)
                nc.vector.tensor_tensor(rows[:, at], ps[q][32 * q:32 * q + 2, :], rows[:, at], ALU.add).then_inc(row_done, 1)
            dve.wait_ge(turned, 1)
            nc.vector.tensor_copy(gain_cols[:], pt[1][:, 0:32]).then_inc(gain_done, 1)
            dve.wait_ge(gain_done, 1)
            dve.wait_ge(turned, 2)
            coefficients(nc, keep, 0, pt[0])


def side_by_side(nc, cond, panels, outs, done):
    for k in range(KD):
        for q, (panel, out) in enumerate(zip(panels, outs)):
            mm = nc.tensor.matmul(out, cond[:, k, :], panel[:, k, :], start=k == 0, stop=k == KD - 1, tile_position=(0, 32 * q))
            if k == KD - 1:
                mm.then_inc(done, 1)


def coefficients(nc, keep, l, turned):
    for n in range(2):
        for c in range(2):
            at = c * 48 + 24 * n
            nc.vector.scalar_tensor_tensor(keep.coef[:, l, n, c, 0, :], turned[:, at + 8:at + 16], 1.0,
                                           keep.gain_cols[:, (2 * l + n) * KD:(2 * l + n + 1) * KD], ALU.add, ALU.mult)
            nc.vector.tensor_copy(keep.coef[:, l, n, c, 1, :], turned[:, at:at + 8])


class Norm:

    def __init__(self, s, nc, keep, l, n, x, hT, make_hT=True):
        self.nc, self.keep, self.l, self.n, self.x, self.hT = nc, keep, l, n, x, hT
        self.sq = s.sb("sq", [P, D])
        self.ss = s.sb("ss", [P, NT])
        self.rstd = s.sb("rstd", [P, NT])
        self.eps = s.sb("eps", [P, 1])
        self.banks = [s.ps(f"turn{i}", [P, BANK]) for i in range(2)]
        self.ready = s.sem("x_ready")
        self.eps_set = s.sem("eps_set")
        self.squared = s.sem("squared")
        self.rooted = s.sem("rooted")
        self.scaled = s.sem("xn_done")
        self.rec = s.sem("rstd_done")
        self.turned = s.sem("turned")
        self.taken = s.sem("hT_done")

    def scalar(self, act, wait_x):
        nc = self.nc
        for at, width, _ in token_groups():
            first, last = at // P, (at + width) // P
            for t in range(first, last):
                wait_x(act, t)
                if t:
                    act.wait_ge(self.squared, t)
                nc.scalar.activation(self.sq[:], self.x[:, t, :], ACT.Square, accum_out=self.ss[:, t:t + 1]).then_inc(self.squared, 1)
            act.wait_ge(self.squared, last)
            if first == 0:
                act.wait_ge(self.eps_set, 1)
            nc.scalar.activation(self.rstd[:, first:last], self.ss[:, first:last], ACT.Sqrt, bias=self.eps[:], scale=1.0 / D).then_inc(self.rooted, 1)

    def vector_eps(self):
        self.nc.vector.memset(self.eps[:], EPS).then_inc(self.eps_set, 1)

    def vector_scale(self, dve, group):
        nc = self.nc
        at, width, _ = token_groups()[group]
        tiles = slice(at // P, (at + width) // P)
        dve.wait_ge(self.rooted, group + 1)
        nc.vector.reciprocal(self.rstd[:, tiles], self.rstd[:, tiles]).then_inc(self.rec, 1)
        dve.wait_ge(self.rec, group + 1)
        for t in range(tiles.start, tiles.stop):
            nc.vector.tensor_scalar(self.x[:, t, :], self.x[:, t, :], self.rstd[:, t:t + 1], None, ALU.mult).then_inc(self.scaled, 1)

    def tensor(self, pe):
        nc, n = self.nc, 0
        for at, width, _ in token_groups():
            for k in range(KD):
                pe.wait_ge(self.scaled, (at + width) // P)
                if n >= 2:
                    pe.wait_ge(self.taken, n - 1)
                for j in range(width // P):
                    mm = nc.tensor.transpose(self.banks[n % 2][:, j * P:(j + 1) * P],
                                             self.x[:, at // P + j, k * P:(k + 1) * P], self.keep.ident[:])
                mm.then_inc(self.turned, 1)
                n += 1

    def vector_turn(self, dve, groups):
        nc, n = self.nc, groups.start * KD
        for at, width, c in token_groups()[groups]:
            for k in range(KD):
                dve.wait_ge(self.turned, n + 1)
                co = self.keep.coef[:, self.l, self.n, c]
                nc.vector.tensor_scalar(self.hT[:, k, at:at + width], self.banks[n % 2][:, 0:width],
                                        co[:, 0, k:k + 1], co[:, 1, k:k + 1], ALU.mult, ALU.add).then_inc(self.taken, 1)
                n += 1
    TURNS = 3 * KD


def load_x(sp, io, x, sems, source, only=None):
    for t in range(NT) if only is None else [only]:
        src = source["x"][t * P:(t + 1) * P, :] if "x" in source else (
            source["xs"][t * P:(t + 1) * P, :] if t < NTS else source["xp"])
        sp.dma_start(x[:, t, :], src).then_inc(sems[t], 16)


def three_passes(nc, out, lhs, rhs, ks):
    passes = [(k, a, b) for k in ks for a, b in ((0, 0), (0, 1), (1, 0))]
    for n, (k, a, b) in enumerate(passes):
        mm = nc.tensor.matmul(out, lhs(a, k), rhs(b, k), start=n == 0, stop=n == len(passes) - 1)
    return mm


def project(nc, io, keep, l):
    even = l == 0
    conv_at = EVEN_TM if even else 0
    tm_at, TMW = (0, EVEN_TM) if even else (CONV, ODD_TM)
    NTM = -(-TMW // BANK)
    tmw = TMW // NTM
    TG = T // 3
    w = io["even_w_in" if even else "odd_w_in"][0].rearrange("(k p) n -> p k n", p=P)
    cw, cb = (io["hy_conv_w"], io["hy_conv_b"]) if even else (io["gdn_conv_w"], None)
    NPC = 3
    PIECES = 4
    KP = KD // PIECES
    panels = [(tm_at + j * tmw, tmw) for j in range(NTM)] + [(conv_at + j * NPC * P, NPC * P) for j in range(CC // NPC)]
    NP, PW = len(panels), max(width for _, width in panels)
    TMN = NTM * NT

    def done_with(p):
        return min(p + 1, NTM) * NT + max(p + 1 - NTM, 0) * 3 * NPC

    with Stage(nc, f"proj{l}") as s:
        x = s.sb("x", [P, NT, D])
        hT_high, hT_low = (s.sb(f"hT_{n}", [P, KD, T], F32R) for n in ("high", "low"))
        w_high, w_low = ([s.sb(f"w_{n}{i}", [P, KD, PW], F32R) for i in range(2)] for n in ("high", "low"))
        hT_raw = [s.sb(f"hT_raw{i}", [P, BANK]) for i in range(3)]
        w_raw = [s.sb(f"w_raw{i}", [P, KP, PW]) for i in range(3)]
        z = [s.sb(f"z{i}", [P, ZW]) for i in range(2)]
        zf = [s.sb(f"zf{i}", [P, ZW]) for i in range(2)]
        out = [s.sb(f"tm{i}", [P, tmw]) for i in range(4)]
        convw = s.sb("convw", [P, 4, CC])
        if not even:
            pad = s.sb("pad", [120, P])
            pad_zero, rpb_in, pad_out = s.sem("pad_zero"), s.pool_dma_sem("rpb_in"), s.pool_dma_sem("pad_out")
        norm = Norm(s, nc, keep, l, 0, x, None)
        banks = [s.ps(f"mm{i}", [P, BANK]) for i in range(6)]
        x_in = [s.sem(f"x_in{t}") for t in range(NT)]
        w_in = [s.sem(f"w_in{i}") for i in range(3)]
        conv_in, pads = s.pool_dma_sem("conv_in"), s.sem("pads")
        mm_done, z_done, tm_done = s.sem("mm_done"), s.sem("z_done"), s.sem("tm_done")
        chain, zf_done = s.sem("conv_step"), s.sem("zf_done")
        hT_up, hT_cut, w_up, w_cut = (s.sem(n) for n in ("hT_up", "hT_cut", "w_up", "w_cut"))
        zf_out = [s.pool_dma_sem(f"zf_out{i}") for i in range(2)]
        tm_out = [s.sem(f"tm_out{i}") for i in range(4)]
        blk = s.block()
        chunks = [(k, at, width, c) for at, width, c in token_groups() for k in range(KD)]

        @blk.sync
        def _(sp):
            def piece_in(m):
                at, width = panels[m // PIECES]
                k = m % PIECES * KP
                if m >= 3:
                    sp.wait_ge(w_cut, m - 2)
                sp.dma_start(w_raw[m % 3][:, :, 0:width], w[:, k:k + KP, at:at + width]).then_inc(w_in[m % 3], 16)

            def tiles_out(p):
                for t in range(NT):
                    n = p * NT + t
                    sp.wait_ge(tm_done, n + 1)
                    sp.dma_start(io["tm"][l][t * P:(t + 1) * P, p * tmw:(p + 1) * tmw], out[n % 4][:]).then_inc(tm_out[n % 4], 16)

            for m in range(3):
                piece_in(m)
            load_x(sp, io, x, x_in, io["x_of"][l])
            for m in range(3, 2 * PIECES):
                piece_in(m)
            for n in range(2, NP + 2):
                if n < NP:
                    piece_in(n * PIECES)
                if n - 2 < NTM:
                    tiles_out(n - 2)
                if n < NP:
                    for m in range(n * PIECES + 1, (n + 1) * PIECES):
                        piece_in(m)
            for i in range(4):
                sp.wait_ge(tm_out[i], 16 * len(range(i, TMN, 4)))

        @blk.gpsimd
        def _(pool):
            for n, (k, at, width, _) in enumerate(chunks):
                pool.wait_ge(hT_up, n + 1)
                nc.gpsimd.tensor_tensor(hT_low[:, k, at:at + width], hT_raw[n % 3][:, 0:width],
                                        hT_high[:, k, at:at + width].bitcast(F32), ALU.subtract).then_inc(hT_cut, 1)
            if not even:
                nc.gpsimd.memset(pad[:], 0.0).then_inc(pad_zero, 1)
                pool.wait_ge(pad_zero, 1)
                pool.dma_start(pad[:, 48:79], io["na_rpb"][0].rearrange("h r c -> (h r) c")).then_inc(rpb_in, 16)
                pool.wait_ge(rpb_in, 16)
                pool.dma_start(io["rpbpad"], pad[:].unsqueeze(1).broadcast_to([120, GRID_W, P])).then_inc(pad_out, 16)
                pool.wait_ge(pad_out, 16)
            for i in range(3):
                pool.dma_start(convw[:, i, :], cw[0, i].rearrange("(c p) -> p c", p=P), allow_slow_non_contiguous=True).then_inc(conv_in, 16)
            if cb is not None:
                pool.dma_start(convw[:, 3, :], cb[0].rearrange("(c p) -> p c", p=P), allow_slow_non_contiguous=True).then_inc(conv_in, 16)
            for c in range(CC):
                pool.wait_ge(zf_done, c + 1)
                rows = io["conv"][l][c * P:(c + 1) * P, :]
                pool.dma_start(rows[:, 0:TS], zf[c % 2][:, 1:1 + TS]).then_inc(zf_out[c % 2], 16)
                pool.dma_start(rows[:, TS:T], zf[c % 2][:, 2 + TS:2 + T]).then_inc(zf_out[c % 2], 16)
            for i in range(2):
                pool.wait_ge(zf_out[i], 32 * CC // 2)

        @blk.tensor
        def _(pe):
            norm.tensor(pe)
            n = 0
            for p, (_, width) in enumerate(panels):
                pe.wait_ge(w_cut, PIECES * (p + 1))
                wp = (w_high[p % 2], w_low[p % 2])
                hp = (hT_high, hT_low)
                for i in range(NT if p < NTM else 3 * NPC):
                    if n >= 6:
                        if n - 6 < TMN:
                            pe.wait_ge(tm_done, n - 5)
                        else:
                            pe.wait_ge(z_done, n - 5 - TMN)
                    if p < NTM:
                        if p == 0:
                            pe.wait_ge(hT_cut, KD * (i // 4 + 1))
                        mm = three_passes(nc, banks[n % 6][:, 0:width], lambda a, k: hp[a][:, k, i * P:(i + 1) * P],
                                          lambda a, k: wp[a][:, k, 0:width], range(KD))
                    else:
                        j, g = divmod(i, 3)
                        if p == NTM:
                            pe.wait_ge(hT_cut, 3 * KD)
                        mm = three_passes(nc, banks[n % 6][:, 0:TG], lambda a, k: wp[a][:, k, j * P:(j + 1) * P],
                                          lambda a, k: hp[a][:, k, g * TG:(g + 1) * TG], range(KD))
                    mm.then_inc(mm_done, 1)
                    n += 1

        @blk.scalar
        def _(act):
            norm.scalar(act, lambda eng, t: eng.wait_ge(x_in[t], 16))
            for n, (k, at, width, _) in enumerate(chunks):
                act.wait_ge(norm.taken, n + 1)
                nc.scalar.activation(hT_high[:, k, at:at + width], hT_raw[n % 3][:, 0:width], ACT.Copy).then_inc(hT_up, 1)
            for n in range(TMN):
                act.wait_ge(mm_done, n + 1)
                if n >= 4:
                    act.wait_ge(tm_out[n % 4], 16 * (n // 4))
                nc.scalar.activation(out[n % 4][:], banks[n % 6][:, 0:tmw], ACT.Copy).then_inc(tm_done, 1)
            act.wait_ge(pads, 2)
            n = TMN
            for c in range(CC):
                if c >= 2:
                    act.wait_ge(zf_done, c - 1)
                for g in range(3):
                    act.wait_ge(mm_done, n + 1)
                    for lo, hi, to in ((g * TG, min((g + 1) * TG, TS), 1), (max(g * TG, TS), (g + 1) * TG, 2)):
                        if lo < hi:
                            ins = nc.scalar.activation(z[c % 2][:, lo + to:hi + to], banks[n % 6][:, lo - g * TG:hi - g * TG], ACT.Copy)
                    ins.then_inc(z_done, 1)
                    n += 1

        @blk.vector
        def _(dve):
            link = Link(dve, chain)

            def piece(m):
                n, k, wd = m // PIECES, m % PIECES * KP, panels[m // PIECES][1]
                raw = w_raw[m % 3][:, :, 0:wd]
                high, low = (a[n % 2][:, k:k + KP, 0:wd] for a in (w_high, w_low))
                dve.wait_ge(w_in[m % 3], 16 * (m // 3 + 1))
                if n >= 2:
                    dve.wait_ge(mm_done, done_with(n - 2))
                nc.vector.tensor_copy(high, raw).then_inc(w_up, 1)
                dve.wait_ge(w_up, m + 1)
                nc.vector.tensor_tensor(low, raw, high.bitcast(F32), ALU.subtract).then_inc(w_cut, 1)

            def panel(n):
                for m in range(n * PIECES, (n + 1) * PIECES):
                    piece(m)

            def convolve(c):
                dve.wait_ge(z_done, 3 * (c + 1))
                if c >= 2:
                    dve.wait_ge(zf_out[c % 2], 32 * (c // 2))
                zi, zo, n = z[c % 2], zf[c % 2], ZW - 2
                link(nc.vector.tensor_scalar(zo[:, 1:1 + n], zi[:, 1:1 + n], convw[:, 1, c:c + 1], convw[:, 3, c:c + 1], ALU.mult, ALU.add))
                link(nc.vector.scalar_tensor_tensor(zo[:, 1:1 + n], zi[:, 0:n], convw[:, 0, c:c + 1], zo[:, 1:1 + n], ALU.mult, ALU.add))
                nc.vector.scalar_tensor_tensor(zo[:, 1:1 + n], zi[:, 2:2 + n], convw[:, 2, c:c + 1], zo[:, 1:1 + n],
                                               ALU.mult, ALU.add).then_inc(zf_done, 1)

            norm.vector_eps()
            for m in range(3):
                piece(m)
            for g in range(3):
                norm.vector_scale(dve, g)
            piece(3)
            for n, (k, at, width, c) in enumerate(chunks):
                dve.wait_ge(norm.turned, n + 1)
                if n >= 3:
                    dve.wait_ge(hT_cut, n - 2)
                co = keep.coef[:, l, 0, c]
                nc.vector.tensor_scalar(hT_raw[n % 3][:, 0:width], norm.banks[n % 2][:, 0:width],
                                        co[:, 0, k:k + 1], co[:, 1, k:k + 1], ALU.mult, ALU.add).then_inc(norm.taken, 1)
            panel(1)
            for i in range(2):
                nc.vector.memset(z[i][:], 0.0).then_inc(pads, 1)
            for p in range(2, NTM + 1):
                panel(p)
            dve.wait_ge(conv_in, 16 * (3 if cb is None else 4))
            if cb is None:
                link(nc.vector.memset(convw[:, 3, :], 0.0))
            for p in range(NTM, NP):
                if p + 1 < NP:
                    panel(p + 1)
                for c in range(NPC * (p - NTM), NPC * (p - NTM + 1)):
                    convolve(c)


class AttnPlan:

    def __init__(self, l):
        self.l = l
        self.even = l == 0
        self.nkc = 1 if self.even else 4
        self.W = 512 if self.even else 768
        self.groups = []
        for t in range(NTS):
            if self.even:
                keys = [k for k in (t - 1, t, t + 1) if 0 <= k < NTS]
            else:
                lo = [0, 0, 0, 1, 2, 3, 4, 4][t]
                hi = [4, 4, 5, 6, 7, 8, 8, 8][t]
                keys = list(range(lo, hi))
            self.groups.append((t, keys, True))
        self.groups.append((NTS, [NTS], False))
        self.units = [(g, h) for g in range(len(self.groups)) for h in range(8)]

    def chunk_half(self, h):
        return (h % 4, h // 4) if self.even else (h // 2, h % 2)

    def kv_chunk(self, h):
        return 0 if self.even else h // 2

    def columns(self, g):
        t, keys, cached = self.groups[g]
        return P * (len(keys) + cached)


def attention(nc, io, keep, l):
    plan = AttnPlan(l)
    even, W, nkc = plan.even, plan.W, plan.nkc
    tmw = EVEN_TM if even else 3 * MIX
    tm_at = 0 if even else MIX + 32
    k_at, v_at = (512, 640) if even else (512, 1024)
    kw = nkc * P
    units, groups = plan.units, plan.groups
    with Stage(nc, f"attn{l}") as s:
        tok = s.sb("tok", [P, NT, tmw])
        QT = s.sb("QT", [P, 4, T])
        KT = s.sb("KT", [P, nkc, T])
        CKT = s.sb("CKT", [P, nkc, P])
        ck = s.sb("ck", [P, kw])
        cv = s.sb("cv", [P, kw])
        SB = 8 if even else 2
        sc_sb = s.sb("sc_sb", [P, SB, W + 1])
        if even:
            band = s.sb("band", [P, 512 + 384])
        else:
            bias = s.sb("bias", [P, 8, 14, GRID_W])
            bias_mid = s.sb("bias_mid", [P, 8, 10, GRID_W])
            zeros = s.sb("zeros", [P, P])
        sink = s.sb("sink", [P, 8])
        attention_setup(nc, io, keep, plan, locals())
        attention_units(nc, io, keep, plan, locals())


def attention_setup(nc, io, keep, plan, m):
    l, even, nkc, W = plan.l, plan.even, plan.nkc, plan.W
    tok, QT, KT, CKT, ck, cv, sink, sc_sb = (m[x] for x in ("tok", "QT", "KT", "CKT", "ck", "cv", "sink", "sc_sb"))
    tm_at, tmw, k_at, v_at, kw = (m[x] for x in ("tm_at", "tmw", "k_at", "v_at", "kw"))
    tm = io["tm"][l]
    cache = ("cache_attn_k", "cache_attn_v") if even else ("cache_na_k", "cache_na_v")
    outk, outv = ("new_attn_k", "new_attn_v") if even else ("new_na_k", "new_na_v")
    with Stage(nc, f"attnset{l}") as s:
        tok_in = [s.sem(f"tok_in{t}") for t in range(NT)]
        ck_in, cv_in, kv_out, mask_in = s.sem("ck_in"), s.sem("cv_in"), s.sem("kv_out"), s.pool_dma_sem("mask_in")
        v_in = s.sem("v_in")
        roped, chain, turned, q_taken, k_taken = (s.sem(n) for n in ("roped", "rope_step", "turned", "q_taken", "k_taken"))
        pq = [s.ps(f"pq{i}", [P, BANK]) for i in range(2)]
        pk = [s.ps(f"pk{i}", [P, BANK]) for i in range(2)]
        if even:
            trig_in = s.sem("trig_in")
            trig = s.sb("trig", [P, 2, NTS, 32])
            c1 = s.sb("c1", [P, 10, 2, 32])
            s1 = s.sb("s1", [P, 10, 2, 32])
        else:
            colm = s.sb("colm", [P, GRID_W])
            bias_done = s.sem("bias_done")
            bias_in = [s.sem(f"bias_in{h}") for h in range(2)]
        blk = s.block()

        def add_columns(eng, half):
            rows = m["bias"][:, 4 * half:4 * half + 4].rearrange("p h r c -> p (h r) c")
            eng.tensor_tensor(rows, rows, colm[:].rearrange("p (o c) -> p o c", o=1).broadcast_to([P, 56, GRID_W]), ALU.add).then_inc(bias_done, 1)

        @blk.sync
        def _(sp):
            for t in range(NT):
                sp.dma_start(tok[:, t, 0:v_at], tm[t * P:(t + 1) * P, tm_at:tm_at + v_at]).then_inc(tok_in[t], 16)
            sp.dma_start(ck[:], io[cache[0]][0, 0].rearrange("t h d -> t (h d)")).then_inc(ck_in, 16)
            sp.dma_start(cv[:], io[cache[1]][0, 0].rearrange("t h d -> t (h d)")).then_inc(cv_in, 16)
            if not even:
                flat = io["rpbpad"]
                for h in range(8):
                    for half in range(2):
                        src = bass.AP(flat.tensor, flat.offset + (h * 15 + 1 - half) * GRID_W * P + 63,
                                      [[P - 1, 64], [GRID_W * P, 14], [1, GRID_W]])
                        sp.dma_start(m["bias"][half * 64:half * 64 + 64, h], src).then_inc(bias_in[h // 4], 16)
            sp.dma_start(tok[:, :, v_at:tmw], tm[:, tm_at + v_at:tm_at + tmw].rearrange("(t p) c -> p t c", p=P)).then_inc(v_in, 16)
            rows = tm[TS:T, :]
            sp.dma_start(io[outk][0, 0].rearrange("t h d -> t (h d)"), rows[:, tm_at + k_at:tm_at + k_at + kw]).then_inc(kv_out, 16)
            sp.dma_start(io[outv][0, 0].rearrange("t h d -> t (h d)"), rows[:, tm_at + v_at:tm_at + v_at + kw]).then_inc(kv_out, 16)
            sp.wait_ge(kv_out, 32)
            sp.wait_ge(cv_in, 16)
            sp.wait_ge(v_in, 16)

        @blk.tensor
        def _(pe):
            for n in range(NT + 1):
                cached = n == NT
                if cached:
                    pe.wait_ge(ck_in, 16)
                else:
                    pe.wait_ge(tok_in[n], 16)
                if even and n < NT:
                    pe.wait_ge(roped, n + 1)
                if n >= 2:
                    pe.wait_ge(q_taken, n - 1)
                    pe.wait_ge(k_taken, n - 1)
                if not cached:
                    for j in range(4):
                        nc.tensor.transpose(pq[n % 2][:, j * P:(j + 1) * P], tok[:, n, j * P:(j + 1) * P], keep.ident[:])
                for j in range(nkc):
                    src = ck[:, j * P:(j + 1) * P] if cached else tok[:, n, k_at + j * P:k_at + (j + 1) * P]
                    mm = nc.tensor.transpose(pk[n % 2][:, j * P:(j + 1) * P], src, keep.ident[:])
                mm.then_inc(turned, 1)

        @blk.scalar
        def _(act):
            if even:
                act.dma_start(trig[:, 0], io["cos"]).then_inc(trig_in, 16)
                act.dma_start(trig[:, 1], io["sin"]).then_inc(trig_in, 16)
            for n in range(NT):
                act.wait_ge(turned, n + 1)
                nc.scalar.activation(QT[:, :, n * P:(n + 1) * P], pq[n % 2][:].rearrange("p (j t) -> p j t", j=4),
                                     ACT.Copy, scale=HD ** -0.5).then_inc(q_taken, 1)
            if not even:
                act.wait_ge(bias_done, 2)
                nc.scalar.activation(m["bias_mid"][:, 4:8, 1:8, :], m["bias"][:, 4:8, 3:10, :], ACT.Copy)

        @blk.gpsimd
        def _(pool):
            if even:
                pool.dma_start(m["band"][:], io["band"]).then_inc(mask_in, 16)
                pool.dma_start(sink[:], all_rows(io["attn_sink"][0])).then_inc(mask_in, 16)
                pool.wait_ge(mask_in, 32)
                nc.gpsimd.tensor_copy(sc_sb[:, :, W:W + 1], sink[:].rearrange("p (h o) -> p h o", o=1))
            else:
                bias, mid = m["bias"], m["bias_mid"]
                nc.gpsimd.memset(m["zeros"][:], 0.0)
                pool.dma_start(colm[:], io["colmask"]).then_inc(mask_in, 16)
                pool.wait_ge(mask_in, 16)
                pool.wait_ge(bias_in[0], 128)
                add_columns(nc.gpsimd, 0)
                pool.wait_ge(bias_done, 2)
                nc.gpsimd.tensor_copy(mid[:, 0:4, 1:8, :], bias[:, 0:4, 3:10, :])

        def take_keys(dve, n):
            dve.wait_ge(turned, n + 1)
            dst = CKT[:] if n == NT else KT[:, :, n * P:(n + 1) * P]
            nc.vector.tensor_copy(dst, pk[n % 2][:, 0:kw].rearrange("p (j t) -> p j t", j=nkc)).then_inc(k_taken, 1)

        @blk.vector
        def _(dve):
            if even:
                dve.wait_ge(trig_in, 32)
            else:
                nc.vector.memset(m["bias_mid"][0:64, :, 8:10, :], NEG)
                nc.vector.memset(m["bias_mid"][64:128, :, 0:1, :], NEG)
                nc.vector.memset(m["bias_mid"][64:128, :, 9:10, :], NEG)
            for n in range(NT):
                if even:
                    dve.wait_ge(tok_in[n], 16)
                    x = tok[:, n, 0:640].rearrange("p (h a d) -> p h a d", a=2, d=32)
                    q_out = tok[:, n, 0:512].rearrange("p (j s a d) -> p s j a d", s=2, a=2, d=32)
                    if n < NTS:
                        cos, sin = (trig[:, i, n:n + 1, :].unsqueeze(1).broadcast_to([P, 10, 2, 32]) for i in range(2))
                        nc.vector.tensor_tensor(c1[:], x, cos, ALU.mult).then_inc(chain, 1)
                        nc.vector.tensor_tensor(s1[:], x, sin, ALU.mult).then_inc(chain, 1)
                        dve.wait_ge(chain, 2 * n + 2)
                        for a, op in ((0, ALU.subtract), (1, ALU.add)):
                            nc.vector.tensor_tensor(x[:, 8:10, a, :], c1[:, 8:10, a, :], s1[:, 8:10, 1 - a, :], op)
                            ins = nc.vector.tensor_tensor(q_out[:, :, :, a, :], c1[:, 0:8, a, :].rearrange("p (s j) d -> p s j d", s=2),
                                                          s1[:, 0:8, 1 - a, :].rearrange("p (s j) d -> p s j d", s=2), op)
                    else:
                        nc.vector.tensor_copy(c1[:], x).then_inc(chain, 1)
                        dve.wait_ge(chain, 2 * n + 1)
                        for a in range(2):
                            ins = nc.vector.tensor_copy(q_out[:, :, :, a, :], c1[:, 0:8, a, :].rearrange("p (s j) d -> p s j d", s=2))
                    ins.then_inc(roped, 1)
                    dve.wait_ge(roped, n + 1)
                if n >= 1:
                    take_keys(dve, n - 1)
            take_keys(dve, NT - 1)
            take_keys(dve, NT)
            if not even:
                dve.wait_ge(mask_in, 16)
                dve.wait_ge(bias_in[1], 128)
                add_columns(nc.vector, 1)
                dve.wait_ge(bias_done, 2)
                nc.vector.tensor_copy(m["bias_mid"][64:128, :, 8:9, :], m["bias"][64:128, :, 10:11, :])
                nc.vector.tensor_copy(m["bias_mid"][0:64, :, 0:1, :], m["bias"][0:64, :, 2:3, :])


def attention_units(nc, io, keep, plan, m):
    l, even, W, units, groups = plan.l, plan.even, plan.W, plan.units, plan.groups
    tok, QT, KT, CKT, cv, sink, sc_sb, SB, v_at = (m[x] for x in ("tok", "QT", "KT", "CKT", "cv", "sink", "sc_sb", "SB", "v_at"))
    NU, NG, WB = len(units), len(groups), -(-W // BANK) * BANK
    RT = 2 if even else 1
    row0 = 0 if even else MIX
    with Stage(nc, f"attnrun{l}") as s:
        mx1 = s.sb("mx1", [P, 4])
        mx = s.sb("mx", [P, 4])
        neg = s.sb("neg", [P, 4])
        prob = s.sb("prob", [P, 2, W + 1])
        rs = s.sb("rs", [P, 2, 8])
        rinv = s.sb("rinv", [P, 2, 8])
        pT = s.sb("pT", [P, 2, W])
        o_sb = s.sb("o_sb", [P, 2, 8, HD])
        oT = s.sb("oT", [P, 2, 4, P])
        psc = [s.ps(f"sc{i}", [P, WB]) for i in range(2)]
        pt = [s.ps(f"pt{i}", [P, WB]) for i in range(RT)]
        po = s.ps("po", [P, 8, P])
        sc_done, red_part, red_done, neg_done, exp_done = (s.sem(n) for n in ("sc_done", "red_part", "red_done", "neg_done", "exp_done"))
        p_turned, pT_done, pv_done, rinv_done, o_done, o_turned, oT_done = (
            s.sem(n) for n in ("p_turned", "pT_done", "pv_done", "rinv_done", "o_done", "o_turned", "oT_done"))
        out = [s.sem(f"oT_out{i}") for i in range(2)]
        MW = BANK // 2
        MG = 6 * D // (4 * MW) if even else 0
        if even:
            m_ring = [s.sb(f"m_w{i}", [P, KD, MW]) for i in range(8)]
            m_part = s.sb("m_part", [2, 2, 4 * MW])
            m_rows = s.sb("m_rows", [2, 6 * D])
            m_flat = s.sb("m_flat", [96, P])
            pm = [s.ps(f"pm{i}", [P, 2, MW]) for i in range(2)]
            m_in = [s.sem(f"m_in{i}") for i in range(8)]
            m_bias_in, m_mm, m_taken, m_added, m_out, m_flat_in, m_turned = (
                s.sem(n) for n in ("m_bias_in", "m_mm", "m_taken", "m_added", "m_out", "m_flat_in", "m_turned"))
        blk = s.block()

        def m_bank(q):
            return pm[q // 2][32 * q:32 * q + 2, q % 2, :]

        def m_load(sp, g):
            for q in range(4):
                r, at = (4 * g + q) % 8, (4 * g + q) * MW
                sp.dma_start(m_ring[r][:], io["w_ada"][1].rearrange("(k p) n -> p k n", p=P)[:, :, at:at + MW]).then_inc(m_in[r], 16)

        turns = []
        for u in range(NU):
            turns.append(("p", u))
            if u % 8 == 1 and u >= 8:
                turns.append(("o", u // 8 - 1))
        turns.append(("o", NG - 1))

        def slot_free(eng, what):
            n = turns.index(what)
            if n >= RT:
                kind, i = turns[n - RT]
                eng.wait_ge(pT_done if kind == "p" else oT_done, i + 1)
            return pt[n % RT]

        def slot(what):
            return pt[turns.index(what) % RT]

        def scores(pe, u):
            g, h = units[u]
            t, keys, cached = groups[g]
            j, half = plan.chunk_half(h)
            rows = slice(64 * half, 64 * half + 64)
            if u >= 2:
                pe.wait_ge(red_done, u - 1)
            q = QT[rows, j, t * P:(t + 1) * P]
            tiles = [KT[rows, plan.kv_chunk(h), k * P:(k + 1) * P] for k in keys]
            if cached:
                tiles = [CKT[rows, plan.kv_chunk(h), :]] + tiles if even else tiles + [CKT[rows, plan.kv_chunk(h), :]]
            at = W - P * len(tiles)
            for i, k in enumerate(tiles):
                mm = nc.tensor.matmul(psc[u % 2][:, at + i * P:at + (i + 1) * P], q, k, start=True, stop=True)
            mm.then_inc(sc_done, 1)

        def turn_probs(pe, u):
            n = plan.columns(units[u][0]) // P
            dst = slot_free(pe, ("p", u))
            pe.wait_ge(exp_done, u + 1)
            for i in range(n):
                mm = nc.tensor.transpose(dst[:, i * P:(i + 1) * P], prob[:, u % 2, W - (n - i) * P:W - (n - i - 1) * P], keep.ident[:])
            mm.then_inc(p_turned, 1)

        def values(pe, u):
            g, h = units[u]
            t, keys, cached = groups[g]
            at = P * plan.kv_chunk(h)
            tiles = [tok[:, k, v_at + at:v_at + at + P] for k in keys]
            if cached:
                tiles = [cv[:, at:at + P]] + tiles if even else tiles + [cv[:, at:at + P]]
            if h == 0 and g >= 1:
                pe.wait_ge(o_done, g)
            pe.wait_ge(pT_done, u + 1)
            for i, v in enumerate(tiles):
                mm = nc.tensor.matmul(po[:, h, :], pT[:, u % 2, i * P:(i + 1) * P], v, start=i == 0, stop=i == len(tiles) - 1)
            mm.then_inc(pv_done, 1)

        def turn_outputs(pe, g):
            dst = slot_free(pe, ("o", g))
            pe.wait_ge(o_done, g + 1)
            for j in range(4):
                mm = nc.tensor.transpose(dst[:, j * P:(j + 1) * P], o_sb[:, g % 2, 2 * j:2 * j + 2, :], keep.ident[:])
            mm.then_inc(o_turned, 1)

        @blk.tensor
        def _(pe):
            scores(pe, 0)
            scores(pe, 1)
            for u in range(NU):
                turn_probs(pe, u)
                if u + 2 < NU:
                    scores(pe, u + 2)
                if u >= 1:
                    values(pe, u - 1)
                if u % 8 == 1 and u >= 8:
                    turn_outputs(pe, u // 8 - 1)
                if u % 8 == 4 and u // 8 < MG:
                    g = u // 8
                    for r in range(4 * (g % 2), 4 * (g % 2) + 4):
                        pe.wait_ge(m_in[r], 16 * (g // 2 + 1))
                    if g:
                        pe.wait_ge(m_taken, g)
                    side_by_side(nc, keep.silu, m_ring[4 * (g % 2):4 * (g % 2) + 4], [m_bank(q) for q in range(4)], m_mm)
            values(pe, NU - 1)
            turn_outputs(pe, NG - 1)
            if even:
                pe.wait_ge(m_flat_in, 16)
                nc.tensor.transpose(pm[0][:].rearrange("p a b -> p (a b)")[:, 0:96], m_flat[:], keep.ident[0:96, 0:96]).then_inc(m_turned, 1)

        @blk.vector
        def _(dve):
            parts = 0

            def take_probs(u):
                n = plan.columns(units[u][0])
                if u >= 2:
                    dve.wait_ge(pv_done, u - 1)
                dve.wait_ge(p_turned, u + 1)
                nc.vector.tensor_copy(pT[:, u % 2, 0:n], slot(("p", u))[:, 0:n]).then_inc(pT_done, 1)

            def take_outputs(g):
                dve.wait_ge(exp_done, 8 * (g + 1))
                nc.vector.reciprocal(rinv[:, g % 2, :], rs[:, g % 2, :]).then_inc(rinv_done, 1)
                dve.wait_ge(rinv_done, g + 1)
                dve.wait_ge(pv_done, 8 * (g + 1))
                if g >= 2:
                    dve.wait_ge(o_turned, g - 1)
                for half in range(2):
                    if even:
                        src, r, dst = po[:, 4 * half:4 * half + 4, 64 * half:64 * half + 64], rinv[:, g % 2, 4 * half:4 * half + 4], o_sb[:, g % 2, 4 * half:4 * half + 4, :]
                    else:
                        src, r, dst = po[:, half:8:2, 64 * half:64 * half + 64], rinv[:, g % 2, half:8:2], o_sb[:, g % 2, half:8:2, :]
                    ins = nc.vector.tensor_tensor(dst, src, r.unsqueeze(2).broadcast_to([P, 4, HD]), ALU.mult)
                ins.then_inc(o_done, 1)

            for u in range(NU + 2):
                if u < NU:
                    g, h = units[u]
                    t, keys, cached = groups[g]
                    n = plan.columns(g)
                    at = W - n
                    dve.wait_ge(sc_done, u + 1)
                    if u >= SB:
                        dve.wait_ge(exp_done, u - SB + 1)
                    if u >= 4:
                        dve.wait_ge(exp_done, u - 3)
                    red = mx[:, u % 4:u % 4 + 1]
                    if even:
                        band = m["band"]
                        mask = band[:, 512:896] if g == 0 else band[:, 0:n]
                        nc.vector.tensor_tensor_reduce(out=sc_sb[:, u % SB, at:W], in0=psc[u % 2][:, at:W], in1=mask, scale=1.0,
                                                       scalar=sink[:, h:h + 1], op0=ALU.add, op1=ALU.max, accum_out=red).then_inc(red_done, 1)
                    elif not cached:
                        nc.vector.tensor_tensor_reduce(out=sc_sb[:, u % SB, at:W], in0=psc[u % 2][:, at:W], in1=m["zeros"][:, 0:n], scale=1.0,
                                                       scalar=-3e38, op0=ALU.add, op1=ALU.max, accum_out=red).then_inc(red_done, 1)
                    else:
                        r0 = 2 * t
                        first = 2 * keys[0] - r0
                        nrow = 2 * len(keys)
                        src = m["bias_mid"][:, h, :, :] if nrow == 10 else m["bias"][:, h, first + 6:first + 6 + nrow, :]
                        nc.vector.tensor_tensor_reduce(out=sc_sb[:, u % SB, W - P:W], in0=psc[u % 2][:, W - P:W], in1=m["zeros"][:], scale=1.0,
                                                       scalar=-3e38, op0=ALU.add, op1=ALU.max, accum_out=mx1[:, u % 4:u % 4 + 1]).then_inc(red_part, 1)
                        parts += 1
                        dve.wait_ge(red_part, parts)
                        nc.vector.tensor_tensor_reduce(out=sc_sb[:, u % SB, at:W - P], in0=psc[u % 2][:, at:W - P], in1=src.rearrange("p r c -> p (r c)"), scale=1.0,
                                                       scalar=mx1[:, u % 4:u % 4 + 1], op0=ALU.add, op1=ALU.max, accum_out=red).then_inc(red_done, 1)
                    dve.wait_ge(red_done, u + 1)
                    nc.vector.tensor_scalar(neg[:, u % 4:u % 4 + 1], red, -1.0, None, ALU.mult).then_inc(neg_done, 1)
                if 1 <= u <= NU:
                    take_probs(u - 1)
                if u >= 9 and (u - 9) % 8 == 0:
                    take_outputs((u - 9) // 8)
            if even:
                dve.wait_ge(m_turned, 1)
                coefficients(nc, keep, 1, pm[0][:].rearrange("p a b -> p (a b)"))

        @blk.scalar
        def _(act):
            def take_turned(g):
                if g >= 2:
                    act.wait_ge(out[g % 2], 16 * (g // 2))
                act.wait_ge(o_turned, g + 1)
                nc.scalar.activation(oT[:, g % 2], slot(("o", g))[:, 0:BANK].rearrange("p (j t) -> p j t", j=4), ACT.Copy).then_inc(oT_done, 1)

            for u in range(NU):
                g, h = units[u]
                at = W - plan.columns(g)
                act.wait_ge(neg_done, u + 1)
                if u >= 2:
                    act.wait_ge(p_turned, u - 1)
                if h == 0 and g >= 2:
                    act.wait_ge(rinv_done, g - 1)
                end = W + 1 if even else W
                nc.scalar.activation(prob[:, u % 2, at:end], sc_sb[:, u % SB, at:end], ACT.Exp, bias=neg[:, u % 4:u % 4 + 1],
                                     accum_out=rs[:, g % 2, h:h + 1]).then_inc(exp_done, 1)
                if u % 8 == 3 and u >= 8:
                    take_turned(u // 8 - 1)
                if u % 8 == 5 and u // 8 < MG:
                    g = u // 8
                    act.wait_ge(m_mm, 4 * (g + 1))
                    if g >= 2:
                        act.wait_ge(m_added, g - 1)
                    for q in range(4):
                        ins = nc.scalar.activation(m_part[:, g % 2, q * MW:(q + 1) * MW], m_bank(q), ACT.Copy)
                    ins.then_inc(m_taken, 1)
            take_turned(NG - 1)

        @blk.gpsimd
        def _(pool):
            for g in range(MG):
                if g == 0:
                    pool.wait_ge(m_bias_in, 32)
                pool.wait_ge(m_taken, g + 1)
                at = slice(4 * g * MW, 4 * (g + 1) * MW)
                nc.gpsimd.tensor_tensor(m_rows[:, at], m_part[:, g % 2, :], m_rows[:, at], ALU.add).then_inc(m_added, 1)

        @blk.sync
        def _(sp):
            if even:
                m_load(sp, 0)
                m_load(sp, 1)
                for c in range(2):
                    sp.dma_start(m_rows[c:c + 1, :], io["b_ada"][1:2, :]).then_inc(m_bias_in, 16)
            for g, (t, _, _) in enumerate(groups):
                if g + 2 < MG:
                    sp.wait_ge(m_mm, 4 * (g + 1))
                    m_load(sp, g + 2)
                if even and g == MG:
                    sp.wait_ge(m_added, MG)
                    sp.dma_start(io["mrow"][1], m_rows[:]).then_inc(m_out, 16)
                    sp.wait_ge(m_out, 16)
                    sp.dma_start(m_flat[:], io["mrow"][1].rearrange("c (j p) -> (c j) p", p=P)).then_inc(m_flat_in, 16)
                sp.wait_ge(oT_done, g + 1)
                sp.dma_start(io["mixT"][l][row0:row0 + MIX, t * P:(t + 1) * P].rearrange("(j p) t -> p j t", p=P), oT[:, g % 2]).then_inc(out[g % 2], 16)
            for i in range(2):
                sp.wait_ge(out[i], 16 * len(range(i, NG, 2)))



SIN_TURN = 2.0 * math.pi
TURN_HI = 6.28125
TURN_LO = SIN_TURN - TURN_HI
ROUND = 1.5 * 2.0 ** 23
PI_DOWN = 3.1415925


def hyena_filters(nc, io, keep):
    FW = 64
    with Stage(nc, "filt") as s:
        feats = s.sb("feats", [33, T])
        w1 = s.sb("w1", [33, FW])
        w2 = s.sb("w2", [FW, FW])
        w3 = s.sb("w3", [FW, 4 * MIX])
        cols = s.sb("cols", [FW, 3])
        fb = s.sb("fb", [FW, 2])
        arg = s.sb("arg", [FW, T])
        turns = s.sb("turns", [FW, T])
        hid = [s.sb(f"hid{i}", [FW, T]) for i in range(2)]
        win = s.sb("win", [P, NT, MIX])
        win_b = s.sb("win_b", [P, 2, MIX])
        A = s.sb("A", [P, 2, MIX])
        B = s.sb("B", [P, 2, MIX])
        absA = s.sb("absA", [P, 2, MIX])
        absB = s.sb("absB", [P, 2, MIX])
        taps = s.sb("taps", [P, NT, 2, 2 * MIX])
        ones = s.sb("ones", [P, P])
        sums_sb = s.sb("sums", [P, 2 * MIX])
        cf = s.sb("cf", [P, 2, NTS, 512])
        cfp = s.sb("cfp", [P, 2, P])
        first = s.sb("first", [P, 2, MIX])
        res = s.sb("res", [P, 2, 2, MIX])
        bk = [s.ps(f"b{i}", [P, BANK]) for i in range(2)]
        hp = s.ps("hp", [P, 4, MIX])
        sp_ = s.ps("sum", [P, 2, MIX])
        small_in, w3_in, win_in, cf_in = s.sem("small_in"), s.sem("w3_in"), s.sem("win_in"), s.sem("cf_in")
        hid_mm, arg_done, red, sin_done = s.sem("hid_mm"), s.sem("arg_done"), s.sem("reduced"), s.sem("sin_done")
        chain, h_done, ab_done, abs_done, abs_sum, taps_done, sum_done = (
            s.sem(n) for n in ("chain", "h_done", "ab_done", "abs_done", "abs_sum", "taps_done", "sum_done"))
        sum_taken, sum_turned, inv_taken = s.sem("sum_taken"), s.sem("sum_turned"), s.sem("inv_taken")
        dft_done, first_done, res_done, ones_set = s.sem("dft_done"), s.sem("first_done"), s.sem("res_done"), s.sem("ones_set")
        res_out = [s.sem(f"res_out{i}") for i in range(2)]
        blk = s.block()
        spans = [(0, 512), (512, 512), (1024, 128)]
        jobs = [(q, o, cs) for q in range(4) for o in range(2) for cs in range(2)] + [(8, o, cs) for o in range(2) for cs in range(2)]

        @blk.sync
        def _(sp):
            sp.dma_start(feats[:], io["feats"]).then_inc(small_in, 16)
            sp.dma_start(w1[:], io["hy_w1"][0]).then_inc(small_in, 16)
            sp.dma_start(w2[:], io["hy_w2"][0]).then_inc(small_in, 16)
            for i, n in enumerate(("hy_b1", "hy_b2", "hy_freq")):
                sp.dma_start(cols[:, i:i + 1], io[n][0].rearrange("(p o) -> p o", o=1), allow_slow_non_contiguous=True).then_inc(small_in, 16)
            sp.dma_start(w3[:], io["hy_w3"][0]).then_inc(w3_in, 16)
            sp.dma_start(win[:], io["win"].rearrange("(t p) c -> p t c", p=P)).then_inc(win_in, 16)
            sp.dma_start(win_b[:], io["win_b"].rearrange("t p c -> p t c")).then_inc(win_in, 16)
            for i in range(2):
                sp.dma_start(cf[:, i], io["filt_dft"][i].rearrange("(t p) f -> p t f", p=P)).then_inc(cf_in, 16)
                sp.dma_start(cfp[:, i], io["filt_dft_p"][i]).then_inc(cf_in, 16)
            for n, (q, o, cs) in enumerate(jobs):
                sp.wait_ge(res_done, n + 1)
                sp.dma_start(io["spec"][q, :, o, cs, :], res[:, n % 2, 0, :]).then_inc(res_out[n % 2], 16)
                if q < 8:
                    sp.dma_start(io["spec"][4 + q, :, o, cs, :], res[:, n % 2, 1, :]).then_inc(res_out[n % 2], 16)
            for i in range(2):
                sp.wait_ge(res_out[i], 16 * sum(1 if q == 8 else 2 for q, _, _ in jobs[i::2]))

        def sums(pe, t):
            if t == NTS:
                pe.wait_ge(sum_taken, 1)
            pe.wait_ge(abs_sum, t + 1)
            for o in range(2):
                mm = nc.tensor.matmul(sp_[:, o, :], ones[:], absA[:, o, :], start=t in (0, NTS), stop=t >= NTS - 1)
            mm.then_inc(sum_done, 1)

        @blk.tensor
        def _(pe):
            pe.wait_ge(small_in, 96)
            for layer in range(2):
                if layer:
                    pe.wait_ge(sin_done, 1)
                for i, (at, w) in enumerate(spans):
                    dst = (bk + [hp[:, 0, :]])[i]
                    lhs, rhs = (w1[:], feats[:, at:at + w]) if layer == 0 else (w2[:], hid[0][:, at:at + w])
                    mm = nc.tensor.matmul(dst[0:FW, 0:w], lhs, rhs, start=True, stop=True)
                mm.then_inc(hid_mm, 1)
            pe.wait_ge(sin_done, 2)
            pe.wait_ge(w3_in, 16)
            pe.wait_ge(ones_set, 1)
            for t in range(NT):
                if t:
                    pe.wait_ge(ab_done, t)
                for j in range(4):
                    mm = nc.tensor.matmul(hp[:, j, :], hid[1][:, t * P:(t + 1) * P], w3[:, j * MIX:(j + 1) * MIX], start=True, stop=True)
                mm.then_inc(h_done, 1)
                if t >= 1:
                    sums(pe, t - 1)
            sums(pe, NT - 1)
            for l in range(2):
                pe.wait_ge(sum_taken, l + 1)
                for j in range(8):
                    mm = nc.tensor.transpose(hp[:, j // 4, (j % 4) * P:(j % 4 + 1) * P], sums_sb[:, j * P:(j + 1) * P], keep.ident[:])
                mm.then_inc(sum_turned, 1)
            pe.wait_ge(taps_done, NT)
            pe.wait_ge(inv_taken, 2)
            pe.wait_ge(cf_in, 64)
            for n, (q, o, cs) in enumerate(jobs):
                if n >= 2:
                    pe.wait_ge(res_done, n - 1)
                pair = [hp[:, 2 * (n % 2), :], hp[:, 2 * (n % 2) + 1, :]]
                if q == 8:
                    mm = nc.tensor.matmul(pair[0], cfp[:, cs, :], taps[:, 8, cs, o * MIX:(o + 1) * MIX], start=True, stop=True)
                else:
                    for par in range(2):
                        for k in range(4):
                            mm = nc.tensor.matmul(pair[par], cf[:, cs, 4 * par + k, q * P:(q + 1) * P],
                                                  taps[:, 4 * par + k, cs, o * MIX:(o + 1) * MIX], start=k == 0, stop=k == 3)
                mm.then_inc(dft_done, 1)

        @blk.scalar
        def _(act):
            act.wait_ge(small_in, 96)
            for layer in range(2):
                nc.scalar.activation(fb[:, layer:layer + 1], cols[:, layer:layer + 1], ACT.Identity, scale=cols[:, 2:3]).then_inc(arg_done, 1)
                act.wait_ge(arg_done, 4 * layer + 1)
                act.wait_ge(hid_mm, layer + 1)
                for i, (at, w) in enumerate(spans):
                    src = (bk + [hp[:, 0, :]])[i]
                    nc.scalar.activation(arg[:, at:at + w], src[0:FW, 0:w], ACT.Identity, bias=fb[:, layer:layer + 1], scale=cols[:, 2:3]).then_inc(arg_done, 1)
                act.wait_ge(red, layer + 1)
                nc.scalar.activation(hid[layer][:], arg[:], ACT.Sin).then_inc(sin_done, 1)
            for t in range(NT):
                act.wait_ge(ab_done, t + 1)
                if t:
                    act.wait_ge(sum_done, t)
                nc.scalar.activation(absA[:], A[:], ACT.Abs)
                nc.scalar.activation(absB[:], B[:], ACT.Abs).then_inc(abs_done, 1)
            for n, (q, o, cs) in enumerate(jobs):
                act.wait_ge(dft_done, n + 1)
                if n >= 2:
                    act.wait_ge(res_done, n - 1)
                nc.scalar.activation(first[:, n % 2, :], hp[:, 2 * (n % 2), :], ACT.Copy).then_inc(first_done, 1)

        @blk.gpsimd
        def _(pool):
            nc.gpsimd.memset(ones[:], 1.0).then_inc(ones_set, 1)
            for t in range(NT):
                pool.wait_ge(abs_done, t + 1)
                nc.gpsimd.tensor_tensor(absA[:], absA[:], absB[:], ALU.add).then_inc(abs_sum, 1)

        def take_sums(dve, l):
            dve.wait_ge(sum_done, NTS + l)
            if l:
                dve.wait_ge(sum_turned, 1)
            nc.vector.tensor_copy(sums_sb[:], sp_[:].rearrange("p o c -> p (o c)")).then_inc(sum_taken, 1)
            dve.wait_ge(sum_turned, l + 1)
            nc.vector.reciprocal(keep.tap_scale[:, l, :], hp[:, 0:2, :].rearrange("p a (b c) -> p (a b) c", c=P)[:, :, 0]).then_inc(inv_taken, 1)

        @blk.vector
        def _(dve):
            link = Link(dve, chain)
            for layer in range(2):
                dve.wait_ge(arg_done, 4 * layer + 4)
                link(nc.vector.tensor_scalar(turns[:], arg[:], 1.0 / SIN_TURN, ROUND, ALU.mult, ALU.add))
                link(nc.vector.tensor_scalar(turns[:], turns[:], ROUND, None, ALU.subtract))
                link(nc.vector.scalar_tensor_tensor(arg[:], turns[:], -TURN_HI, arg[:], ALU.mult, ALU.add))
                link(nc.vector.scalar_tensor_tensor(arg[:], turns[:], -TURN_LO, arg[:], ALU.mult, ALU.add))
                nc.vector.tensor_scalar(arg[:], arg[:], PI_DOWN, -PI_DOWN, ALU.min, ALU.max).then_inc(red, 1)
            dve.wait_ge(win_in, 32)
            for t in range(NT):
                dve.wait_ge(h_done, t + 1)
                if t:
                    dve.wait_ge(abs_done, t)
                wa = win[:, t:t + 1, :].broadcast_to([P, 2, MIX])
                wb = win_b[:, t // NTS:t // NTS + 1, :].broadcast_to([P, 2, MIX]) if t in (0, NTS) else wa
                nc.vector.tensor_tensor(A[:], hp[:, 0:2, :], wa, ALU.mult)
                nc.vector.tensor_tensor(B[:], hp[:, 2:4, :], wb, ALU.mult).then_inc(ab_done, 1)
                dve.wait_ge(ab_done, t + 1)
                a, b = A[:].rearrange("p o c -> p (o c)"), B[:].rearrange("p o c -> p (o c)")
                nc.vector.tensor_tensor(taps[:, t, 0, :], a, b, ALU.add)
                nc.vector.tensor_tensor(taps[:, t, 1, :], a, b, ALU.subtract).then_inc(taps_done, 1)
                dve.wait_ge(taps_done, t + 1)
                if t == NT - 1:
                    take_sums(dve, 0)
            take_sums(dve, 1)
            for n, (q, o, cs) in enumerate(jobs):
                if n >= 2:
                    dve.wait_ge(res_out[n % 2], 16 * sum(1 if j[0] == 8 else 2 for j in jobs[n % 2:n:2]))
                dve.wait_ge(first_done, n + 1)
                f, second = first[:, n % 2, :], hp[:, 2 * (n % 2) + 1, :]
                if q == 8:
                    nc.vector.tensor_copy(res[:, n % 2, 0, :], f).then_inc(res_done, 1)
                    continue
                nc.vector.tensor_tensor(res[:, n % 2, 0, :], second, f, ALU.add)
                if cs == 0:
                    nc.vector.tensor_tensor(res[:, n % 2, 1, :], f, second, ALU.subtract).then_inc(res_done, 1)
                else:
                    nc.vector.tensor_tensor(res[:, n % 2, 1, :], second, f, ALU.subtract).then_inc(res_done, 1)



class Signal:

    def __init__(self, i):
        self.i = i
        self.L = (TS, TP)[i]
        self.at = (0, TS)[i]
        self.half = self.L // 2
        self.rows = min(self.half, P)
        self.nt = self.half // self.rows
        self.ft = self.L // P
        self.spec0 = (0, NTS)[i]


def hyena_signals(nc, io, keep):
    NCH = MIX // P
    sigs = [Signal(0), Signal(1)]
    runs = [(g, o) for g in sigs for o in range(2)]
    with Stage(nc, "hyena") as s:
        u_of = [s.sb("u", [P, NCH, TS]), s.sb("u_prompt", [P, NCH, TP])]
        gate = s.sb("gate", [P, 2, TS])
        eo = s.sb("eo", [P, NCH, 2, TS // 2])
        eoT = s.sb("eoT", [P, 4, 2, MIX])
        fwd = s.sb("fwd", [P, 2, 4, TS])
        bwd = s.sb("bwd", [P, 2, 8, TS // 2])
        fwd_p = s.sb("fwd_p", [64, 2, P])
        bwd_p = s.sb("bwd_p", [P, 2, 64])
        spec = [s.sb(f"spec{i}", [P, 2, MIX]) for i in range(2)]
        prod = s.sb("prod", [P, 2, 2, MIX])
        Y = s.sb("Y", [P, 8, 2, MIX])
        odd = s.sb("odd", [P, 2, TS // 2])
        conv = s.sb("conv", [P, TS])
        skip = s.sb("skip", [P, 2, NCH])
        bk = [s.ps(f"b{i}", [P, BANK]) for i in range(8)]
        u_in = [s.sem(f"u_in{i}") for i in range(2)]
        fwd_in, bwd_in = s.sem("fwd_in"), s.sem("bwd_in")
        spec_in = [s.sem(f"spec_in{i}") for i in range(2)]
        gate_in = [s.sem(f"gate_in{i}") for i in range(2)]
        folded, turned, turn_taken, dft_done, prod_done, y_done, inv_done, odd_done, conv_done, u_done = (
            s.sem(n) for n in ("folded", "turned", "turn_taken", "dft_done", "prod_done", "y_done", "inv_done", "odd_done", "conv_step", "u_done"))
        u_out = s.sem("u_out")
        blk = s.block()
        FT = [g.ft for g, _ in runs]
        NTN = [g.nt for g, _ in runs]
        ft0 = [sum(FT[:r]) for r in range(5)]
        nt0 = [2 * sum(NTN[:r]) for r in range(5)]

        @blk.sync
        def _(sp):
            for c in range(NCH):
                sp.dma_start(u_of[0][:, c, :], io["conv"][0][c * P:(c + 1) * P, 0:TS]).then_inc(u_in[0], 16)
            for i in range(2):
                sp.dma_start(fwd[:, i], io["sig_dft"][i].rearrange("(t p) f -> p t f", p=P)).then_inc(fwd_in, 16)
                sp.dma_start(fwd_p[:, i], io["sig_dft_p"][i]).then_inc(fwd_in, 16)
            for r, (g, o) in enumerate(runs):
                for f in range(g.ft):
                    n = ft0[r] + f
                    if n == 2:
                        for c in range(NCH):
                            sp.dma_start(u_of[1][:, c, :], io["conv"][0][c * P:(c + 1) * P, TS:T]).then_inc(u_in[1], 16)
                        for i in range(2):
                            sp.dma_start(bwd_p[:, i], io["sig_idft_p"][i]).then_inc(bwd_in, 16)
                            sp.dma_start(bwd[:, i], io["sig_idft"][i].rearrange("(t p) n -> p t n", p=P)).then_inc(bwd_in, 16)
                            sp.dma_start(skip[:, i], io["hy_skip"][0, i].rearrange("(c p) -> p c", p=P), allow_slow_non_contiguous=True).then_inc(bwd_in, 16)
                    if n >= 2:
                        sp.wait_ge(prod_done, 2 * (n - 1))
                    sp.dma_start(spec[n % 2][:], io["spec"][g.spec0 + f, :, o]).then_inc(spec_in[n % 2], 16)
                for c in range(NCH):
                    n = r * NCH + c
                    if n >= 2:
                        sp.wait_ge(u_done, n - 1)
                    row = MIX * (1 + o) + c * P
                    sp.dma_start(gate[:, n % 2, 0:g.L], io["conv"][0][row:row + P, g.at:g.at + g.L]).then_inc(gate_in[n % 2], 16)
                    if o == 1:
                        sp.wait_ge(u_done, n + 1)
                        sp.dma_start(io["mixT"][0][MIX + c * P:MIX + (c + 1) * P, g.at:g.at + g.L], u_of[g.i][:, c, :]).then_inc(u_out, 16)
            sp.wait_ge(u_out, 32 * NCH)

        def pair(n):
            return (bk[6], bk[7]) if n % 2 == 0 else (bk[4], bk[5])

        def ready(dve, r):
            if r % 2 == 0:
                dve.wait_ge(u_in[r // 2], 16 * NCH)
            else:
                dve.wait_ge(u_done, NCH * r)

        @blk.tensor
        def _(pe):
            for r, (g, o) in enumerate(runs):
                fm, bm = (fwd, bwd) if g.i == 0 else (fwd_p, bwd_p)
                pe.wait_ge(folded, NCH * (r + 1))
                if r:
                    pe.wait_ge(odd_done, NCH * r)
                    pe.wait_ge(u_done, NCH * r)
                for t in range(g.nt):
                    for part in range(2):
                        n = nt0[r] + 2 * t + part
                        if n >= 2:
                            pe.wait_ge(turn_taken, n - 1)
                        for c in range(NCH):
                            mm = nc.tensor.transpose(bk[n % 2][0:g.rows, c * P:(c + 1) * P], eo[:, c, part, t * g.rows:(t + 1) * g.rows], keep.ident[:])
                        mm.then_inc(turned, 1)
                pe.wait_ge(turn_taken, nt0[r + 1])
                if r == 0:
                    pe.wait_ge(fwd_in, 64)
                for f in range(g.ft):
                    n = ft0[r] + f
                    if n >= 2:
                        pe.wait_ge(prod_done, 2 * (n - 1))
                    for cs in range(2):
                        for t in range(g.nt):
                            lhs = fm[:, cs, t, f * P:(f + 1) * P] if g.i == 0 else fm[:, cs, :]
                            mm = nc.tensor.matmul(bk[2 + 2 * (n % 2) + cs][:], lhs, eoT[0:g.rows, t, cs, :], start=t == 0, stop=t == g.nt - 1)
                    mm.then_inc(dft_done, 1)
                pe.wait_ge(y_done, 2 * ft0[r + 1])
                if r == 0:
                    pe.wait_ge(bwd_in, 96)
                for c in range(NCH):
                    n = r * NCH + c
                    if n >= 2:
                        pe.wait_ge(conv_done, 3 * (n - 1) - 1)
                    for cs in range(2):
                        for f in range(g.ft):
                            rhs = bm[:, cs, f, :] if g.i == 0 else bm[:, cs, :]
                            mm = nc.tensor.matmul(pair(n)[cs][:, 0:g.half], Y[:, f, cs, c * P:(c + 1) * P], rhs, start=f == 0, stop=f == g.ft - 1)
                    mm.then_inc(inv_done, 1)

        @blk.scalar
        def _(act):
            for r, (g, o) in enumerate(runs):
                for n in range(nt0[r], nt0[r + 1]):
                    t, part = divmod(n - nt0[r], 2)
                    act.wait_ge(turned, n + 1)
                    if r:
                        act.wait_ge(dft_done, ft0[r])
                    nc.scalar.activation(eoT[0:g.rows, t, part, :], bk[n % 2][0:g.rows, :], ACT.Copy).then_inc(turn_taken, 1)
                for c in range(NCH):
                    n = r * NCH + c
                    act.wait_ge(inv_done, n + 1)
                    if n >= 2:
                        act.wait_ge(conv_done, 3 * (n - 1) - 1)
                    at = 4 * o + c
                    nc.scalar.activation(odd[:, n % 2, 0:g.half], pair(n)[1][:, 0:g.half], ACT.Copy, scale=keep.tap_scale[:, g.i, at:at + 1]).then_inc(odd_done, 1)

        @blk.vector
        def _(dve):
            for r, (g, o) in enumerate(runs):
                h, u = g.half, u_of[g.i]
                ready(dve, r)
                if r:
                    dve.wait_ge(turned, nt0[r])
                for c in range(NCH):
                    later, earlier = u[:, c, h:2 * h], u[:, c, h - 1::-1]
                    nc.vector.tensor_tensor(eo[:, c, 0, 0:h], later, earlier, ALU.add)
                    nc.vector.tensor_tensor(eo[:, c, 1, 0:h], later, earlier, ALU.subtract).then_inc(folded, 1)
                for f in range(g.ft):
                    n = ft0[r] + f
                    dve.wait_ge(dft_done, n + 1)
                    dve.wait_ge(spec_in[n % 2], 16 * (n // 2 + 1))
                    if n >= 1:
                        dve.wait_ge(y_done, 2 * n)
                    uc, us = bk[2 + 2 * (n % 2)], bk[3 + 2 * (n % 2)]
                    hc, hs = spec[n % 2][:, 0, :], spec[n % 2][:, 1, :]
                    nc.vector.tensor_tensor(prod[:, 0, 0, :], uc[:], hc, ALU.mult)
                    nc.vector.tensor_tensor(prod[:, 0, 1, :], us[:], hs, ALU.mult).then_inc(prod_done, 1)
                    nc.vector.tensor_tensor(prod[:, 1, 0, :], uc[:], hs, ALU.mult)
                    nc.vector.tensor_tensor(prod[:, 1, 1, :], us[:], hc, ALU.mult).then_inc(prod_done, 1)
                for c in range(NCH):
                    n = r * NCH + c
                    at = 4 * o + c
                    scale = keep.tap_scale[:, g.i, at:at + 1]
                    dve.wait_ge(odd_done, n + 1)
                    nc.vector.scalar_tensor_tensor(conv[:, h:2 * h], pair(n)[0][:, 0:h], scale, odd[:, n % 2, 0:h], ALU.mult, ALU.add).then_inc(conv_done, 1)
                    nc.vector.scalar_tensor_tensor(conv[:, h - 1::-1], pair(n)[0][:, 0:h], scale, odd[:, n % 2, 0:h], ALU.mult, ALU.subtract).then_inc(conv_done, 1)
                    dve.wait_ge(conv_done, 3 * n + 2)
                    nc.vector.scalar_tensor_tensor(conv[:, 0:g.L], u[:, c, 0:g.L], skip[:, o, c:c + 1], conv[:, 0:g.L], ALU.mult, ALU.add).then_inc(conv_done, 1)
                    dve.wait_ge(conv_done, 3 * n + 3)
                    dve.wait_ge(gate_in[n % 2], 16 * (n // 2 + 1))
                    nc.vector.tensor_tensor(u[:, c, 0:g.L], conv[:, 0:g.L], gate[:, n % 2, 0:g.L], ALU.mult).then_inc(u_done, 1)
                    dve.wait_ge(u_done, n + 1)

        @blk.gpsimd
        def _(pool):
            for r, (g, o) in enumerate(runs):
                if r:
                    pool.wait_ge(inv_done, NCH * r)
                for f in range(g.ft):
                    n = ft0[r] + f
                    pool.wait_ge(prod_done, 2 * n + 1)
                    nc.gpsimd.tensor_tensor(Y[:, f, 0, :], prod[:, 0, 0, :], prod[:, 0, 1, :], ALU.subtract).then_inc(y_done, 1)
                    pool.wait_ge(prod_done, 2 * n + 2)
                    nc.gpsimd.tensor_tensor(Y[:, f, 1, :], prod[:, 1, 0, :], prod[:, 1, 1, :], ALU.add).then_inc(y_done, 1)



def expert_buffers(wall):
    return [wall[:, i * KD * D:(i + 1) * KD * D].rearrange("p (k n) -> p k n", n=D) for i in range(3)]


def mix_out(nc, io, keep, l, wall):
    w = io["even_w_out" if l == 0 else "odd_w_out"][0].rearrange("(k p) n -> p k n", p=P)
    with Stage(nc, f"out{l}") as s:
        x = s.sb("x", [P, NT, D])
        hT = s.sb("hT", [P, KD, T])
        mixT = wall[:, 0:KD * T].rearrange("p (k t) -> p k t", t=T)
        wo = wall[:, KD * T:KD * (T + D)].rearrange("p (k n) -> p k n", n=D)
        gate = s.sb("gate", [P, 2, D])
        tmp = s.sb("tmp", [P, D])
        wr = s.sb("wr", [P, KD, E])
        logT = s.sb("logT", [E, T])
        lg = s.sb("lg", [P, NT, E])
        red = s.sb("red", [P, 2, NT])
        HALF = TS // 2
        LATE = 32
        aff = s.sb("aff", [LATE + E, HALF])
        affp = s.sb("affp", [E, TP])
        best = s.sb("best", [LATE + E, CAP_S])
        place = s.sb("place", [LATE + E, CAP_S], U32)
        placep = s.sb("placep", [E, CAP_P], U32)
        late = s.sb("late", [E, 2, CAP_S])
        early = s.sb("early", [E, CAP_S])
        top = s.sb("top", [E, SLOTS])
        idxf = s.sb("idxf", [E, SLOTS])
        norm = Norm(s, nc, keep, l, 1, x, hT)
        acc = [s.ps(f"acc{i}", [P, 2, BANK]) for i in range(2)]
        rt = [s.ps(f"rt{i}", [P, BANK]) for i in range(2)]
        x_in = [s.sem(f"x_in{t}") for t in range(NT)]
        mix_in, wo_in, w_in = [s.sem(f"mix_in{t}") for t in range(NT)], [s.sem(f"wo_in{h}") for h in range(2)], s.sem("w_in")
        gate_in, wr_in = s.sem("gate_in"), s.sem("wr_in")
        acc_done, gated, x_done, xn_out = s.sem("acc_done"), s.sem("gated"), s.sem("x_done"), s.sem("xn_out")
        x_out = [s.sem(f"x_out{g}") for g in range(3)]
        log_done, log_taken, log_turned, soft, prob_done, aff_turned, aff_done, top_step, top_done, slots_turned = (
            s.sem(n) for n in ("log_done", "log_taken", "log_turned", "soft_step", "prob_done", "aff_turned", "aff_done", "top_step", "top_done", "slots_turned"))
        shifted, exp_done = s.sem("shifted"), s.sem("exp_done")
        blk = s.block()

        TG = T // 3

        def router_bank(n):
            return (rt[0], rt[1], acc[0][:, 0, :])[n][32 * n:32 * n + E, 0:TG]

        def load_mix(sp, t):
            at = slice(t * P, (t + 1) * P)
            sp.dma_start(mixT[:, :, at], io["mixT"][l].rearrange("(k p) t -> p k t", p=P)[:, :, at]).then_inc(mix_in[t], 16)

        @blk.sync
        def _(sp):
            for h in range(2):
                sp.dma_start(wo[:, :, h * BANK:(h + 1) * BANK], w[:, :, h * BANK:(h + 1) * BANK]).then_inc(wo_in[h], 16)
                if h == 0:
                    load_mix(sp, 0)
            for c in range(2):
                sp.dma_start(gate[:, c, :], all_rows(io["mrow"][l, c, 2 * D:3 * D])).then_inc(gate_in, 16)
            for t in range(NT):
                load_x(sp, io, x, x_in, io["x_of"][l], t)
                if t + 1 < NT:
                    load_mix(sp, t + 1)
            sp.dma_start(wr[:], io["moe_router"][l].rearrange("(k p) e -> p k e", p=P)).then_inc(wr_in, 16)
            for t in range(NT):
                sp.wait_ge(x_done, t + 1)
                sp.dma_start(io["x"][l][t * P:(t + 1) * P, :], x[:, t, :]).then_inc(x_out[t // 4], 16)
            sp.wait_ge(acc_done, NT)
            for buf, name in zip(expert_buffers(wall), ("moe_w_gate", "moe_w_up", "moe_w_down")):
                sp.dma_start(buf, io[name][l, 0].rearrange("(k p) n -> p k n", p=P)).then_inc(w_in, 16)
            for t in range(NT):
                sp.wait_ge(norm.scaled, t + 1)
                sp.dma_start(io["xn"][t * P:(t + 1) * P, :], x[:, t, :]).then_inc(xn_out, 16)
            sp.wait_ge(xn_out, 16 * NT)
            sp.wait_ge(w_in, 48)

        @blk.tensor
        def _(pe):
            for t in range(NT):
                pe.wait_ge(mix_in[t], 16)
                if t >= 2:
                    pe.wait_ge(gated, t - 1)
                for h in range(2):
                    if t == 0:
                        pe.wait_ge(wo_in[h], 16)
                    for k in range(KD):
                        mm = nc.tensor.matmul(acc[t % 2][:, h, :], mixT[:, k, t * P:(t + 1) * P], wo[:, k, h * BANK:(h + 1) * BANK],
                                              start=k == 0, stop=k == KD - 1)
                mm.then_inc(acc_done, 1)
            norm.tensor(pe)
            pe.wait_ge(wr_in, 16)
            pe.wait_ge(norm.taken, norm.TURNS)
            for k in range(KD):
                for n in range(3):
                    mm = nc.tensor.matmul(router_bank(n), wr[:, k, :], hT[:, k, n * TG:(n + 1) * TG],
                                          start=k == 0, stop=k == KD - 1, tile_position=(0, 32 * n))
                    if k == KD - 1:
                        mm.then_inc(log_done, 1)
            pe.wait_ge(log_taken, 3)
            for t in range(NT):
                mm = nc.tensor.transpose(rt[1][:, t * E:(t + 1) * E], logT[:, t * P:(t + 1) * P], keep.ident[0:E, 0:E])
            mm.then_inc(log_turned, 1)
            pe.wait_ge(prob_done, 1)
            for t in range(NT):
                dst = acc[0][0:E, t // 4, (t % 4) * P:(t % 4 + 1) * P] if t < 8 else acc[1][0:E, 0, 0:P]
                mm = nc.tensor.transpose(dst, lg[:, t, :], keep.ident[:])
            mm.then_inc(aff_turned, 1)
            pe.wait_ge(top_done, 1)
            for n, src in enumerate((idxf, top)):
                nc.tensor.transpose(rt[0][:, n * E:(n + 1) * E], src[:, 0:CAP_S], keep.ident[0:E, 0:E])
                mm = nc.tensor.transpose(rt[1][0:CAP_P, n * E:(n + 1) * E], src[:, CAP_S:SLOTS], keep.ident[0:E, 0:E])
            mm.then_inc(slots_turned, 1)

        @blk.scalar
        def _(act):
            norm.scalar(act, lambda eng, t: eng.wait_ge(x_done, t + 1))
            act.wait_ge(log_done, 3)
            for n in range(3):
                nc.scalar.activation(logT[:, n * TG:(n + 1) * TG], router_bank(n), ACT.Copy).then_inc(log_taken, 1)
            act.wait_ge(shifted, 1)
            nc.scalar.activation(lg[:], lg[:], ACT.Exp).then_inc(exp_done, 1)

        @blk.vector
        def _(dve):
            norm.vector_eps()
            dve.wait_ge(gate_in, 32)

            def scale(g):
                dve.wait_ge(x_out[g], 16 * (1 if g == 2 else 4))
                norm.vector_scale(dve, g)

            for t in range(NT):
                dve.wait_ge(acc_done, t + 1)
                nc.vector.tensor_tensor(tmp[:], acc[t % 2][:].rearrange("p h n -> p (h n)"), gate[:, t // NTS, :], ALU.mult).then_inc(gated, 1)
                dve.wait_ge(gated, t + 1)
                dve.wait_ge(x_in[t], 16)
                nc.vector.tensor_tensor(x[:, t, :], x[:, t, :], tmp[:], ALU.add).then_inc(x_done, 1)
                dve.wait_ge(x_done, t + 1)
                if t in (6, 7):
                    scale(t - 6)
            norm.vector_turn(dve, slice(0, 2))
            scale(2)
            norm.vector_turn(dve, slice(2, 3))
            link = Link(dve, soft)
            dve.wait_ge(log_turned, 1)
            logits = rt[1][:, 0:NT * E].rearrange("p (t e) -> p t e", e=E)
            link(nc.vector.tensor_reduce(red[:, 0, :], logits, axis=AX.X, op=ALU.max))
            nc.vector.tensor_tensor(lg[:], logits, red[:, 0, :].unsqueeze(2).broadcast_to([P, NT, E]), ALU.subtract).then_inc(shifted, 1)
            dve.wait_ge(shifted, 1)
            dve.wait_ge(exp_done, 1)
            link(nc.vector.tensor_reduce(red[:, 0, :], lg[:], axis=AX.X, op=ALU.add))
            link(nc.vector.reciprocal(red[:, 1, :], red[:, 0, :]))
            nc.vector.tensor_tensor(lg[:], lg[:], red[:, 1, :].unsqueeze(2).broadcast_to([P, NT, E]), ALU.mult).then_inc(prob_done, 1)
            dve.wait_ge(aff_turned, 1)
            link(nc.vector.memset(aff[:], 0.0))
            for h in range(2):
                nc.vector.tensor_copy(aff[LATE * h:LATE * h + E, :], acc[0][0:E, h, :])
            nc.vector.tensor_copy(affp[:], acc[1][0:E, 0, 0:P]).then_inc(aff_done, 1)
            dve.wait_ge(aff_done, 1)
            step = Link(dve, top_step)
            for n in range(SLOTS // 8):
                sample = n < CAP_S // 8
                eight = slice(8 * n, 8 * n + 8) if sample else slice(8 * n - CAP_S, 8 * n - CAP_S + 8)
                row, val, at = (aff[:], best[:, eight], place[:, eight]) if sample else (affp[:], top[:, 8 * n:8 * n + 8], placep[:, eight])
                step(nc.vector.max(val, row))
                nc.vector.max_index(at, val, row)
                step(nc.vector.match_replace(row, val, row, -1.0))
            step(nc.vector.tensor_copy(late[:, 0, :], best[LATE:LATE + E, CAP_S - 1::-1]))
            step(nc.vector.tensor_copy(late[:, 1, :], place[LATE:LATE + E, CAP_S - 1::-1]))
            step(nc.vector.tensor_scalar(late[:, 1, :], late[:, 1, :], float(HALF), None, ALU.add))
            step(nc.vector.tensor_copy(idxf[:, 0:CAP_S], place[0:E, :]))
            step(nc.vector.tensor_tensor(early[:], best[0:E, :], late[:, 0, :], ALU.is_ge))
            step(nc.vector.tensor_tensor(idxf[:, 0:CAP_S], idxf[:, 0:CAP_S], late[:, 1, :], ALU.subtract))
            step(nc.vector.tensor_tensor(idxf[:, 0:CAP_S], idxf[:, 0:CAP_S], early[:], ALU.mult))
            nc.vector.tensor_tensor(idxf[:, 0:CAP_S], idxf[:, 0:CAP_S], late[:, 1, :], ALU.add)
            nc.vector.tensor_tensor(top[:, 0:CAP_S], best[0:E, :], late[:, 0, :], ALU.max)
            step(nc.vector.tensor_copy(idxf[:, CAP_S:SLOTS], placep[:]))
            nc.vector.tensor_scalar(idxf[:, CAP_S:SLOTS], idxf[:, CAP_S:SLOTS], float(TS), None, ALU.add).then_inc(top_done, 1)
            dve.wait_ge(slots_turned, 1)
            for dst, src, rows in ((keep.slot_s, rt[0], CAP_S), (keep.slot_p, rt[1], CAP_P)):
                nc.vector.tensor_copy(dst[0:rows, 0:E], src[0:rows, 0:E])
                nc.vector.tensor_copy(dst[0:rows, E:E + 1], src[0:rows, 0:1])
            nc.vector.tensor_copy(keep.gate_s[:], rt[0][:, E:2 * E])
            nc.vector.tensor_copy(keep.gate_p[0:CAP_P, :], rt[1][0:CAP_P, E:2 * E])


def experts(nc, io, keep, l, wall):
    FC = D // P
    weights = [io[n][l] for n in ("moe_w_gate", "moe_w_up", "moe_w_down")]
    with Stage(nc, f"moe{l}") as s:
        w = expert_buffers(wall)
        xg = [s.sb(f"xg{i}", [P, D]) for i in range(2)]
        xgp = [s.sb(f"xgp{i}", [CAP_P, D]) for i in range(2)]
        slot = [s.sb(f"slot{i}", [P, 1], U32) for i in range(2)]
        slotp = [s.sb(f"slotp{i}", [CAP_P, 1], U32) for i in range(2)]
        xT = s.sb("xT", [P, KD, SLOTS])
        sg = s.sb("sg", [P, FC, SLOTS])
        gu = s.sb("gu", [P, FC, SLOTS])
        yT = s.sb("yT", [P, KD, SLOTS])
        ys = [s.sb(f"ys{i}", [P, D]) for i in range(2)]
        yp = [s.sb(f"yp{i}", [CAP_P, D]) for i in range(2)]
        rowg = s.sb("rowg", [P, 2, D])
        bk = [s.ps(f"b{i}", [P, BANK]) for i in range(3)]
        bx = [s.ps(f"x{i}", [P, BANK]) for i in range(2)]
        by = [s.ps(f"y{i}", [P, BANK]) for i in range(2)]
        byp = s.ps("yp", [P, BANK])
        w_in = [s.sem(f"w_in{i}") for i in range(3)]
        g_mm, u_mm, d_mm = s.sem("g_mm"), s.sem("u_mm"), s.sem("d_mm")
        mm_sems = (g_mm, u_mm, d_mm)
        sg_done, gu_done, yT_done = s.sem("sg_done"), s.sem("gu_done"), s.sem("yT_done")
        slot_set = s.sem("slot_set")
        xg_in = [s.pool_dma_sem(f"xg_in{i}") for i in range(2)]
        x_turned, xT_done = s.sem("x_turned"), s.sem("xT_done")
        y_turned, yp_turned, ys_done, yp_done = s.sem("y_turned"), s.sem("yp_turned"), s.sem("ys_done"), s.sem("yp_done")
        row_in, fetching, results_free = s.sem("row_in"), s.sem("fetching"), s.sem("results_free")
        added = [s.pool_dma_sem(f"added{i}") for i in range(2)]
        blk = s.block()

        @blk.sync
        def _(sp):
            for c in range(2):
                sp.dma_start(rowg[:, c, :], all_rows(io["mrow"][l, c, 5 * D:6 * D])).then_inc(row_in, 16)
            with sp.Fori(0, E - 1) as e:
                for i in range(3):
                    sp.wait_ge(mm_sems[i], e * FC + 2 * FC)
                    sp.dma_start(w[i][:], weights[i][bass.ds(e + 1, 1)].rearrange("o (k p) n -> p (o k) n", p=P)).then_inc(w_in[i], 16)

        def set_slots(pool, e, par):
            nc.gpsimd.tensor_copy(slot[par][:], keep.slot_s[:, bass.ds(e, 1)])
            nc.gpsimd.tensor_copy(slotp[par][:], keep.slot_p[0:CAP_P, bass.ds(e, 1)]).then_inc(slot_set, 1)

        def fetch(pool, par):
            for dst, sl in ((xg, slot), (xgp, slotp)):
                nc.gpsimd.indirect_dma_start(out=dst[par][:], out_offset=None, in_=io["xn"],
                                             in_offset=bass.IndirectOffsetOnAxis(ap=sl[par][:, 0:1], axis=0)).then_inc(xg_in[par], 16)

        def add_back(pool, par):
            for src, sl in ((ys, slot), (yp, slotp)):
                nc.gpsimd.indirect_dma_start(out=io["x"][l], out_offset=bass.IndirectOffsetOnAxis(ap=sl[par][:, 0:1], axis=0),
                                             in_=src[par][:], in_offset=None, compute_op=ALU.add).then_inc(added[par], 16)

        @blk.gpsimd
        def _(pool):
            pool.sem_inc(results_free, 2)
            set_slots(pool, 0, 0)
            pool.wait_ge(slot_set, 1)
            fetch(pool, 0)
            with pool.Fori(0, E // 2) as i:
                for j in range(2):
                    set_slots(pool, i * 2 + (j + 1), 1 - j)
                    pool.wait_ge(slot_set, i * 2 + (j + 2))
                    pool.wait_ge(x_turned, i * (2 * KD) + (j + 1) * KD)
                    pool.sem_inc(fetching, 1)
                    fetch(pool, 1 - j)
                    pool.wait_ge(ys_done, i * 4 + (2 * j + 4))
                    pool.wait_ge(yp_done, i * 4 + (2 * j + 3))
                    pool.sem_inc(fetching, 1)
                    add_back(pool, j)
                    pool.wait_ge(added[j], i * 32 + 32)
                    pool.sem_inc(results_free, 1)
            pool.wait_ge(xg_in[0], 32 * (E // 2 + 1))

        def turn_tokens(pe, par, base):
            for k in range(KD):
                pe.wait_ge(xT_done, base + (k + 1))
                nc.tensor.transpose(bx[k % 2][:, 0:CAP_S], xg[par][:, k * P:(k + 1) * P], keep.ident[:])
                nc.tensor.transpose(bx[k % 2][:, CAP_S:SLOTS], xgp[par][:, k * P:(k + 1) * P],
                                    keep.ident[0:CAP_P, 0:CAP_P]).then_inc(x_turned, 1)

        def turn_results(pe, i, j, f, e8):
            h, q = divmod(f, 4)
            if q == 0:
                pe.wait_ge(ys_done, i * 4 + (2 * j + h + 1))
                pe.wait_ge(yp_done, i * 4 + (2 * j + h + 1))
            pe.wait_ge(yT_done, e8(FC + f + 1))
            ms = nc.tensor.transpose(by[h][:, q * P:(q + 1) * P], yT[:, f, 0:CAP_S], keep.ident[:])
            if q == 3:
                ms.then_inc(y_turned, 1)
            mp = nc.tensor.transpose(byp[0:CAP_P, q * P:(q + 1) * P], yT[:, f, CAP_S:SLOTS], keep.ident[:])
            if q == 3:
                mp.then_inc(yp_turned, 1)

        @blk.tensor
        def _(pe):
            for q, n in ((w_in[0], 16), (w_in[1], 16), (w_in[2], 16), (g_mm, FC), (u_mm, FC), (d_mm, FC), (yT_done, FC), (xT_done, 2), (ys_done, 2), (yp_done, 1)):
                pe.sem_inc(q, n)
            pe.wait_ge(xg_in[0], 32)
            turn_tokens(pe, 0, 0)
            with pe.Fori(0, E // 2) as i:
                for j in range(2):
                    e8 = lambda n: i * (2 * FC) + (j * FC + n)

                    def bank_free(c):
                        b = c - 3
                        if b < 0:
                            pe.wait_ge(yT_done, e8(FC + 1 + b))
                        elif b < FC:
                            pe.wait_ge(sg_done, e8(b + 1))
                        elif b < 2 * FC:
                            pe.wait_ge(gu_done, e8(b - FC + 1))
                        else:
                            pe.wait_ge(yT_done, e8(FC + b - 2 * FC + 1))

                    pe.wait_ge(xT_done, e8(FC + 2))
                    for m in range(3):
                        pe.wait_ge(w_in[m], i * 32 + 16 * (j + 1))
                        if m == 2:
                            pe.wait_ge(xg_in[1 - j], i * 32 + 32 * (j + 1))
                            turn_tokens(pe, 1 - j, e8(FC))
                            pe.wait_ge(gu_done, e8(FC))
                        for f in range(FC):
                            c = m * FC + f
                            bank_free(c)
                            src = gu if m == 2 else xT
                            for k in range(KD):
                                mm = nc.tensor.matmul(bk[c % 3][:, 0:SLOTS], w[m][:, k, f * P:(f + 1) * P], src[:, k, :],
                                                      start=k == 0, stop=k == KD - 1)
                            mm.then_inc(mm_sems[m], 1)
                            if m == 2 and f >= 2:
                                turn_results(pe, i, j, f - 2, e8)
                    for f in (FC - 2, FC - 1):
                        turn_results(pe, i, j, f, e8)

        @blk.scalar
        def _(act):
            with act.Fori(0, E // 2) as i:
                for j in range(2):
                    for f in range(FC):
                        act.wait_ge(g_mm, i * (2 * FC) + ((j + 1) * FC + f + 1))
                        nc.scalar.activation(sg[:, f, :], bk[f % 3][:, 0:SLOTS], ACT.Silu).then_inc(sg_done, 1)
                    for f in range(FC):
                        act.wait_ge(d_mm, i * (2 * FC) + ((j + 1) * FC + f + 1))
                        nc.scalar.activation(yT[:, f, :], bk[(2 * FC + f) % 3][:, 0:SLOTS], ACT.Copy).then_inc(yT_done, 1)

        def take_tokens(dve, base):
            for k in range(KD):
                dve.wait_ge(x_turned, base + (k + 1))
                for c, cols in ((0, slice(0, CAP_S)), (1, slice(CAP_S, SLOTS))):
                    co = keep.coef[:, l, 1, c]
                    ins = nc.vector.tensor_scalar(xT[:, k, cols], bx[k % 2][:, cols], co[:, 0, k:k + 1], co[:, 1, k:k + 1], ALU.mult, ALU.add)
                ins.then_inc(xT_done, 1)

        @blk.vector
        def _(dve):
            dve.wait_ge(row_in, 32)
            take_tokens(dve, 0)
            with dve.Fori(0, E // 2) as i:
                for j in range(2):
                    for f in range(FC):
                        dve.wait_ge(u_mm, i * (2 * FC) + ((j + 1) * FC + f + 1))
                        dve.wait_ge(sg_done, i * (2 * FC) + (j * FC + f + 1))
                        nc.vector.tensor_tensor(gu[:, f, :], sg[:, f, :], bk[(FC + f) % 3][:, 0:SLOTS], ALU.mult).then_inc(gu_done, 1)
                    take_tokens(dve, i * (2 * KD) + (j + 1) * KD)
                    dve.wait_ge(results_free, i * 2 + (j + 1))
                    for h in range(2):
                        half = slice(h * BANK, (h + 1) * BANK)
                        dve.wait_ge(y_turned, i * 4 + (2 * j + h + 1))
                        nc.vector.scalar_tensor_tensor(ys[j][:, half], by[h][:], keep.gate_s[:, bass.ds(i * 2 + j, 1)], rowg[:, 0, half],
                                                       ALU.mult, ALU.mult).then_inc(ys_done, 1)
                        dve.wait_ge(yp_turned, i * 4 + (2 * j + h + 1))
                        nc.vector.scalar_tensor_tensor(yp[j][:, half], byp[0:CAP_P, :], keep.gate_p[0:CAP_P, bass.ds(i * 2 + j, 1)],
                                                       rowg[0:CAP_P, 1, half], ALU.mult, ALU.mult).then_inc(yp_done, 1)


def mix_and_experts(nc, io, keep, l):
    with Stage(nc, f"ffn{l}") as s:
        wall = s.sb("w", [P, 3 * KD * D])
        mix_out(nc, io, keep, l, wall)
        experts(nc, io, keep, l, wall)


def final_norm(nc, io, keep):
    with Stage(nc, "final") as s:
        x = s.sb("x", [P, NT, D])
        gain = s.sb("gain", [P, D])
        norm = Norm(s, nc, keep, 0, 0, x, None)
        x_in = [s.sem(f"x_in{t}") for t in range(NT)]
        gain_in, y_done, y_out = s.sem("gain_in"), s.sem("y_done"), s.sem("y_out")
        blk = s.block()

        @blk.sync
        def _(sp):
            load_x(sp, io, x, x_in, {"x": io["x"][1]})
            sp.dma_start(gain[:], all_rows(io["norm_final"])).then_inc(gain_in, 16)
            for t in range(NT):
                sp.wait_ge(y_done, t + 1)
                dst = io["y_sample"][0, t * P:(t + 1) * P, :] if t < NTS else io["y_prompt"][0]
                sp.dma_start(dst, x[:, t, :]).then_inc(y_out, 16)
            sp.wait_ge(y_out, 16 * NT)

        @blk.scalar
        def _(act):
            norm.scalar(act, lambda eng, t: eng.wait_ge(x_in[t], 16))

        @blk.vector
        def _(dve):
            norm.vector_eps()
            dve.wait_ge(gain_in, 16)
            for g, (at, width, _) in enumerate(token_groups()):
                norm.vector_scale(dve, g)
                for t in range(at // P, (at + width) // P):
                    dve.wait_ge(norm.scaled, t + 1)
                    nc.vector.tensor_tensor(x[:, t, :], x[:, t, :], gain[:], ALU.mult).then_inc(y_done, 1)



HEADS = 8
LEVELS = 7


def delta_net(nc, io, keep):
    with Stage(nc, "gdn") as s:
        m = {}
        m["kv"] = s.sb("kv", [P, NT, 2, MIX])
        m["QT"] = s.sb("QT", [P, 4, T])
        m["KT"] = s.sb("KT", [P, 4, T])
        for n in ("beta", "g", "gc", "egc", "begc"):
            m[n] = s.sb(n, [P, NT, 2, HEADS])
        m["incl"] = s.sb("incl", [P, 2, P])
        m["joins"] = s.sb("joins", [P, LEVELS, 2, P])
        m["S"] = s.sb("S", [P, 4, 4, P])
        delta_prepare(nc, io, keep, m)
        m["o"] = s.sb("o", [P, NT, MIX])
        delta_chunks(nc, io, keep, m)
        delta_outputs(nc, io, keep, m)


def delta_prepare(nc, io, keep, m):
    kv, QT, KT, beta, g, gc, egc, begc, incl, S = (m[x] for x in ("kv", "QT", "KT", "beta", "g", "gc", "egc", "begc", "incl", "S"))
    with Stage(nc, "gdnp") as s:
        zc = s.sb("zc", [P, CC, T])
        q = s.sb("q", [P, NT, MIX])
        sq = s.sb("sq", [P, 2, MIX])
        ss = s.sb("ss", [P, NT, 2, HEADS])
        ab = s.sb("ab", [P, NT, 4, HEADS])
        a_log = s.sb("a_log", [P, 2, HEADS])
        dt_bias = s.sb("dt_bias", [P, 2, HEADS])
        x = s.sb("x", [P, NT, 2, HEADS])
        soft = s.sb("soft", [P, NT, 2, HEADS])
        eps = s.sb("eps", [P, 1])
        bq, bkk, bv = ([s.ps(f"{n}{i}", [P, BANK]) for i in range(2)] for n in ("bq", "bk", "bv"))
        bg = s.ps("bg", [P, 2, NT * HEADS])
        z_in = [s.sem(f"z_in{c}") for c in range(CC)]
        ab_in, small_in, s_in, s_zero = s.sem("ab_in"), s.sem("small_in"), s.sem("s_in"), s.sem("s_zero")
        silu_done, turned, q_taken, v_taken, squared, summed = (s.sem(n) for n in ("silu_done", "turned", "q_taken", "v_taken", "squared", "summed"))
        rooted, recip, scaled, back, back_taken = (s.sem(n) for n in ("rooted", "recip", "scaled", "back", "back_taken"))
        gate_act, gate_dve, g_mm, eps_set = s.sem("gate_act"), s.sem("gate_dve"), s.sem("g_mm"), s.sem("eps_set")
        blk = s.block()

        @blk.sync
        def _(sp):
            sp.dma_start(ab[:].rearrange("p t a h -> p t (a h)"), io["tm"][1][:, MIX:MIX + 32].rearrange("(t p) a -> p t a", p=P)).then_inc(ab_in, 16)
            sp.dma_start(incl[:], io["incl"].rearrange("d p i -> p d i")).then_inc(small_in, 16)
            sp.dma_start(a_log[:].rearrange("p d h -> p (d h)"), all_rows(io["gdn_a_log"][0].rearrange("d h -> (d h)"))).then_inc(small_in, 16)
            sp.dma_start(dt_bias[:].rearrange("p d h -> p (d h)"), all_rows(io["gdn_dt_bias"][0].rearrange("d h -> (d h)"))).then_inc(small_in, 16)
            for c in range(CC):
                sp.dma_start(zc[:, c, :], io["conv"][1][c * P:(c + 1) * P, :]).then_inc(z_in[c], 16)
            sp.dma_start(m["joins"][:], io["joins"].rearrange("s d p i -> p s d i")).then_inc(s_in, 16)
            sp.wait_ge(s_zero, 1)
            for d in range(2):
                for r in range(2):
                    sp.dma_start(S[64 * r:64 * r + 64, d, :, 64 * r:64 * r + 64],
                                 io["state_delta"][0, 0, d, r:8:2].rearrange("h k v -> k h v")).then_inc(s_in, 16)
            sp.wait_ge(s_in, 80)

        @blk.gpsimd
        def _(pool):
            nc.gpsimd.memset(S[:], 0.0).then_inc(s_zero, 1)
            nc.gpsimd.memset(eps[:], EPS).then_inc(eps_set, 1)

        @blk.tensor
        def _(pe):
            pe.wait_ge(silu_done, CC)
            for t in range(NT):
                if t >= 2:
                    pe.wait_ge(q_taken, 2 * (t - 1))
                    pe.wait_ge(v_taken, t - 1)
                for n, bank in enumerate((bq, bkk, bv)):
                    for j in range(4):
                        mm = nc.tensor.transpose(bank[t % 2][:, j * P:(j + 1) * P], zc[:, 4 * n + j, t * P:(t + 1) * P], keep.ident[:])
                mm.then_inc(turned, 1)
            pe.wait_ge(gate_dve, 4)
            for d in range(2):
                mm = nc.tensor.matmul(bg[:, d, :], incl[:, d, :], g[:, :, d, :], start=True, stop=True)
            mm.then_inc(g_mm, 1)
            for t in range(NT):
                if t >= 2:
                    pe.wait_ge(back_taken, 2 * (t - 1))
                elif t == 0:
                    pe.wait_ge(q_taken, 2 * NT)
                pe.wait_ge(scaled, 2 * (t + 1))
                for n, (bank, src) in enumerate(((bq, q[:, t, :]), (bkk, kv[:, t, 0, :]))):
                    for j in range(4):
                        mm = nc.tensor.transpose(bank[t % 2][:, j * P:(j + 1) * P], src[:, j * P:(j + 1) * P], keep.ident[:])
                mm.then_inc(back, 1)

        @blk.scalar
        def _(act):
            act.wait_ge(ab_in, 16)
            act.wait_ge(small_in, 48)
            nc.scalar.activation(beta[:], ab[:, :, 2:4, :], ACT.Sigmoid).then_inc(gate_act, 1)
            act.wait_ge(gate_dve, 1)
            nc.scalar.activation(soft[:], x[:], ACT.Abs).then_inc(gate_act, 1)
            act.wait_ge(gate_act, 2)
            nc.scalar.activation(soft[:], soft[:], ACT.Exp, scale=-1.0).then_inc(gate_act, 1)
            nc.scalar.activation(a_log[:], a_log[:], ACT.Exp).then_inc(gate_act, 1)
            act.wait_ge(gate_act, 4)
            act.wait_ge(gate_dve, 2)
            nc.scalar.activation(soft[:], soft[:], ACT.Ln).then_inc(gate_act, 1)
            for c in range(CC):
                act.wait_ge(z_in[c], 16)
                nc.scalar.activation(zc[:, c, :], zc[:, c, :], ACT.Silu).then_inc(silu_done, 1)
            for t in range(NT):
                act.wait_ge(turned, t + 1)
                nc.scalar.activation(kv[:, t, 1, :], bv[t % 2][:], ACT.Copy).then_inc(v_taken, 1)
                act.wait_ge(q_taken, 2 * (t + 1))
                if t:
                    act.wait_ge(summed, t)
                nc.scalar.activation(sq[:, 0, :], q[:, t, :], ACT.Square)
                nc.scalar.activation(sq[:, 1, :], kv[:, t, 0, :], ACT.Square).then_inc(squared, 1)
            act.wait_ge(gate_dve, 5)
            nc.scalar.activation(egc[:], gc[:], ACT.Exp).then_inc(gate_act, 1)
            act.wait_ge(summed, NT)
            act.wait_ge(eps_set, 1)
            nc.scalar.activation(ss[:], ss[:], ACT.Sqrt, bias=eps[:]).then_inc(rooted, 1)
            for t in range(NT):
                act.wait_ge(back, t + 1)
                at = slice(t * P, (t + 1) * P)
                nc.scalar.activation(QT[:, :, at], bq[t % 2][:].rearrange("p (j t) -> p j t", j=4), ACT.Copy).then_inc(back_taken, 1)
                nc.scalar.activation(KT[:, :, at], bkk[t % 2][:].rearrange("p (j t) -> p j t", j=4), ACT.Copy).then_inc(back_taken, 1)

        @blk.vector
        def _(dve):
            dve.wait_ge(ab_in, 16)
            dve.wait_ge(small_in, 48)
            rows = lambda a: a[:].unsqueeze(1).broadcast_to([P, NT, 2, HEADS])
            nc.vector.tensor_tensor(x[:], ab[:, :, 0:2, :], rows(dt_bias), ALU.add).then_inc(gate_dve, 1)
            dve.wait_ge(gate_act, 3)
            nc.vector.tensor_scalar(soft[:], soft[:], 1.0, None, ALU.add).then_inc(gate_dve, 1)
            dve.wait_ge(gate_act, 5)
            nc.vector.scalar_tensor_tensor(x[:].rearrange("p t d h -> p (t d h)"), x[:].rearrange("p t d h -> p (t d h)"), 0.0,
                                           soft[:].rearrange("p t d h -> p (t d h)"), ALU.max, ALU.add).then_inc(gate_dve, 1)
            dve.wait_ge(gate_dve, 3)
            nc.vector.scalar_tensor_tensor(g[:].rearrange("p t d h -> p t (d h)"), x[:].rearrange("p t d h -> p t (d h)"), -1.0,
                                           a_log[:].rearrange("p d h -> p (d h)").unsqueeze(1).broadcast_to([P, NT, 16]), ALU.mult, ALU.mult).then_inc(gate_dve, 1)
            for t in range(NT):
                dve.wait_ge(turned, t + 1)
                nc.vector.tensor_copy(q[:, t, :], bq[t % 2][:]).then_inc(q_taken, 1)
                nc.vector.tensor_copy(kv[:, t, 0, :], bkk[t % 2][:]).then_inc(q_taken, 1)
                dve.wait_ge(squared, t + 1)
                nc.vector.tensor_reduce(ss[:, t].rearrange("p a h -> p (a h)"), sq[:].rearrange("p a (h d) -> p (a h) d", d=HD), axis=AX.X, op=ALU.add).then_inc(summed, 1)
            dve.wait_ge(g_mm, 1)
            nc.vector.tensor_copy(gc[:].rearrange("p t d h -> p d t h"), bg[:].rearrange("p d (t h) -> p d t h", h=HEADS)).then_inc(gate_dve, 1)
            dve.wait_ge(gate_act, 6)
            nc.vector.tensor_tensor(begc[:], egc[:], beta[:], ALU.mult)
            dve.wait_ge(rooted, 1)
            nc.vector.reciprocal(ss[:], ss[:]).then_inc(recip, 1)
            dve.wait_ge(recip, 1)
            nc.vector.tensor_scalar(ss[:, :, 0, :], ss[:, :, 0, :], HD ** -0.5, None, ALU.mult).then_inc(recip, 1)
            dve.wait_ge(recip, 2)
            for t in range(NT):
                for a, y in ((0, q[:, t, :]), (1, kv[:, t, 0, :])):
                    y = y.rearrange("p (h d) -> p h d", d=HD)
                    nc.vector.tensor_tensor(y, y, ss[:, t, a, :].unsqueeze(2).broadcast_to([P, HEADS, HD]), ALU.mult).then_inc(scaled, 1)


def delta_chunks(nc, io, keep, m):
    kv, QT, KT, beta, g, gc, egc, begc, incl, joins, S, o = (
        m[x] for x in ("kv", "QT", "KT", "beta", "g", "gc", "egc", "begc", "incl", "joins", "S", "o"))
    items = [(NTS, 0, 2), (NTS, 1, 3)]
    for t in range(NTS):
        items += [(t, 0, 0), (NTS - 1 - t, 1, 1)]
    N_IT = len(items)
    NL = LEVELS - 1
    with Stage(nc, "gdnc") as s:
        HW = [P, HEADS, P]
        E_ = s.sb("E", HW)
        gam = s.sb("gam", HW)
        kg = s.sb("kg", HW)
        qg = s.sb("qg", HW)
        N = s.sb("N", HW)
        NTr = [s.sb(f"NT{i}", HW) for i in range(2)]
        AT = [s.sb(f"AT{i}", HW) for i in range(2)]
        part = [s.sb(f"part{i}", HW) for i in range(2)]
        Tm = [s.sb(f"T{i}", HW) for i in range(2)]
        TT = [s.sb(f"TT{i}", HW) for i in range(2)]
        W = s.sb("W", HW)
        gl = s.sb("gl", [P, 3, HEADS])
        dl = s.sb("dl", [P, 3, HEADS])
        egl = s.sb("egl", [P, 3, HEADS])
        egk = s.sb("egk", [P, 3, HEADS])
        vb = s.sb("vb", [P, MIX])
        kd = s.sb("kd", [P, MIX])
        r = s.sb("r", [P, MIX])
        vn = s.sb("vn", [P, MIX])
        mq = s.sb("mq", [P, MIX])
        ba = [s.ps(f"a{i}", [P, 4, P]) for i in range(2)]
        bb = [s.ps(f"b{i}", [P, 4, P]) for i in range(2)]
        bz = s.ps("z", HW)
        bx = s.ps("x", HW)
        z_mm, gbc_taken, gam_step, kk_taken, kq_taken, nt_taken = (s.sem(n) for n in ("z_mm", "gbc_taken", "gam_step", "kk_taken", "kq_taken", "nt_taken"))
        N_done, AT_done, T_set, T_step, TT_set, TT_step, part_done = (s.sem(n) for n in ("N_done", "AT_done", "T_set", "T_step", "TT_set", "TT_step", "part_done"))
        W_mm, W_taken, TU_mm, TU_done = s.sem("W_mm"), s.sem("W_taken"), s.sem("TU_mm"), s.sem("TU_done")
        x_mm, r_step, r_done, vn_done, o_step, o_done, S_step, S_done = (s.sem(n) for n in ("x_mm", "r_step", "r_done", "vn_done", "o_step", "o_done", "S_step", "S_done"))
        vb_done, kd_done, last_done, small_done = s.sem("vb_done"), s.sem("kd_done"), s.sem("last_done"), s.sem("small_done")
        st_out = s.sem("st_out")
        T_turned, TT_done = s.sem("T_turned"), s.sem("TT_done")
        blk = s.block()

        def lvl(n, li, hg):
            return (n * NL + li) * 2 + hg + 1

        def tt(n, li, hg):
            return (n * (NL - 1) + li) * 2 + hg + 1

        def z_decay(pe, n):
            t, d, _ = items[n]
            if n:
                pe.wait_ge(nt_taken, n)
            for h in range(HEADS):
                mm = nc.tensor.matmul(bz[:, h, :], g[:, t, d, h:h + 1].broadcast_to([P, P]), incl[:, d, :], start=True, stop=True)
            mm.then_inc(z_mm, 1)

        def z_keys(pe, n, src, taken):
            t = items[n][0]
            pe.wait_ge(taken, n + 1)
            at = slice(t * P, (t + 1) * P)
            for h in range(HEADS):
                rows = slice(64 * (h % 2), 64 * (h % 2) + 64)
                mm = nc.tensor.matmul(bz[:, 4 * (h % 2) + h // 2, :], KT[rows, h // 2, at], src[rows, h // 2, at], start=True, stop=True)
            mm.then_inc(z_mm, 1)

        def z_turn(pe, n):
            pe.wait_ge(kq_taken, n + 1)
            pe.wait_ge(N_done, n + 1)
            for h in range(HEADS):
                mm = nc.tensor.transpose(bz[:, h, :], N[:, h, :], keep.ident[:])
            mm.then_inc(z_mm, 1)

        def prep(pe, n, li):
            if n < N_IT:
                if li == 0:
                    z_decay(pe, n)
                elif li == 1:
                    z_keys(pe, n, KT, gbc_taken)
                elif li == 2:
                    z_keys(pe, n, QT, kk_taken)
                elif li == 3:
                    z_turn(pe, n)

        def scan(pe, n, li):
            if n < 0 or li > 3:
                return
            t, d, st = items[n]
            at = slice(t * P, (t + 1) * P)
            xf = bx[:].rearrange("p h i -> p (h i)")
            if li == 0:
                if n:
                    pe.wait_ge(S_done, n)
                for a, src in enumerate((KT, QT)):
                    for j in range(4):
                        mm = nc.tensor.matmul(xf[:, a * MIX + j * P:a * MIX + (j + 1) * P], src[:, j, at], S[:, st, j, :], start=True, stop=True)
            elif li == 1:
                pe.wait_ge(r_done, n + 1)
                pe.wait_ge(TU_done, lvl(n, NL - 1, 1))
                for h in range(HEADS):
                    mm = nc.tensor.matmul(bx[:, h, :], TT[n % 2][:, h, :], r[:, (h // 2) * P:(h // 2 + 1) * P], start=True, stop=True)
            elif li == 2:
                pe.wait_ge(vn_done, n + 1)
                pe.wait_ge(AT_done, n + 1)
                for h in range(HEADS):
                    mm = nc.tensor.matmul(bx[:, h, :], AT[n % 2][:, h, :], vn[:, (h // 2) * P:(h // 2 + 1) * P], start=True, stop=True)
            else:
                pe.wait_ge(o_done, n + 1)
                pe.wait_ge(kd_done, n + 1)
                for j in range(4):
                    mm = nc.tensor.matmul(xf[:, j * P:(j + 1) * P], kd[:, j * P:(j + 1) * P], vn[:, j * P:(j + 1) * P], start=True, stop=True)
            mm.then_inc(x_mm, 1)

        @blk.tensor
        def _(pe):
            for n in range(-1, N_IT + 1):
                live = 0 <= n < N_IT
                b = n % 2
                for li in range(NL):
                    if live:
                        pe.wait_ge(part_done, n * NL + li + 1)
                        if li == 0:
                            pe.wait_ge(T_set, n + 1)
                        for hg in range(2):
                            if n or li:
                                pe.wait_ge(TU_done, lvl(n, li - 1, hg))
                            for h in range(4):
                                mm = nc.tensor.matmul(ba[hg][:, h, :], part[li % 2][:, 4 * hg + h, :], Tm[b][:, 4 * hg + h, :], start=True, stop=True)
                            mm.then_inc(W_mm, 1)
                            if li:
                                for h in range(4):
                                    mm = nc.tensor.transpose(bb[hg][:, h, :], Tm[b][:, 4 * hg + h, :], keep.ident[:])
                                mm.then_inc(T_turned, 1)
                    prep(pe, n + 1, li)
                    if live:
                        if li == 0:
                            pe.wait_ge(TT_set, n + 1)
                        for hg in range(2):
                            pe.wait_ge(W_taken, lvl(n, li, hg))
                            if li < NL - 1:
                                if li:
                                    pe.wait_ge(TT_done, tt(n, li - 1, hg))
                                for h in range(4):
                                    mm = nc.tensor.matmul(bb[hg][:, h, :], TT[b][:, 4 * hg + h, :], W[:, 4 * hg + h, :], start=True, stop=True)
                                mm.then_inc(TU_mm, 1)
                            else:
                                pe.wait_ge(TT_done, tt(n, li - 1, hg))
                                for h in range(4):
                                    mm = nc.tensor.matmul(ba[hg][:, h, :], W[:, 4 * hg + h, :], TT[b][:, 4 * hg + h, :], start=True, stop=True)
                                mm.then_inc(TU_mm, 1)
                    scan(pe, n - 1, li)

        @blk.scalar
        def _(act):
            for n in range(-1, N_IT + 1):
                live = 0 <= n < N_IT
                p = n + 1
                for li in range(NL):
                    if live:
                        for hg in range(2):
                            act.wait_ge(W_mm, lvl(n, li, hg))
                            if n or li:
                                act.wait_ge(TU_mm, lvl(n, li - 1, hg))
                            nc.scalar.activation(W[:, 4 * hg:4 * hg + 4, :], ba[hg][:], ACT.Copy).then_inc(W_taken, 1)
                            if li:
                                act.wait_ge(T_turned, tt(n, li - 1, hg))
                                nc.scalar.activation(TT[n % 2][:, 4 * hg:4 * hg + 4, :], bb[hg][:], ACT.Copy).then_inc(TT_done, 1)
                    if p < N_IT and li == 0:
                        act.wait_ge(gbc_taken, p + 1)
                        nc.scalar.activation(E_[:], E_[:], ACT.Abs).then_inc(gam_step, 1)
                        act.wait_ge(gam_step, 2 * p + 1)
                        if p:
                            act.wait_ge(kq_taken, p)
                        nc.scalar.activation(gam[:], E_[:], ACT.Exp, scale=-1.0).then_inc(gam_step, 1)
                        act.wait_ge(last_done, p + 1)
                        nc.scalar.activation(egl[:, p % 3, :], gl[:, p % 3, :], ACT.Exp)
                        nc.scalar.activation(egk[:, p % 3, :], dl[:, p % 3, :], ACT.Exp).then_inc(small_done, 1)
                    if p < N_IT and li == 3:
                        act.wait_ge(z_mm, 4 * p + 4)
                        if p >= 2:
                            act.wait_ge(part_done, (p - 1) * NL)
                            act.wait_ge(TT_set, p - 1)
                        nc.scalar.activation(NTr[p % 2][:], bz[:], ACT.Copy).then_inc(nt_taken, 1)

        def by_half(a):
            return a[:].rearrange("p (j r) i -> p r j i", r=2)

        def prep_dve(dve, p, li):
            t, d, _ = items[p]
            halves = bz[:].rearrange("p (r j) i -> p r j i", r=2)
            if li == 0:
                dve.wait_ge(z_mm, 4 * p + 1)
                if p:
                    dve.wait_ge(gam_step, 2 * p)
                nc.vector.tensor_tensor(E_[:], bz[:], gc[:, t, d, :].unsqueeze(2).broadcast_to(HW), ALU.subtract)
                last = P - 1 if d == 0 else 0
                nc.vector.tensor_copy(gl[:, p % 3, :], bz[:, :, last]).then_inc(gbc_taken, 1)
                dve.wait_ge(gbc_taken, p + 1)
                nc.vector.tensor_tensor(dl[:, p % 3, :], gl[:, p % 3, :], gc[:, t, d, :], ALU.subtract).then_inc(last_done, 1)
            elif li == 1:
                dve.wait_ge(z_mm, 4 * p + 2)
                dve.wait_ge(gam_step, 2 * p + 2)
                if p:
                    dve.wait_ge(N_done, p)
                nc.vector.tensor_tensor(by_half(kg), halves, by_half(gam), ALU.mult).then_inc(kk_taken, 1)
            elif li == 2:
                dve.wait_ge(z_mm, 4 * p + 3)
                if p:
                    dve.wait_ge(AT_done, p)
                nc.vector.tensor_tensor(by_half(qg), halves, by_half(gam), ALU.mult).then_inc(kq_taken, 1)
            elif li == 4:
                dve.wait_ge(N_done, p + 1)
                nc.vector.tensor_tensor(Tm[p % 2][:], N[:], joins[:, 0, 1 - d, :].unsqueeze(1).broadcast_to(HW), ALU.mult).then_inc(T_step, 1)
                dve.wait_ge(T_step, p + 1)
                nc.vector.tensor_tensor(Tm[p % 2][:], keep.ident[:].unsqueeze(1).broadcast_to(HW), Tm[p % 2][:], ALU.subtract).then_inc(T_set, 1)

        def scan_dve(dve, q, li):
            t, d, st = items[q]
            heads = lambda a: a.rearrange("p (h e) -> p h e", e=HD)
            spread = lambda a: a.unsqueeze(2).broadcast_to([P, HEADS, HD])
            xf = bx[:].rearrange("p h i -> p (h i)")
            if li == 0:
                dve.wait_ge(x_mm, 4 * q + 1)
                nc.vector.tensor_tensor(heads(r[:]), heads(xf[:, 0:MIX]), spread(begc[:, t, d, :]), ALU.mult).then_inc(r_step, 1)
                nc.vector.tensor_tensor(heads(mq[:]), heads(xf[:, MIX:2 * MIX]), spread(egc[:, t, d, :]), ALU.mult)
                dve.wait_ge(r_step, q + 1)
                dve.wait_ge(vb_done, q + 1)
                nc.vector.tensor_tensor(r[:], vb[:], r[:], ALU.subtract).then_inc(r_done, 1)
            elif li == 1:
                dve.wait_ge(x_mm, 4 * q + 2)
                for half in range(2):
                    cols = slice(64 * half, 64 * half + 64)
                    ins = nc.vector.tensor_copy(heads(vn[:])[:, half:8:2, :], bx[:, half:8:2, cols])
                ins.then_inc(vn_done, 1)
            elif li == 2:
                dve.wait_ge(x_mm, 4 * q + 3)
                for half in range(2):
                    cols = slice(64 * half, 64 * half + 64)
                    dst = heads(mq[:])[:, half:8:2, :]
                    ins = nc.vector.tensor_tensor(dst, dst, bx[:, half:8:2, cols], ALU.add)
                ins.then_inc(o_step, 1)
                dve.wait_ge(o_step, q + 1)
                first = t not in [x[0] for x in items[:q]]
                if first:
                    nc.vector.tensor_copy(o[:, t, :], mq[:]).then_inc(o_done, 1)
                else:
                    nc.vector.tensor_tensor(o[:, t, :], o[:, t, :], mq[:], ALU.add).then_inc(o_done, 1)
            elif li == 3:
                for half in range(2):
                    rows = slice(64 * half, 64 * half + 64)
                    ins = nc.vector.tensor_tensor(S[rows, st, :, rows], S[rows, st, :, rows],
                                                  egl[rows, q % 3, half:8:2].unsqueeze(2).broadcast_to([64, 4, HD]), ALU.mult)
                ins.then_inc(S_step, 1)
                dve.wait_ge(S_step, q + 1)
                dve.wait_ge(x_mm, 4 * q + 4)
                for half in range(2):
                    rows = slice(64 * half, 64 * half + 64)
                    ins = nc.vector.tensor_tensor(S[rows, st, :, rows], S[rows, st, :, rows],
                                                  bx[:].rearrange("p h i -> p (h i)")[rows, 0:MIX].rearrange("p (j c) -> p j c", c=P)[:, :, rows], ALU.add)
                ins.then_inc(S_done, 1)

        @blk.vector
        def _(dve):
            for n in range(-1, N_IT + 1):
                live = 0 <= n < N_IT
                p, q = n + 1, n - 1
                for li in range(NL):
                    if p < N_IT:
                        prep_dve(dve, p, li)
                    if live:
                        b = n % 2
                        for hg in range(2):
                            dve.wait_ge(TU_mm, lvl(n, li, hg))
                            hs = slice(4 * hg, 4 * hg + 4)
                            if li < NL - 1:
                                nc.vector.tensor_tensor(Tm[b][:, hs, :], Tm[b][:, hs, :], bb[hg][:], ALU.subtract).then_inc(TU_done, 1)
                            else:
                                nc.vector.tensor_tensor(TT[b][:, hs, :], TT[b][:, hs, :], ba[hg][:], ALU.subtract).then_inc(TU_done, 1)
                    if q >= 0:
                        scan_dve(dve, q, li)

        @blk.gpsimd
        def _(pool):
            for n in range(-1, N_IT + 1):
                live = 0 <= n < N_IT
                p = n + 1

                def join(li):
                    if not live:
                        return
                    k = n * NL + li
                    if li == 0:
                        pool.wait_ge(nt_taken, n + 1)
                    if k >= 2:
                        pool.wait_ge(W_mm, 2 * (k - 1))
                    mask = joins[:, li + 1, items[n][1], :].unsqueeze(1).broadcast_to(HW)
                    nc.gpsimd.tensor_tensor(part[li % 2][:], NTr[n % 2][:], mask, ALU.mult).then_inc(part_done, 1)

                join(0)
                if live:
                    d = items[n][1]
                    if n >= 2:
                        pool.wait_ge(x_mm, 4 * (n - 2) + 2)
                    nc.gpsimd.tensor_tensor(TT[n % 2][:], NTr[n % 2][:], joins[:, 0, d, :].unsqueeze(1).broadcast_to(HW), ALU.mult).then_inc(TT_step, 1)
                    pool.wait_ge(TT_step, n + 1)
                    nc.gpsimd.tensor_tensor(TT[n % 2][:], keep.ident[:].unsqueeze(1).broadcast_to(HW), TT[n % 2][:], ALU.subtract).then_inc(TT_set, 1)
                join(1)
                join(2)
                if p < N_IT:
                    t, d, _ = items[p]
                    pool.wait_ge(kk_taken, p + 1)
                    if p:
                        pool.wait_ge(T_set, p)
                        pool.wait_ge(z_mm, 4 * p)
                    nc.gpsimd.tensor_tensor(N[:], kg[:], beta[:, t, d, :].unsqueeze(2).broadcast_to(HW), ALU.mult).then_inc(N_done, 1)
                join(3)
                if p < N_IT:
                    pool.wait_ge(kq_taken, p + 1)
                    if p >= 2:
                        pool.wait_ge(x_mm, 4 * (p - 2) + 3)
                    nc.gpsimd.tensor_tensor(AT[p % 2][:], qg[:], incl[:, d, :].unsqueeze(1).broadcast_to(HW), ALU.mult).then_inc(AT_done, 1)
                if live:
                    t, d, _ = items[n]
                    if n:
                        pool.wait_ge(r_done, n)
                    heads = lambda a: a.rearrange("p (h e) -> p h e", e=HD)
                    spread = lambda a: a.unsqueeze(2).broadcast_to([P, HEADS, HD])
                    nc.gpsimd.tensor_tensor(heads(vb[:]), heads(kv[:, t, 1, :]), spread(beta[:, t, d, :]), ALU.mult).then_inc(vb_done, 1)
                join(4)
                if live:
                    if n:
                        pool.wait_ge(x_mm, 4 * n)
                    pool.wait_ge(small_done, n + 1)
                    nc.gpsimd.tensor_tensor(heads(kd[:]), heads(kv[:, t, 0, :]), spread(egk[:, n % 3, :]), ALU.mult).then_inc(kd_done, 1)
                join(5)

        @blk.sync
        def _(sp):
            sp.wait_ge(S_done, 2)
            for d in range(2):
                for h in range(2):
                    sp.dma_start(io["new_state"][0, 0, d, h:8:2].rearrange("h k v -> k h v"),
                                 S[64 * h:64 * h + 64, 2 + d, :, 64 * h:64 * h + 64]).then_inc(st_out, 16)
            sp.wait_ge(st_out, 64)


def delta_outputs(nc, io, keep, m):
    o = m["o"]
    with Stage(nc, "gdno") as s:
        zg = s.sb("zg", [P, NT, MIX])
        sq = s.sb("sq", [P, 2, MIX])
        ss = s.sb("ss", [P, NT, HEADS])
        w = s.sb("w", [P, HD])
        eps = s.sb("eps", [P, 1])
        oT = s.sb("oT", [P, 2, 4, P])
        bt = [s.ps(f"t{i}", [P, BANK]) for i in range(2)]
        zg_in, w_in, silu_done, squared, summed, eps_set, rooted, recip, step, o_done, turned, taken = (
            s.sem(n) for n in ("zg_in", "w_in", "silu_done", "squared", "summed", "eps_set", "rooted", "recip", "step", "o_done", "turned", "taken"))
        out = [s.sem(f"out{i}") for i in range(2)]
        blk = s.block()

        @blk.sync
        def _(sp):
            sp.dma_start(zg[:], io["tm"][1][:, 0:MIX].rearrange("(t p) c -> p t c", p=P)).then_inc(zg_in, 16)
            sp.dma_start(w[:], all_rows(io["gdn_norm"][0])).then_inc(w_in, 16)
            for t in range(NT):
                sp.wait_ge(taken, t + 1)
                sp.dma_start(io["mixT"][1][0:MIX, t * P:(t + 1) * P].rearrange("(j p) t -> p j t", p=P), oT[:, t % 2]).then_inc(out[t % 2], 16)
            for i in range(2):
                sp.wait_ge(out[i], 16 * len(range(i, NT, 2)))

        @blk.scalar
        def _(act):
            for t in range(NT):
                if t >= 2:
                    act.wait_ge(summed, t - 1)
                nc.scalar.activation(sq[:, t % 2, :], o[:, t, :], ACT.Square).then_inc(squared, 1)
            act.wait_ge(summed, NT)
            act.wait_ge(eps_set, 1)
            nc.scalar.activation(ss[:], ss[:], ACT.Sqrt, bias=eps[:], scale=1.0 / HD).then_inc(rooted, 1)
            act.wait_ge(zg_in, 16)
            for t in range(NT):
                nc.scalar.activation(zg[:, t, :], zg[:, t, :], ACT.Silu).then_inc(silu_done, 1)
            for t in range(NT):
                act.wait_ge(turned, t + 1)
                if t >= 2:
                    act.wait_ge(out[t % 2], 16 * (t // 2))
                nc.scalar.activation(oT[:, t % 2], bt[t % 2][:].rearrange("p (j t) -> p j t", j=4), ACT.Copy).then_inc(taken, 1)

        @blk.vector
        def _(dve):
            nc.vector.memset(eps[:], EPS).then_inc(eps_set, 1)
            for t in range(NT):
                dve.wait_ge(squared, t + 1)
                nc.vector.tensor_reduce(ss[:, t, :], sq[:, t % 2, :].rearrange("p (h d) -> p h d", d=HD), axis=AX.X, op=ALU.add).then_inc(summed, 1)
            dve.wait_ge(rooted, 1)
            nc.vector.reciprocal(ss[:], ss[:]).then_inc(recip, 1)
            dve.wait_ge(recip, 1)
            dve.wait_ge(w_in, 16)
            link = Link(dve, step)
            for t in range(NT):
                y = o[:, t, :].rearrange("p (h d) -> p h d", d=HD)
                z = zg[:, t, :].rearrange("p (h d) -> p h d", d=HD)
                dve.wait_ge(silu_done, t + 1)
                nc.vector.tensor_tensor(z, z, w[:].unsqueeze(1).broadcast_to([P, HEADS, HD]), ALU.mult)
                link(nc.vector.tensor_tensor(y, y, ss[:, t, :].unsqueeze(2).broadcast_to([P, HEADS, HD]), ALU.mult))
                nc.vector.tensor_tensor(y, y, z, ALU.mult).then_inc(o_done, 1)

        @blk.tensor
        def _(pe):
            for t in range(NT):
                pe.wait_ge(o_done, t + 1)
                if t >= 2:
                    pe.wait_ge(taken, t - 1)
                for j in range(4):
                    mm = nc.tensor.transpose(bt[t % 2][:, j * P:(j + 1) * P], o[:, t, j * P:(j + 1) * P], keep.ident[:])
                mm.then_inc(turned, 1)



class Keep:

    def __init__(self, s):
        self.ident = s.sb("ident", [P, P])
        self.coef = s.sb("coef", [P, 2, 2, 2, 2, KD])
        self.silu = s.sb("silu", [P, KD, 2])
        self.gain_cols = s.sb("gain_cols", [P, 4 * KD])
        self.tap_scale = s.sb("tap_scale", [P, 2, 2 * MIX // P])

        self.slot_s = s.sb("slot_s", [P, E + 1], U32)
        self.slot_p = s.sb("slot_p", [P, E + 1], U32)
        self.gate_s = s.sb("gate_s", [P, E])
        self.gate_p = s.sb("gate_p", [P, E])


SCRATCH = {
    "mrow": (2, 2, 6 * D),
    "tm0": (T, EVEN_TM), "tm1": (T, ODD_TM),
    "conv0": (CONV, T), "conv1": (CONV, T),
    "mixT0": (D, T), "mixT1": (D, T),
    "x0": (T, D), "x1": (T, D),
    "xn": (T, D), "rpbpad": (120, GRID_W, P), "spec": (NT, P, 2, 2, MIX),
}
INPUTS = ["x_prompt", "x_sample", "cache_attn_k", "cache_attn_v", "state_delta", "cache_na_k", "cache_na_v", "c", "c_ctx",
          "w_ada", "b_ada", "norm_mix", "norm_ffn", "norm_final", "even_w_in", "even_w_out", "attn_sink", "hy_conv_w",
          "hy_conv_b", "hy_w1", "hy_b1", "hy_w2", "hy_b2", "hy_w3", "hy_freq", "hy_skip", "odd_w_in", "odd_w_out",
          "gdn_conv_w", "gdn_a_log", "gdn_dt_bias", "gdn_norm", "na_rpb", "moe_router", "moe_w_gate", "moe_w_up",
          "moe_w_down", "ident", "band", "cos", "sin", "colmask", "feats", "win", "win_b", "filt_dft", "filt_dft_p",
          "sig_dft", "sig_dft_p", "sig_idft", "sig_idft_p", "incl", "joins"]
OUTPUTS = {
    "y_prompt": (1, TP, D), "y_sample": (1, TS, D), "new_attn_k": (1, 1, TP, 2, HD), "new_attn_v": (1, 1, TP, 2, HD),
    "new_state": (1, 1, 2, 8, HD, HD), "new_na_k": (1, 1, TP, 8, HD), "new_na_v": (1, 1, TP, 8, HD),
}


def constants():
    f = np.float32
    i, j = np.arange(P)[:, None], np.arange(P)[None, :]
    none, before, after = np.zeros((P, P), f), np.where(j >= i, f(0), f(NEG)), np.where(j <= i, f(0), f(NEG))
    band = np.concatenate([none, before, none, after, none, none, after], axis=1).astype(f)
    t = np.arange(TS)
    inv = (10000.0 ** (-np.arange(HD // 4, dtype=f) / (HD // 4))).astype(f)
    angle = np.concatenate([(t // GRID_W).astype(f)[:, None] * inv, (t % GRID_W).astype(f)[:, None] * inv], axis=-1)
    by_tile = lambda a: np.ascontiguousarray(a.reshape(NTS, P, 32).transpose(1, 0, 2)).astype(f)
    c = np.arange(P)[:, None] % GRID_W
    lo = np.clip(c - 8, 0, GRID_W - 16)
    kc = np.arange(GRID_W)[None, :]
    colmask = np.where((kc >= lo) & (kc < lo + 16), f(0), f(NEG)).astype(f)
    out = {}
    feats, wins, last = [], [], []
    for L in (TS, TP):
        n = np.arange(L)
        order = np.concatenate([n[0::2], n[1::2]]) if L == TS else n
        tt = np.linspace(0.0, 1.0, L, dtype=f)[:, None]
        bands = np.linspace(1e-4, 15, 16, dtype=f)[None, :]
        omega = (2.0 * math.pi * n.astype(f)[:, None] / L).astype(f)
        ph = (bands * omega).astype(f).astype(np.float64)
        feats.append(np.concatenate([tt, np.cos(ph), -np.sin(ph)], axis=1)[order].T)
        lo, hi = math.log(1e-2) / 1.5, math.log(1e-2) / 0.3
        deltas = np.abs(np.linspace(lo, hi, MIX, dtype=f))
        w = (np.exp((-tt * deltas).astype(np.float64)) + 0.05)[order]
        wins.append(w)
        head = w[0:P].copy()
        head[0] = 0.0
        last.append(head)
        freq = np.pi * (2 * np.arange(L) + 1) / (2 * L)
        if L == TS:
            a = np.outer(order, freq[0:L // 2])
            freq = np.concatenate([freq[0:L // 2], np.pi - freq[0:L // 2]])
            names = ("filt_dft", "sig_dft", "sig_idft")
        else:
            a = np.outer(order, freq)
            names = ("filt_dft_p", "sig_dft_p", "sig_idft_p")
        b = np.outer(np.arange(L // 2) + 0.5, freq)
        out[names[0]] = np.stack([np.cos(a), np.sin(a)]).astype(f)
        out[names[1]] = np.stack([np.cos(b), np.sin(b)]).astype(f)
        out[names[2]] = np.stack([np.cos(b).T / L, np.sin(b).T / L]).astype(f)
    out["feats"] = np.concatenate(feats, axis=1).astype(f)
    out["win"] = np.concatenate(wins).astype(f)
    out["win_b"] = np.stack(last).astype(f)
    out["incl"] = np.stack([j >= i, j <= i]).astype(f)
    joins = []
    for lv in range(LEVELS):
        b = 2 << lv
        later = (i // b == j // b) & (i % b < b // 2) & (j % b >= b // 2)
        joins.append(np.stack([later, later.T]))
    out["joins"] = np.stack(joins).astype(f)
    return out | {"ident": np.eye(P, dtype=f), "band": band, "cos": by_tile(np.cos(angle)), "sin": by_tile(np.sin(angle)),
            "colmask": colmask}


def wire(io, scratch, outs):
    io["mrow"] = scratch["mrow"]
    io["x_of"] = [{"xs": io["x_sample"][0], "xp": io["x_prompt"][0]}, {"x": scratch["x0"]}]
    for n in ("tm", "conv", "mixT", "x"):
        io[n] = [scratch[n + "0"], scratch[n + "1"]]
    io["rpbpad"], io["spec"] = scratch["rpbpad"], scratch["spec"]
    io["xn"] = scratch["xn"]
    io.update(outs)


def program(nc, io):
    with Stage(nc, "keep") as s:
        keep = Keep(s)
        modulation(nc, io, keep)
        project(nc, io, keep, 0)
        attention(nc, io, keep, 0)
        hyena_filters(nc, io, keep)
        hyena_signals(nc, io, keep)
        mix_and_experts(nc, io, keep, 0)
        project(nc, io, keep, 1)
        attention(nc, io, keep, 1)
        delta_net(nc, io, keep)
        mix_and_experts(nc, io, keep, 1)
        final_norm(nc, io, keep)


def kernel(**inputs):
    import concourse.bacc as bacc
    from concourse.bass_utils import run_bass_kernel_spmd

    nc = bacc.Bacc("TRN2", target_bir_lowering=False, num_devices=1)
    shapes = constants()
    arrays, io, scratch, outs = {}, {}, {}, {}
    for name in INPUTS:
        a = np.ascontiguousarray(shapes[name] if name in shapes else inputs[name])
        arrays[name] = a
        io[name] = nc.dram_tensor(name, a.shape, F32, kind="ExternalInput").ap()
    for name, shape in SCRATCH.items():
        scratch[name] = nc.dram_tensor("scratch_" + name, shape, F32, kind="Internal").ap()
    for name, shape in OUTPUTS.items():
        outs[name] = nc.dram_tensor(name, shape, F32, kind="ExternalOutput").ap()
    wire(io, scratch, outs)
    program(nc, io)
    r = run_bass_kernel_spmd(nc, [arrays], core_ids=[0])
    return tuple(r.results[0][name] for name in OUTPUTS)
```
